# Optimizing a Trainium2 kernel written in Bass

```python
import jax, jax.numpy as jnp
from jax import lax
import numpy as np

D_MODEL = 1024
BATCH = 1
SEQ = 128
DEPTH = 2
DEC_BATCH = 1
DEC_SEQ = 512
PAST_LEN = 128

GRID_W = 64
D_SSM = 1024
HEAD_DIM_SSM = 64
N_HEADS_SSM = D_SSM // HEAD_DIM_SSM
N_GROUPS_SSM = 4
D_STATE = 128
D_CONV = 5
SSD_CHUNK = 128
CONV_DIM = D_SSM + 2 * N_GROUPS_SSM * D_STATE
D_GMLP = 1024
N_GROUPS_GMLP = 8
GMLP_GROUP_DIM = D_GMLP // N_GROUPS_GMLP
GMLP_CHUNK = 128
IN_SIZES = (CONV_DIM, D_SSM, 2 * N_HEADS_SSM, D_GMLP, D_GMLP, D_GMLP, D_MODEL, D_MODEL)
D_IN = CONV_DIM + D_SSM + 2 * N_HEADS_SSM + 3 * D_GMLP + 2 * D_MODEL
EPS = 1e-6

kernel_name = 'hybrid_ssd_gmlp_diffusion_step'

def _split_points(sizes):
    pts, acc = [], 0
    for s in sizes[:-1]:
        acc += s
        pts.append(acc)
    return pts

def rms_norm(x, w):
    xf = x.astype(jnp.float32)
    y = xf * lax.rsqrt(jnp.mean(xf * xf, axis=-1, keepdims=True) + EPS)
    return (y * w.astype(jnp.float32)).astype(x.dtype)

def layer_norm(x, w, b):
    xf = x.astype(jnp.float32)
    mu = jnp.mean(xf, axis=-1, keepdims=True)
    xc = xf - mu
    y = xc * lax.rsqrt(jnp.mean(xc * xc, axis=-1, keepdims=True) + EPS)
    return (y * w.astype(jnp.float32) + b.astype(jnp.float32)).astype(x.dtype)

def _dwconv(x, w, b):
    y = lax.conv_general_dilated(x, w[:, None, :], window_strides=(1,), padding='SAME',
                                 dimension_numbers=('NWC', 'WIO', 'NWC'),
                                 feature_group_count=x.shape[-1])
    return y + b

def _grid_to_col_major(t, rows):
    b, l = t.shape[:2]
    rest = t.shape[2:]
    return t.reshape((b, rows, GRID_W) + rest).swapaxes(1, 2).reshape((b, l) + rest)

def _col_major_to_grid(t, rows):
    b, l = t.shape[:2]
    rest = t.shape[2:]
    return t.reshape((b, GRID_W, rows) + rest).swapaxes(1, 2).reshape((b, l) + rest)

def _segsum(a):
    cs = jnp.cumsum(a, axis=-1)
    diff = cs[..., :, None] - cs[..., None, :]
    t = a.shape[-1]
    mask = jnp.tril(jnp.ones((t, t), dtype=bool))
    return jnp.where(mask, diff, -jnp.inf)

def _ssd_scan(x, dt, a, b_mat, c_mat, h0):
    bsz, l, h, p = x.shape
    n = b_mat.shape[-1]
    rep = h // b_mat.shape[2]
    nc = l // SSD_CHUNK
    bh = jnp.repeat(b_mat, rep, axis=2).reshape(bsz, nc, SSD_CHUNK, h, n)
    chh = jnp.repeat(c_mat, rep, axis=2).reshape(bsz, nc, SSD_CHUNK, h, n)
    xc = (x * dt[..., None]).reshape(bsz, nc, SSD_CHUNK, h, p)
    a_dt = (dt * a).reshape(bsz, nc, SSD_CHUNK, h).transpose(0, 3, 1, 2)
    a_cum = jnp.cumsum(a_dt, axis=-1)
    lmat = jnp.exp(_segsum(a_dt))
    y_diag = jnp.einsum('bclhn,bcshn,bhcls,bcshp->bclhp', chh, bh, lmat, xc)
    decay_states = jnp.exp(a_cum[..., -1:] - a_cum)
    states = jnp.einsum('bcshn,bhcs,bcshp->bchpn', bh, decay_states, xc)
    states = jnp.concatenate([h0[:, None], states], axis=1)
    chunk_decay = jnp.exp(_segsum(jnp.pad(a_cum[..., -1], ((0, 0), (0, 0), (1, 0)))))
    new_states = jnp.einsum('bhzc,bchpn->bzhpn', chunk_decay, states)
    states_in, final = new_states[:, :-1], new_states[:, -1]
    y_off = jnp.einsum('bclhn,bchpn,bhcl->bclhp', chh, states_in, jnp.exp(a_cum))
    return (y_diag + y_off).reshape(bsz, l, h, p), final

def _ssd_branch(xbc_raw, dt_raw, z, h0, conv_w, conv_b, dt_bias, a_log, d_skip, ssm_norm_w, rows):
    col_major = rows is not None
    if col_major:
        xbc_raw = _grid_to_col_major(xbc_raw, rows)
        dt_raw = _grid_to_col_major(dt_raw, rows)
    xbc = jax.nn.silu(_dwconv(xbc_raw, conv_w, conv_b))
    bsz, l, _ = xbc.shape
    xs, bm, cm = jnp.split(xbc, [D_SSM, D_SSM + N_GROUPS_SSM * D_STATE], axis=-1)
    f32 = jnp.float32
    xs = xs.reshape(bsz, l, N_HEADS_SSM, HEAD_DIM_SSM).astype(f32)
    bm = bm.reshape(bsz, l, N_GROUPS_SSM, D_STATE).astype(f32)
    cm = cm.reshape(bsz, l, N_GROUPS_SSM, D_STATE).astype(f32)
    dt = jax.nn.softplus(dt_raw.astype(f32).reshape(bsz, l, 2, N_HEADS_SSM) + dt_bias.astype(f32))
    a = -jnp.exp(a_log.astype(f32))
    h0 = h0.astype(f32)
    y_f, h_f = _ssd_scan(xs, dt[:, :, 0], a[0], bm, cm, h0[:, 0])
    y_b, h_b = _ssd_scan(jnp.flip(xs, 1), jnp.flip(dt[:, :, 1], 1), a[1],
                         jnp.flip(bm, 1), jnp.flip(cm, 1), h0[:, 1])
    y = y_f + jnp.flip(y_b, 1) + d_skip.astype(f32)[:, None] * xs
    y = y.reshape(bsz, l, D_SSM).astype(z.dtype)
    if col_major:
        y = _col_major_to_grid(y, rows)
    y = rms_norm(y * jax.nn.silu(z), ssm_norm_w)
    return y, jnp.stack([h_f, h_b], axis=1)

def _gmlp_branch(u_raw, v_raw, z, ln_w, ln_b, w_sp, b_sp):
    u = jax.nn.gelu(u_raw)
    v = layer_norm(jax.nn.gelu(v_raw), ln_w, ln_b)
    bsz, l, _ = v.shape
    vg = v.reshape(bsz, l // GMLP_CHUNK, GMLP_CHUNK, N_GROUPS_GMLP, GMLP_GROUP_DIM)
    s = jnp.einsum('gts,bnsgc->bntgc', w_sp, vg) + b_sp.T[None, None, :, :, None]
    return u * s.reshape(bsz, l, D_GMLP) * jax.nn.silu(z)

def _layer(x, mod, h0, lw, rows):
    (w_in, norm_w, conv_w, conv_b, dt_bias, a_log, d_skip, ssm_norm_w, w_out_m,
     sgu_ln_w, sgu_ln_b, w_sp, b_sp, w_out_g, w_out) = lw
    shift, scale, gate = jnp.split(mod, 3, axis=-1)
    h = rms_norm(x, norm_w) * (1 + scale[:, None]) + shift[:, None]
    proj = h @ w_in
    xbc_raw, z_m, dt_raw, u_raw, v_raw, z_g, gl_m, gl_g = jnp.split(
        proj, _split_points(IN_SIZES), axis=-1)
    y_m, h_fin = _ssd_branch(xbc_raw, dt_raw, z_m, h0, conv_w, conv_b, dt_bias, a_log,
                             d_skip, ssm_norm_w, rows)
    y_g = _gmlp_branch(u_raw, v_raw, z_g, sgu_ln_w, sgu_ln_b, w_sp, b_sp)
    merged = jax.nn.sigmoid(gl_m) * (y_m @ w_out_m) + jax.nn.sigmoid(gl_g) * (y_g @ w_out_g)
    return x + gate[:, None] * (merged @ w_out), h_fin

def setup_inputs(seed: int = 0) -> dict:
    key = jax.random.key(seed)
    ks = jax.random.split(key, 24)
    nrm = jax.random.normal
    f32 = jnp.float32
    dt_lo = CONV_DIM + D_SSM
    dt_hi = dt_lo + 2 * N_HEADS_SSM
    w_in = nrm(ks[5], (DEPTH, D_MODEL, D_IN), f32) * D_MODEL ** -0.5
    w_in = w_in.at[:, :, dt_lo:dt_hi].multiply(0.1)
    dt_init = jnp.exp(jax.random.uniform(ks[8], (DEPTH, 2, N_HEADS_SSM), f32,
                                         np.log(1e-3), np.log(1e-1)))
    dt_bias = dt_init + jnp.log(-jnp.expm1(-dt_init))
    return {
        'x_prompt': nrm(ks[0], (BATCH, SEQ, D_MODEL), f32),
        'x_sample': nrm(ks[1], (DEC_BATCH, DEC_SEQ, D_MODEL), f32),
        'state_ssm': 0.5 * nrm(ks[2], (DEC_BATCH, DEPTH, 2, N_HEADS_SSM, HEAD_DIM_SSM, D_STATE), f32),
        'c': nrm(ks[3], (DEC_BATCH, D_MODEL), f32),
        'c_ctx': nrm(ks[4], (D_MODEL,), f32),
        'w_ada': nrm(ks[6], (DEPTH, D_MODEL, 3 * D_MODEL), f32) * 0.5 * D_MODEL ** -0.5,
        'b_ada': 0.01 * nrm(ks[7], (DEPTH, 3 * D_MODEL), f32),
        'norm_w': 1.0 + 0.1 * nrm(ks[9], (DEPTH, D_MODEL), f32),
        'w_in': w_in,
        'conv_w': nrm(ks[10], (DEPTH, D_CONV, CONV_DIM), f32) * D_CONV ** -0.5,
        'conv_b': 0.01 * nrm(ks[11], (DEPTH, CONV_DIM), f32),
        'dt_bias': dt_bias,
        'a_log': jnp.log(jax.random.uniform(ks[12], (DEPTH, 2, N_HEADS_SSM), f32, 1.0, 16.0)),
        'd_skip': 1.0 + 0.1 * nrm(ks[13], (DEPTH, N_HEADS_SSM), f32),
        'ssm_norm_w': 1.0 + 0.1 * nrm(ks[14], (DEPTH, D_SSM), f32),
        'w_out_m': nrm(ks[15], (DEPTH, D_SSM, D_MODEL), f32) * D_SSM ** -0.5,
        'sgu_ln_w': 1.0 + 0.1 * nrm(ks[16], (DEPTH, D_GMLP), f32),
        'sgu_ln_b': 0.1 * nrm(ks[17], (DEPTH, D_GMLP), f32),
        'w_sp': nrm(ks[18], (DEPTH, N_GROUPS_GMLP, GMLP_CHUNK, GMLP_CHUNK), f32) * GMLP_CHUNK ** -0.5,
        'b_sp': 1.0 + 0.1 * nrm(ks[19], (DEPTH, N_GROUPS_GMLP, GMLP_CHUNK), f32),
        'w_out_g': nrm(ks[20], (DEPTH, D_GMLP, D_MODEL), f32) * D_GMLP ** -0.5,
        'w_out': nrm(ks[21], (DEPTH, D_MODEL, D_MODEL), f32) * D_MODEL ** -0.5,
        'final_norm_w': 1.0 + 0.1 * nrm(ks[22], (D_MODEL,), f32),
    }

def reference(x_prompt, x_sample, state_ssm, c, c_ctx, w_ada, b_ada, norm_w, w_in, conv_w,
              conv_b, dt_bias, a_log, d_skip, ssm_norm_w, w_out_m, sgu_ln_w, sgu_ln_b,
              w_sp, b_sp, w_out_g, w_out, final_norm_w):
    rows = x_sample.shape[1] // GRID_W
    h_ctx = x_prompt
    h_lat = x_sample
    h0_ctx = jnp.zeros((x_prompt.shape[0], 2, N_HEADS_SSM, HEAD_DIM_SSM, D_STATE), jnp.float32)
    silu_c = jax.nn.silu(c)
    silu_cctx = jax.nn.silu(c_ctx)[None, :]
    ctx_states = []
    for i in range(DEPTH):
        lw = (w_in[i], norm_w[i], conv_w[i], conv_b[i], dt_bias[i], a_log[i], d_skip[i],
              ssm_norm_w[i], w_out_m[i], sgu_ln_w[i], sgu_ln_b[i], w_sp[i], b_sp[i],
              w_out_g[i], w_out[i])
        mod_ctx = silu_cctx @ w_ada[i] + b_ada[i]
        mod_lat = silu_c @ w_ada[i] + b_ada[i]
        h_ctx, st = _layer(h_ctx, mod_ctx, h0_ctx, lw, None)
        ctx_states.append(st.astype(x_prompt.dtype))
        h_lat, _ = _layer(h_lat, mod_lat, state_ssm[:, i], lw, rows if i % 2 == 1 else None)
    new_state_ssm = jnp.stack(ctx_states, axis=1)
    y_prompt = rms_norm(h_ctx, final_norm_w)
    y_sample = rms_norm(h_lat, final_norm_w)
    return (y_prompt, y_sample, new_state_ssm)


_drawn_inputs = setup_inputs


def setup_inputs(seed=0):
    import zlib

    import numpy as np

    out = dict(_drawn_inputs(seed))
    spreads = {}
    factors = {'conv_b': 2.886,
     'd_skip': 12.576,
     'sgu_ln_w': 5.518,
     'sgu_ln_b': 4.897,
     'b_sp': 5.325,
     'ssm_norm_w': 2.768}
    for name, (base, spread) in spreads.items():
        noise = np.random.default_rng([zlib.crc32(name.encode()), seed]).standard_normal(out[name].shape)
        drawn = base * np.exp(spread * noise) if base else spread * noise
        out[name] = __import__('jax').numpy.asarray(drawn.astype(out[name].dtype))
    for name, factor in factors.items():
        out[name] = (out[name] * factor).astype(out[name].dtype)
    return out
```

```python
from contextlib import ExitStack

import concourse.bass as bass
from concourse import mybir

P = 128
DEPTH, DM = 2, 1024
KC = DM // P
CTX, LAT = 128, 512
TOK = CTX + LAT
HALF = TOK // 2
GW, GH = 64, LAT // 64
NCH = TOK // P
NH, HD, NG = 16, 64, 4
HPG = NH // NG
GC = HPG * HD
TAPS = 5
PAD = TAPS // 2
CW = CTX + PAD + LAT
LAT0 = CTX + PAD
RAW = CW + 2 * PAD
PITCH = (RAW + 7) // 8 * 8
NCONV = 16
EPS = 1e-6

N_TILES = 1 + NCONV + 8 + 16 + 8 + 32 + 8
T_CONV, T_V, T_UZ, T_ZM, T_S5, T_OUT = 1, 17, 25, 41, 49, 81

F32 = mybir.dt.float32
F32R = mybir.dt.float32r
ALU = mybir.AluOpType
ACT = mybir.ActivationFunctionType
AXX = mybir.AxisListType.X

A_UNITS = [(c, g) for g in range(NG) for c in range(NCH)]
B_UNITS = [(c, g) for c in range(NCH) for g in range(NG)]
NU = len(A_UNITS)
A_STEPS = (2, 5, 8)
B_STEPS = [10 + 29 * b // 5 for b in range(NU + 1)]
JOBS_FIRST = [(0, q, h) for q in (0, 1) for h in (0, 1)]
JOBS_LATER = [(0, 2, 0), (0, 2, 1)] + [(1, q, h) for q in range(3) for h in (0, 1)]


def order_uz():
    out = [((8 * (n + 1), 1), ("tile", n)) for n in range(16)]
    out += [((at, 0), ("burst", b)) for b, at in enumerate(B_STEPS)]
    return [x for _, x in sorted(out)]


class Chain:

    def __init__(self, eng, sem):
        self.eng, self.sem, self.n = eng, sem, 0

    def mark(self, ins):
        ins.then_inc(self.sem, 1)
        self.n += 1
        return self.n

    def wait(self, n=None):
        self.eng.wait_ge(self.sem, self.n if n is None else n)

    def link(self, ins):
        self.mark(ins)
        self.wait()


def build(nc, xT, wts, wada, cT, bada, normw, finalw, ssmw, convw, dtb, alog, dskip, lnw, lnb,
          wsp, bsp, h0, yT, st_out, x_mid):
    ctx = ExitStack()
    pos = [1152]

    def region(nbytes):
        at = pos[0]
        pos[0] += (nbytes + 31) // 32 * 32
        assert pos[0] <= nc.sbuf_usable_end, pos[0]
        return at

    def place(name, shape, at, dt=F32):
        return nc.alloc_sbuf_tensor_at(name, shape, dt, offset=at)

    def new(name, shape, dt=F32):
        n = 4
        for s in shape[1:]:
            n *= s
        return place(name, shape, region(n), dt)

    ACTB = KC * TOK * 4
    h_hi = new("h_hi", [P, KC, TOK], F32R)
    h_lo = new("h_lo", [P, KC, TOK], F32R)
    w_st = new("w_st", [P, 2, KC * P])
    w_hi = new("w_hi", [P, 2, KC * P], F32R)
    w_lo = new("w_lo", [P, 2, KC * P], F32R)
    r_v = region(ACTB)
    v_tok = place("v_tok", [P, NCH, DM], r_v)
    mg = place("mg", [P, KC, TOK], r_v)
    r_uz = region(ACTB)
    uz = place("uz", [P, KC, TOK], r_uz)
    yg_lo = place("yg_lo", [P, KC, TOK], r_uz, F32R)
    r_r = region(ACTB)
    yg_hi = place("yg_hi", [P, KC, TOK], r_r, F32R)
    bsp_row = place("bsp_row", [1, DM], r_r + 15360)
    r_x = region(ACTB)
    x_tok = place("x_tok", [P, NCH, DM], r_x)
    xr = place("xr", [P, KC, TOK], r_x)
    r_bc = region(8 * CW * 4)
    bc = place("bc", [P, 8, CW], r_bc)
    ym_lo = place("ym_lo", [P, KC, TOK], r_bc, F32R)
    r_t = region(ACTB)
    ym_hi = place("ym_hi", [P, KC, TOK], r_t, F32R)
    raw = place("raw", [P, 2, PITCH], r_t)
    cv = place("cv", [P, 2, PITCH], r_t + 8 * PITCH)
    cvt = place("cvt", [P, PITCH], r_t + 16 * PITCH)
    xo = place("xo", [P, 2, PITCH], r_t + 20 * PITCH)
    dmat = place("dmat", [P, HPG, P], r_t)
    mmat = place("mmat", [P, 2, HPG, P], r_t + 2048)
    xfb = place("xfb", [P, 2, HPG, HD], r_t + 6144)
    gm = place("gm", [P, 2, P], r_t + 8192)
    yab = place("yab", [P, 2, HPG, HD], r_t + 9216)
    scan_tmp = place("scan_tmp", [P, DM], r_t + 11264)
    r_wp = region(8 * DM)
    wsp_sb = place("wsp_sb", [P, 8, P], r_wp)
    lnb_sb = place("lnb_sb", [P, DM], r_wp + 4 * DM)
    pbb = place("pbb", [P, 8, P], r_wp + 4 * DM)
    ada_st = place("ada_st", [P, 2, 2, 512], r_wp)
    r_c = region(5 * TOK * 4)
    c_buf = [place(f"c_buf{i}", [P, TOK], r_c + i * TOK * 4) for i in range(5)]
    xw = place("xw", [P, 2, 2, HPG, HD], r_c + 2 * TOK * 4)
    bt = place("bt", [P, 2, P], r_c + 2 * TOK * 4 + 4096)
    ctx_st = place("ctx_st", [P, 2 * GC], r_c + 4 * TOK * 4)
    dta = place("dta", [64, TOK], r_c + 4 * TOK * 4)
    adup = place("adup", [P, NCH, 4, NH], r_c + 3 * TOK * 4)
    cum_r = place("cum_r", [64, TOK], r_c, F32R)
    r_a0, r_a1 = region(4096), region(4096)
    ada_acc = [place(f"ada_acc{i}", [P, 2, 512], at) for i, at in enumerate((r_a0, r_a1))]
    st_at = [r_r + i * 4096 for i in range(5)] + [r_wp, r_wp + 4096, r_a0]
    states = [place(f"states{i}", [P, DM], at) for i, at in enumerate(st_at)]
    tm = place("tm", [P, NCH, 64], r_a1)
    ex = place("ex", [P, 6, NCH, NH], r_a1 + 1280)
    ncf = place("ncf", [P, NCH, NH], r_a1 + 3200)
    ebs = place("ebs", [P, NCH, NH], r_a1 + 3520)
    r_cum = region(TOK * 4)
    cum_t = place("cum_t", [64, TOK], r_cum, F32R)
    ssq = place("ssq", [P, TOK], r_cum)
    tri = new("tri", [P, 2, P])
    maskb = new("maskb", [P, P])
    ident = new("ident", [P, P])
    ones = new("ones", [P, P])
    sel32 = new("sel32", [64, 32])
    sel = new("sel", [64, 32], F32R)
    dupm = new("dupm", [64, NH])
    m64 = new("m64", [64, 1])
    c_sb = new("c_sb", [P, KC, 2])
    sc = new("sc", [P, 2, KC, 2])
    mods = new("mods", [P, DEPTH * 3, 2, KC])
    amul = new("amul", [P, DEPTH, 2, KC])
    bada_sb = new("bada_sb", [P, DEPTH * 3, KC])
    normw_sb = new("normw_sb", [P, DEPTH, KC])
    finalw_sb = new("finalw_sb", [P, KC])
    ssmw_sb = new("ssmw_sb", [P, DEPTH, KC])
    convw_sb = new("convw_sb", [P, DEPTH, NCONV, TAPS + 1])
    dtb_sb = new("dtb_sb", [32, DEPTH])
    ea = new("ea", [32, DEPTH])
    dskip_sb = new("dskip_sb", [P, DEPTH, NH])
    lnw_sb = new("lnw_sb", [P, DEPTH, KC])
    bst = new("bst", [P, NCH, 12])
    mv = new("mv", [P, NCH, 2])
    rv = new("rv", [P, NCH, 1])
    rst = new("rst", [P, 2, NCH])
    eps_sb = new("eps_sb", [P, 1])

    acc = [ctx.enter_context(nc.psum_tensor(f"acc{i}", [P, 2, 512], F32)) for i in range(2)]
    X = [ctx.enter_context(nc.psum_tensor(f"X{i}", [P, 512], F32)) for i in range(4)]

    def sem(name):
        return ctx.enter_context(nc.semaphore(name))

    w_landed = [sem("w_landed0"), sem("w_landed1")]
    w_split, tile_done, w_go = sem("w_split"), sem("tile_done"), sem("w_go")
    acc_free = [sem("acc_free0"), sem("acc_free1")]
    consts_in, consts_made, x_in = sem("consts_in"), sem("consts_made"), sem("x_in")
    x_stored, out_done, wsp_in = sem("x_stored"), sem("out_done"), sem("wsp_in")
    st_in, st_stored = sem("st_in"), sem("st_stored")
    ada_in = [sem("ada_in0"), sem("ada_in1")]
    ada_used, ada_mm = sem("ada_used"), sem("ada_mm")
    c_in, ct_ready, mods_ready = sem("c_in"), sem("ct_ready"), sem("mods_ready")
    sq_ready, sq_used, ssq_ready, stat_ready = sem("sq_ready"), sem("sq_used"), sem("ssq_ready"), sem("stat_ready")
    root_ready, rstd_ready, rbc_ready = sem("root_ready"), sem("rstd_ready"), sem("rbc_ready")
    hpre_ready, hhi_ready, h_ready = sem("hpre_ready"), sem("hhi_ready"), sem("h_ready")
    dte_arg, dte_ready = sem("dte_arg"), sem("dte_ready")
    dtu_ready, dtl_ready, dta_ready = sem("dtu_ready"), sem("dtl_ready"), sem("dta_ready")
    tmT_ready, tm_ready, cum_mm, adup_ready = sem("tmT_ready"), sem("tm_ready"), sem("cum_mm"), sem("adup_ready")
    cumT_mm, cum_ready, ex_arg, ex_ready = sem("cumT_mm"), sem("cum_ready"), sem("ex_arg"), sem("ex_ready")
    pads_ready, cv_ready, cvt_ready, conv_done = sem("pads_ready"), sem("cv_ready"), sem("cvt_ready"), sem("conv_done")
    tp_ready, tp_out, ln_ready = sem("tp_ready"), sem("tp_out"), sem("ln_ready")
    bt_mm, bt_ready, xw_ready, s_mm, s_out = sem("bt_mm"), sem("bt_ready"), sem("xw_ready"), sem("s_mm"), sem("s_out")
    scan_done, vvar, vroot = sem("scan_done"), sem("vvar"), sem("vroot")
    fbg_ready, t_ready, d_ready, e_ready = sem("fbg_ready"), sem("t_ready"), sem("d_ready"), sem("e_ready")
    m_ready, y_ready = sem("m_ready"), sem("y_ready")
    zt_ready = sem("zt_ready")
    pbb_mm, pbb_ready, sp_mm, sp_used = sem("pbb_mm"), sem("pbb_ready"), sem("sp_mm"), sem("sp_used")
    ya_ready, yghi_ready, yg_ready = sem("ya_ready"), sem("yghi_ready"), sem("yg_ready")
    yT_mm, y2_ready, ymhi_ready, ym_ready = sem("yT_mm"), sem("y2_ready"), sem("ymhi_ready"), sem("ym_ready")
    ry_ready, gt_ready, mg_ready, mhi_ready, mh_ready = sem("ry_ready"), sem("gt_ready"), sem("mg_ready"), sem("mhi_ready"), sem("mh_ready")
    fin_ready = sem("fin_ready")
    s_act, s_dve, s_pool = sem("s_act"), sem("s_dve"), sem("s_pool")

    def acc_of(t):
        return acc[t % 2]

    def f(ap):
        return ap.bitcast(F32)

    def chunk_off(c):
        return 0 if c == 0 else LAT0 + P * (c - 1)

    def xcols(pair, c):
        return pair[1][:, 0:P] if c == 0 else pair[0][:, P * (c - 1):P * c]

    def evacuated(eng, t):
        eng.wait_ge(acc_free[t % 2], t // 2 + 1)

    def halves(buf):
        return buf[:, 0:TOK].rearrange("p (b n) -> p b n", b=2)

    block = ctx.enter_context(nc.Block())

    @block.sync
    def _(sp):
        def weight(t, slot):
            sp.dma_start(w_st[:, slot, :], wts[t, :, :]).then_inc(w_landed[slot], 16)

        def ada(n):
            if n >= 2:
                sp.wait_ge(ada_used, n - 1)
            L, q, hf = (JOBS_FIRST + JOBS_LATER)[n // 4]
            sp.dma_start(ada_st[:, n % 2, :, :], wada[L, q, hf, n % 4, :, :, :]).then_inc(ada_in[n % 2], 16)

        sp.dma_start(c_sb[:, :, :], cT).then_inc(c_in, 16)
        for n in range(2):
            ada(n)
        for dst, src in ((bada_sb, bada), (normw_sb, normw), (finalw_sb, finalw), (ssmw_sb, ssmw),
                         (convw_sb, convw), (dtb_sb, dtb), (ea, alog), (dskip_sb, dskip), (lnw_sb, lnw)):
            dst = dst[:]
            sp.dma_start(dst, src).then_inc(consts_in, 16)
        for n in range(2, 16):
            ada(n)
            if n in (8, 9):
                weight(n - 8, n - 8)

        def stream(lo, hi):
            with sp.Fori(lo // 2, hi // 2) as i:
                for slot in range(2):
                    sp.wait_ge(w_split, 2 * i + slot - 1)
                    weight(2 * i + slot, slot)

        stream(2, 50)
        for n in range(16, 48):
            t = 34 + n
            sp.wait_ge(w_split, t - 1)
            weight(t, t % 2)
            if n == 16:
                sp.wait_ge(sp_used, 8)
            ada(n)
        stream(82, DEPTH * N_TILES)
        for k in range(KC):
            sp.wait_ge(fin_ready, k + 1)
            sp.dma_start(yT[:, k, :], xr[:, k, :]).then_inc(out_done, 16)
        sp.wait_ge(out_done, 16 * KC)
        sp.wait_ge(st_stored, 32 * NG * DEPTH)
        sp.wait_ge(x_stored, 16)

    @block.gpsimd
    def _(pool):
        own = Chain(pool, s_pool)
        nc.gpsimd.memset(tri[:, :, :], 1.0)
        nc.gpsimd.memset(maskb[:, :], 1.0)
        nc.gpsimd.memset(ident[:, :], 0.0)
        nc.gpsimd.memset(ones[:, :], 1.0)
        nc.gpsimd.memset(sel32[:, :], 0.0)
        nc.gpsimd.memset(eps_sb[:, :], EPS)
        own.link(nc.gpsimd.memset(dupm[:, :], 0.0))
        for d in range(2):
            nc.gpsimd.affine_select(out=tri[:, d, :], in_=tri[:, d, :], compare_op=ALU.is_ge, fill=0.0,
                                    base=-d, pattern=[[1, P]], channel_multiplier=-1)
        nc.gpsimd.affine_select(out=maskb[:, :], in_=maskb[:, :], compare_op=ALU.is_ge, fill=0.0,
                                base=0, pattern=[[-1, P]], channel_multiplier=1)
        nc.gpsimd.affine_select(out=ident[:, :], in_=ident[:, :], compare_op=ALU.not_equal, fill=1.0,
                                base=0, pattern=[[-1, P]], channel_multiplier=1)
        for d, sign in ((0, 1.0), (1, -1.0)):
            for part in range(2):
                cols = sel32[:, NH * d:NH * (d + 1)]
                own.link(nc.gpsimd.affine_select(out=cols, in_=cols, compare_op=ALU.not_equal, fill=sign,
                                                 base=-(32 * d + 16 * part), pattern=[[-1, NH]],
                                                 channel_multiplier=1))
            own.link(nc.gpsimd.affine_select(out=dupm[:, :], in_=dupm[:, :], compare_op=ALU.not_equal, fill=-1.0,
                                             base=-(32 * d + 16), pattern=[[-1, NH]], channel_multiplier=1))
        nc.gpsimd.tensor_copy(sel[:, :], sel32[:, :]).then_inc(consts_made, 1)

        def split(slot, landed, done):
            pool.wait_ge(w_landed[slot], landed)
            if done is not None:
                pool.wait_ge(tile_done, done)
                pool.sem_inc(w_go, 1)
            nc.gpsimd.tensor_copy(w_hi[:, slot, :], w_st[:, slot, :]).then_inc(s_pool, 1)

        def split_lo(slot, n):
            pool.wait_ge(s_pool, n)
            nc.gpsimd.tensor_tensor(w_lo[:, slot, :], w_st[:, slot, :], f(w_hi[:, slot, :]),
                                    ALU.subtract).then_inc(w_split, 1)

        base = own.n
        for slot in range(2):
            split(slot, 16, None)
            split_lo(slot, base + slot + 1)
        with pool.Fori(1, DEPTH * N_TILES // 2) as i:
            for slot in range(2):
                split(slot, 16 * i + 16, 2 * i + slot - 1)
                split_lo(slot, 2 * i + (base + slot + 1))

    @block.tensor
    def _(pe):
        mm = nc.tensor.matmul

        def tile(t, hi, lo, ready=None, hooks=()):
            pe.wait_ge(w_split, t + 1)
            if t >= 2:
                pe.wait_ge(acc_free[t % 2], t // 2)
            a, s = acc_of(t), t % 2
            for k in range(KC):
                if ready is not None:
                    ready(k)
                cols = slice(k * P, (k + 1) * P)
                for n, (w, x) in enumerate(((w_hi, hi), (w_hi, lo), (w_lo, hi))):
                    for hf in range(2):
                        last = mm(a[:, hf, 0:HALF], w[:, s, cols], x[:, k, hf * HALF:(hf + 1) * HALF],
                                  start=(k == 0 and n == 0), stop=(k == KC - 1 and n == 2))
                if k == KC - 1:
                    last.then_inc(tile_done, 1)
                for at, hook in hooks:
                    if at == k + 1:
                        hook()

        def job_mm(n):
            pe.wait_ge(ada_used, 4 * (n + 1))
            for v in range(2):
                for j in range(4):
                    last = mm(X[2][:, 4 * v + j:4 * v + j + 1], ada_acc[n % 2][:, v, P * j:P * (j + 1)],
                              ones[:, 0:1], start=True, stop=True)
            last.then_inc(ada_mm, 1)

        def stat_mm(n):
            pe.wait_ge(ssq_ready, n + 1)
            for c in range(NCH):
                last = mm(X[0][:, c:c + 1], ssq[:, P * c:P * (c + 1)], ones[:, 0:1], start=True, stop=True)
            last.then_inc(stat_ready, 1)

        def stat_bc(n):
            pe.wait_ge(rstd_ready, n + 1)
            for c in range(NCH):
                last = mm(xcols((X[0], X[1]), c), rst[:, 1, c:c + 1].broadcast_to([P, P]), ident[:, :],
                          start=True, stop=True)
            last.then_inc(rbc_ready, 1)

        def transposes(src, n):
            if n > 0:
                pe.wait_ge(tp_out, n)
            for c in range(NCH):
                last = nc.tensor.transpose(xcols((X[0], X[1]), c), src(c), ident[:, :])
            last.then_inc(tp_ready, 1)

        def dt_cums(L):
            pe.wait_ge(dta_ready, L + 1)
            for c in range(NCH):
                last = nc.tensor.transpose(X[2][:, 64 * c:64 * (c + 1)], dta[:, P * c:P * (c + 1)], ident[0:64, 0:64])
            last.then_inc(tmT_ready, 1)

        def dt_cums2(L):
            pe.wait_ge(tm_ready, L + 1)
            mm(X[3][:, 0:80], tri[:, 0, :], tm[:, :, 32:48], start=True, stop=True)
            mm(X[3][:, 80:160], tri[:, 1, :], tm[:, :, 48:64], start=True, stop=True)
            mm(X[3][:, 160:320], ones[:, :], tm[:, :, 32:64], start=True, stop=True).then_inc(cum_mm, 1)

        def dt_cums3(L):
            pe.wait_ge(adup_ready, L + 1)
            for d in range(2):
                for c in range(NCH):
                    last = mm(xcols((X[0], X[1]), c)[32 * d:32 * (d + 1), :],
                              adup[:, c, 2 * d:2 * d + 2, :].rearrange("p r h -> p (r h)"), tri[:, d, :], start=True, stop=True)
            last.then_inc(cumT_mm, 1)

        def a_burst(L, a):
            if a > 0:
                c, g = A_UNITS[a - 1]
                n = NU * L + a
                pe.wait_ge(bt_ready, n)
                pe.wait_ge(xw_ready, n)
                if n > 1:
                    pe.wait_ge(s_out, n - 1)
                s = (a - 1) % 2
                cols = slice(0, GC) if c == 1 else slice(GC, 2 * GC) if c == NCH - 1 else slice(0, 2 * GC)
                mm(X[3][:, cols], bt[:, s, :], xw[:, s, :, :, :].rearrange("p d h w -> p (d h w)")[:, cols],
                   start=True, stop=True).then_inc(s_mm, 1)
            if a < NU:
                c, g = A_UNITS[a]
                if c == 0:
                    pe.wait_ge(tp_out, 16 * L + 2 * (g + 1))
                off = chunk_off(c)
                nc.tensor.transpose(X[2][:, 0:P], bc[:, g, off:off + P], ident[:, :]).then_inc(bt_mm, 1)

        def b_burst(L, b):
            if b > 0:
                c, g = B_UNITS[b - 1]
                pe.wait_ge(m_ready, NU * L + b)
                if b - 1 == HPG:
                    pe.wait_ge(scan_done, L + 1)
                off = chunk_off(c)
                for h in range(HPG):
                    y = X[3][:, h * HD:(h + 1) * HD]
                    mm(y, mmat[:, 0, h, :], xfb[:, 0, h, :], start=True, stop=False)
                    last = mm(y, mmat[:, 1, h, :], xfb[:, 1, h, :], start=False, stop=True)
                if c > 0:
                    cg = bc[:, 4 + g, off:off + P]
                    cols = slice(g * GC, (g + 1) * GC)
                    mm(X[2][:, P:P + GC], cg, states[2 * (c - 1)][:, cols], start=True, stop=True)
                    last = mm(X[3][:, GC:2 * GC], cg, states[2 * (c - 1) + 1][:, cols], start=True, stop=True)
                if b == NU:
                    last.then_inc(fbg_ready, 1)
            if b < NU:
                c, g = B_UNITS[b]
                off = chunk_off(c)
                if b == 0:
                    pe.wait_ge(tp_out, 16 * (L + 1))
                    pe.wait_ge(s_out, NU * (L + 1))
                for d in range(2):
                    for h in range(HPG):
                        j = NH * d + HPG * g + h
                        mm(X[d][:, P * h:P * (h + 1)], sel[:, j:j + 1].broadcast_to([64, P]),
                           cum_t[:, P * c:P * (c + 1)], start=True, stop=True)
                mm(X[2][:, 0:P], bc[:, g, off:off + P], bc[:, 4 + g, off:off + P],
                   start=True, stop=True).then_inc(fbg_ready, 1)

        def pbb_products(L):
            pe.wait_ge(wsp_in, 48 * (L + 1))
            pe.wait_ge(y_ready, NU * (L + 1))
            for g in range(8):
                o = X[2 + g // 4][:, P * (g % 4):P * (g % 4 + 1)]
                mm(o, lnb_sb[:, P * g:P * (g + 1)], wsp_sb[:, g, :], start=True, stop=False)
                last = mm(o, ones[0:1, :], bsp_row[0:1, P * g:P * (g + 1)], start=False, stop=True)
            last.then_inc(pbb_mm, 1)

        def spatial(L, g):
            if g == 0:
                pe.wait_ge(ln_ready, NCH * (L + 1))
                pe.wait_ge(pbb_ready, 2 * (L + 1))
            else:
                pe.wait_ge(sp_used, 8 * L + g)
            for c in range(NCH):
                last = mm(xcols((X[2], X[3]), c), v_tok[:, c, P * g:P * (g + 1)], wsp_sb[:, g, :],
                          start=True, stop=True)
            last.then_inc(sp_mm, 1)

        def y_transposes(L, j):
            if j == 0:
                pe.wait_ge(y_ready, NU * (L + 1))
            else:
                pe.wait_ge(y2_ready, 8 * L + j)
            for c in range(NCH):
                last = nc.tensor.transpose(xcols((X[0], X[1]), c), x_tok[:, c, P * j:P * (j + 1)], ident[:, :])
            last.then_inc(yT_mm, 1)

        pe.wait_ge(consts_made, 1)
        for n in range(4):
            job_mm(n)
        for L in range(DEPTH):
            T0 = L * N_TILES
            stat_mm(2 * L)
            stat_bc(2 * L)
            h = (h_hi, h_lo)
            tile(T0, *h, ready=lambda k: pe.wait_ge(h_ready, 8 * L + k + 1))
            for i in range(NCONV):
                tile(T0 + T_CONV + i, *h)
                if i == 2:
                    dt_cums(L)
                if i == 4:
                    dt_cums2(L)
                if i == 5:
                    dt_cums3(L)
                if i >= 10:
                    j = i - 10
                    pe.wait_ge(conv_done, NCONV * L + 9 + j)
                    if j == 0:
                        pe.wait_ge(cum_ready, L + 1)
                    transposes(lambda c: xo[:, j % 2, chunk_off(c):chunk_off(c) + P], 16 * L + j)
            for i in range(8):
                def bursts(n):
                    return lambda: a_burst(L, n)
                hooks = [(s, bursts(3 * i + n)) for n, s in enumerate(A_STEPS) if 3 * i + n <= NU]
                tile(T0 + T_V + i, *h, hooks=hooks)
                if i < 2:
                    j = 6 + i
                    pe.wait_ge(conv_done, NCONV * L + 9 + j)
                    transposes(lambda c: xo[:, j % 2, chunk_off(c):chunk_off(c) + P], 16 * L + j)
                if i >= 1:
                    evacuated(pe, T0 + T_V + i - 1)
                    transposes(lambda c: c_buf[(i - 1) % 2][:, P * c:P * (c + 1)], 16 * L + 7 + i)
            for n in range(16):
                hooks = []
                for b, at in enumerate(B_STEPS):
                    if 8 * n < at <= 8 * (n + 1):
                        hooks.append((at - 8 * n, (lambda b=b: b_burst(L, b))))
                tile(T0 + T_UZ + n, *h, hooks=hooks)
                if n == 0:
                    evacuated(pe, T0 + T_V + 7)
                    transposes(lambda c: c_buf[1][:, P * c:P * (c + 1)], 16 * L + 15)
            for j in range(8):
                hooks = [(5, lambda: pbb_products(L))] if j == 0 else []
                tile(T0 + T_ZM + j, *h, hooks=hooks)
                y_transposes(L, j)
                spatial(L, j)
            for j in range(8):
                t = T0 + T_S5 + 4 * j
                job = 4 + j
                tile(t, *h)
                if j == 0:
                    stat_mm(2 * L + 1)
                tile(t + 1, yg_hi, yg_lo,
                     ready=(lambda k: pe.wait_ge(yg_ready, 8 * L + k + 1)) if j == 0 else None)
                if j == 0:
                    stat_bc(2 * L + 1)
                if L == 0 and j > 0:
                    job_mm(job - 1)
                tile(t + 2, *h)
                tile(t + 3, ym_hi, ym_lo,
                     ready=(lambda k: pe.wait_ge(ym_ready, 8 * L + k + 1)) if j == 0 else None)
            if L == 0:
                job_mm(11)
            for j in range(8):
                tile(T0 + T_OUT + j, *h,
                     ready=(lambda k: pe.wait_ge(mh_ready, 8 * L + k + 1)) if j == 0 else None)
        stat_mm(2 * DEPTH)
        stat_bc(2 * DEPTH)

    @block.scalar
    def _(act):
        own = Chain(act, s_act)
        A = nc.scalar.activation

        def free(t, ins):
            ins.then_inc(acc_free[t % 2], 1)

        def pieces(a, dst_ctx, dst_lat, L, parts=P):
            n0 = (HALF - CTX) // GW
            if L % 2 == 0:
                lat = dst_lat.rearrange("p (r w) -> p r w", w=GW)
            else:
                lat = dst_lat.rearrange("p (w r) -> p r w", r=GH)
            return [(dst_ctx, a[0:parts, 0, 0:CTX]),
                    (lat[:, 0:n0, :], a[0:parts, 0, CTX:HALF].rearrange("p (r w) -> p r w", w=GW)),
                    (lat[:, n0:GH, :], a[0:parts, 1, 0:HALF].rearrange("p (r w) -> p r w", w=GW))]

        def root(n):
            act.wait_ge(stat_ready, n + 1)
            A(rst[:, 0, :], X[0][:, 0:NCH], ACT.Sqrt, scale=1.0 / DM, bias=eps_sb[:, 0:1]).then_inc(root_ready, 1)

        def square(n, k, src):
            if k >= 2:
                act.wait_ge(sq_used, 7 * n + k - 1)
            elif n > 0:
                act.wait_ge(ssq_ready, n)
            A(c_buf[2 + k % 2][:, :], src, ACT.Square).then_inc(sq_ready, 1)

        def tp_copy(dst, n):
            act.wait_ge(tp_ready, n + 1)
            A(dst[:, 1:NCH, :], X[0][:, :].rearrange("p (c n) -> p c n", n=P), ACT.Copy)
            A(dst[:, 0, :], X[1][:, 0:P], ACT.Copy).then_inc(tp_out, 1)

        act.dma_start(xr[:, :, :], xT).then_inc(x_in, 16)
        act.wait_ge(c_in, 16)
        A(sc[:, 0, :, :], c_sb[:, :, :], ACT.Tanh, scale=0.5).then_inc(ct_ready, 1)
        act.wait_ge(consts_in, 16 * 9)
        own.link(A(ea[:, :], ea[:, :], ACT.Exp))
        act.wait_ge(consts_made, 1)
        act.wait_ge(x_in, 16)
        for k in range(KC):
            square(0, k, xr[:, k, :])

        for L in range(DEPTH):
            T0 = L * N_TILES

            root(2 * L)
            for k in range(KC):
                act.wait_ge(hpre_ready, 8 * L + k + 1)
                for v, cols in ((0, slice(0, CTX)), (1, slice(CTX, TOK))):
                    last = A(h_hi[:, k, cols], c_buf[k % 4][:, cols], ACT.Identity, bias=mods[:, 3 * L, v, k:k + 1])
                last.then_inc(hhi_ready, 1)

            act.wait_ge(tile_done, T0 + 1)
            for dst, src in pieces(acc_of(T0), c_buf[0][0:32, 0:CTX], c_buf[0][0:32, CTX:TOK], L, 32):
                last = A(dst, src, ACT.Identity, bias=dtb_sb[:, L:L + 1])
            free(T0, last)

            for i in range(NCONV + 1):
                if i < NCONV:
                    t = T0 + T_CONV + i
                    act.wait_ge(tile_done, t + 1)
                    if i >= 2:
                        act.wait_ge(cv_ready, NCONV * L + i - 1)
                    else:
                        act.wait_ge(pads_ready, L + 1)
                    r = raw[:, i % 2, :]
                    for dst, src in pieces(acc_of(t), r[:, PAD:PAD + CTX], r[:, PAD + LAT0:PAD + LAT0 + LAT], L):
                        last = A(dst, src, ACT.Copy)
                    free(t, last)
                if i == 0:
                    act.wait_ge(dte_arg, L + 1)
                    A(c_buf[1][0:32, :], c_buf[1][0:32, :], ACT.Exp, scale=-1.0).then_inc(dte_ready, 1)
                    act.wait_ge(dtu_ready, L + 1)
                    A(c_buf[3][0:32, :], c_buf[2][0:32, :], ACT.Ln).then_inc(dtl_ready, 1)
                if i == 3:
                    act.wait_ge(tmT_ready, L + 1)
                    A(tm[:, :, :], X[2][:, 0:NCH * 64].rearrange("p (c r) -> p c r", r=64), ACT.Copy)\
                        .then_inc(tm_ready, 1)
                if i == 7:
                    act.wait_ge(ex_arg, L + 1)
                    A(ex[:, :, :, :], ex[:, :, :, :], ACT.Exp).then_inc(ex_ready, 1)
                if i >= 1:
                    n = NCONV * L + i - 1
                    act.wait_ge(cv_ready, n + 1)
                    if n > 0:
                        act.wait_ge(conv_done, n)
                    A(cvt[:, 0:CW], cv[:, (i - 1) % 2, 0:CW], ACT.Tanh).then_inc(cvt_ready, 1)
                if 11 <= i:
                    j = i - 11
                    if L > 0 and j == 0:
                        act.wait_ge(x_stored, 16)
                    tp_copy(x_tok[:, :, P * j:P * (j + 1)], 16 * L + j)

            def a_copies(a):
                if a > 0:
                    c, g = A_UNITS[a - 1]
                    n = NU * L + a
                    act.wait_ge(s_mm, n)
                    cols = slice(g * GC, (g + 1) * GC)
                    if c == 0:
                        if g > 0 or L > 0:
                            act.wait_ge(st_stored, 32 * (NG * L + g))
                        A(ctx_st[:, :], X[3][:, :], ACT.Copy).then_inc(s_out, 1)
                        act.wait_ge(s_out, n)
                        for d in range(2):
                            act.dma_start(st_out[L, d, :, cols], ctx_st[:, d * GC:(d + 1) * GC])\
                                .then_inc(st_stored, 16)
                    else:
                        if c < NCH - 1:
                            last = A(states[2 * c][:, cols], X[3][:, 0:GC], ACT.Copy)
                        if c > 1:
                            last = A(states[2 * (c - 2) + 1][:, cols], X[3][:, GC:2 * GC], ACT.Copy)
                        last.then_inc(s_out, 1)
                if a < NU:
                    n = NU * L + a
                    act.wait_ge(bt_mm, n + 1)
                    if a >= 2:
                        act.wait_ge(s_mm, n - 1)
                    A(bt[:, a % 2, :], X[2][:, 0:P], ACT.Copy).then_inc(bt_ready, 1)

            act.dma_start(states[0][:, :], h0[L, 0, :, :]).then_inc(st_in, 16)
            act.dma_start(states[2 * (NCH - 2) + 1][:, :], h0[L, 1, :, :]).then_inc(st_in, 16)
            for i in range(8):
                t = T0 + T_V + i
                for n in range(3):
                    if 3 * i + n <= NU:
                        a_copies(3 * i + n)
                act.wait_ge(tile_done, t + 1)
                if i >= 2:
                    act.wait_ge(tp_ready, 16 * L + 8 + i - 1)
                free(t, A(halves(c_buf[i % 2]), acc_of(t)[:, :, 0:HALF], ACT.Gelu_apprx_tanh))
                if i < 2:
                    tp_copy(x_tok[:, :, P * (6 + i):P * (7 + i)], 16 * L + 6 + i)
                if i >= 1:
                    tp_copy(v_tok[:, :, P * (i - 1):P * i], 16 * L + 7 + i)

            for what, n in order_uz():
                if what == "burst":
                    if n < NU:
                        c, g = B_UNITS[n]
                        act.wait_ge(fbg_ready, (NU + 1) * L + n + 1)
                        for h in range(HPG):
                            j = HPG * g + h
                            last = A(dmat[:, h, :], X[0][:, P * h:P * (h + 1)], ACT.Identity, bias=ncf[:, c, j:j + 1])
                        last.then_inc(t_ready, 1)
                        act.wait_ge(d_ready, NU * L + n + 1)
                        A(dmat[:, :, :], dmat[:, :, :], ACT.Exp).then_inc(e_ready, 1)
                    continue
                t = T0 + T_UZ + n
                act.wait_ge(tile_done, t + 1)
                if n % 2 == 0:
                    free(t, A(halves(uz[:, n // 2, :]), acc_of(t)[:, :, 0:HALF], ACT.Gelu_apprx_tanh))
                else:
                    if n > 1:
                        evacuated(act, t - 2)
                    A(halves(c_buf[0]), acc_of(t)[:, :, 0:HALF], ACT.Tanh, scale=0.5).then_inc(zt_ready, 1)
                if n == 0:
                    tp_copy(v_tok[:, :, P * 7:P * 8], 16 * L + 15)
                if n == 3:
                    act.wait_ge(vvar, L + 1)
                    A(rv[:, :, :], mv[:, :, 1:2], ACT.Sqrt, bias=eps_sb[:, 0:1]).then_inc(vroot, 1)

            act.wait_ge(y_ready, NU * (L + 1))
            act.dma_start(wsp_sb[:, :, :], wsp[L, :, :, :]).then_inc(wsp_in, 16)
            act.dma_start(lnb_sb[:, :], lnb[L:L + 1, :].partition_broadcast(P)).then_inc(wsp_in, 16)
            act.dma_start(bsp_row[:, :], bsp[L:L + 1, :]).then_inc(wsp_in, 16)
            for j in range(8):
                t = T0 + T_ZM + j
                if j == 0:
                    act.wait_ge(pbb_mm, L + 1)
                    for i in range(2):
                        A(pbb[:, 4 * i:4 * i + 4, :], X[2 + i][:, :].rearrange("p (g n) -> p g n", n=P), ACT.Copy)\
                            .then_inc(pbb_ready, 1)
                act.wait_ge(tile_done, t + 1)
                if j > 0:
                    evacuated(act, t - 1)
                else:
                    evacuated(act, T0 + T_UZ + 15)
                A(halves(c_buf[0]), acc_of(t)[:, :, 0:HALF], ACT.Tanh, scale=0.5).then_inc(zt_ready, 1)
                act.wait_ge(y2_ready, 8 * L + j + 1)
                square(2 * L + 1, j, c_buf[1][:, :])
                A(ym_hi[:, j, :], c_buf[1][:, :], ACT.Copy, scale=ssmw_sb[:, L, j:j + 1]).then_inc(ymhi_ready, 1)
                act.wait_ge(ya_ready, 8 * L + j + 1)
                A(yg_hi[:, j, :], c_buf[4][:, :], ACT.Copy).then_inc(yghi_ready, 1)

            act.dma_start(xr[:, :, :], xT if L == 0 else x_mid).then_inc(x_in, 16)
            for j in range(8):
                t = T0 + T_S5 + 4 * j
                for b, tt in ((0, t), (1, t + 2)):
                    act.wait_ge(tile_done, tt + 1)
                    if j > 0:
                        evacuated(act, t - 3 + 2 * b)
                    free(tt, A(halves(c_buf[b]), acc_of(tt)[:, :, 0:HALF], ACT.Tanh, scale=0.5))
                    if j == 0 and b == 0:
                        root(2 * L + 1)
                        act.wait_ge(rbc_ready, 2 * L + 2)
                        A(c_buf[2][:, CTX:TOK], X[0][:, :], ACT.Copy, scale=0.5)
                        A(c_buf[2][:, 0:CTX], X[1][:, 0:P], ACT.Copy, scale=0.5).then_inc(ry_ready, 1)
            for k in range(KC):
                act.wait_ge(mg_ready, 8 * L + k + 1)
                A(h_hi[:, k, :], mg[:, k, :], ACT.Copy).then_inc(mhi_ready, 1)
            for j in range(8):
                evacuated(act, T0 + T_OUT + j)
                square(2 * L + 2, j, xr[:, j, :])
            if L < DEPTH - 1:
                act.dma_start(x_mid, xr[:, :, :]).then_inc(x_stored, 16)
        root(2 * DEPTH)

    @block.vector
    def _(dve):
        own = Chain(dve, s_dve)
        TT, STT, TS = nc.vector.tensor_tensor, nc.vector.scalar_tensor_tensor, nc.vector.tensor_scalar

        def free(t, ins):
            ins.then_inc(acc_free[t % 2], 1)

        def per_head(ap, w):
            return ap.unsqueeze(2).broadcast_to([P, ap.shape[1], w])

        def ada(n):
            job, part = n // 4, n % 4
            dve.wait_ge(ada_in[n % 2], 16 * (n // 2 + 1))
            if part == 0 and job >= 2:
                dve.wait_ge(ada_mm, job - 1)
            if part > 0:
                dve.wait_ge(ada_used, n)
            for kk in range(2):
                k = 2 * part + kk
                for v in range(2):
                    o, w, s = ada_acc[job % 2][:, v, :], ada_st[:, n % 2, kk, :], sc[:, 1, k, v:v + 1]
                    ins = TS(o, w, s, None, ALU.mult) if k == 0 else \
                        STT(out=o, in0=w, scalar=s, in1=o, op0=ALU.mult, op1=ALU.add)
                    if kk == 1 and v == 1:
                        ins.then_inc(ada_used, 1)
                    else:
                        own.mark(ins)
                if kk == 0:
                    own.wait()

        def job_out(n):
            L, q, hf = (JOBS_FIRST + JOBS_LATER)[n]
            dve.wait_ge(ada_mm, n + 1)
            cols = slice(4 * hf, 4 * hf + 4)
            own.link(TT(mods[:, 3 * L + q, :, cols], X[2][:, 0:8].rearrange("p (v j) -> p v j", v=2),
                        bada_sb[:, 3 * L + q, cols].unsqueeze(1).broadcast_to([P, 2, 4]), ALU.add))
            if q == 1 and hf == 1:
                own.link(STT(out=amul[:, L, :, :], in0=mods[:, 3 * L + 1, :, :], scalar=1.0,
                             in1=normw_sb[:, L, :].unsqueeze(1).broadcast_to([P, 2, KC]),
                             op0=ALU.add, op1=ALU.mult))

        def add_square(n, k):
            dve.wait_ge(sq_ready, 8 * n + k + 1)
            src = c_buf[2 + k % 2][:, :]
            ins = nc.vector.tensor_copy(ssq[:, :], src) if k == 0 else TT(ssq[:, :], ssq[:, :], src, ALU.add)
            if k < KC - 1:
                ins.then_inc(sq_used, 1)
                dve.wait_ge(sq_used, 7 * n + k + 1)
            else:
                ins.then_inc(ssq_ready, 1)

        def rstd(n):
            dve.wait_ge(root_ready, n + 1)
            nc.vector.reciprocal(rst[:, 1, :], rst[:, 0, :]).then_inc(rstd_ready, 1)

        dve.wait_ge(ct_ready, 1)
        own.link(STT(out=sc[:, 1, :, :], in0=sc[:, 0, :, :], scalar=1.0, in1=c_sb[:, :, :], op0=ALU.add, op1=ALU.mult))
        own.link(TS(sc[:, 1, :, :], sc[:, 1, :, :], 0.5, None, ALU.mult))
        dve.wait_ge(consts_in, 16 * 9)
        dve.wait_ge(consts_made, 1)
        own.link(nc.vector.tensor_reduce(m64[:, :], dupm[:, :], AXX, ALU.add))
        own.link(TS(convw_sb[:, :, :, :], convw_sb[:, :, :, :], 0.5, None, ALU.mult))
        for n in range(16):
            ada(n)
            if n == 8:
                for k in range(KC):
                    add_square(0, k)
            if n % 4 == 0 and n > 0:
                job_out(n // 4 - 1)
        job_out(3)

        for L in range(DEPTH):
            T0 = L * N_TILES

            rstd(2 * L)
            dve.wait_ge(rbc_ready, 2 * L + 1)
            SEG = ((0, slice(0, CTX), X[1][:, 0:CTX]), (1, slice(CTX, TOK), X[0][:, 0:LAT]))
            for k in range(KC + 1):
                if k < KC:
                    if k >= 4:
                        dve.wait_ge(h_ready, 8 * L + k - 3)
                    for v, cols, r in SEG:
                        last = STT(out=c_buf[k % 4][:, cols], in0=xr[:, k, cols], scalar=amul[:, L, v, k:k + 1],
                                   in1=r, op0=ALU.mult, op1=ALU.mult)
                    last.then_inc(hpre_ready, 1)
                if k > 0:
                    kk = k - 1
                    dve.wait_ge(hhi_ready, 8 * L + kk + 1)
                    for v, cols, r in SEG:
                        last = STT(out=h_lo[:, kk, cols], in0=c_buf[kk % 4][:, cols],
                                   scalar=mods[:, 3 * L, v, kk:kk + 1], in1=f(h_hi[:, kk, cols]),
                                   op0=ALU.add, op1=ALU.subtract)
                    last.then_inc(h_ready, 1)

            dve.wait_ge(h_ready, 8 * (L + 1))
            for at in (0, PAD + CTX, RAW - PAD):
                last = nc.vector.memset(raw[:, :, at:at + PAD], 0.0)
            last.then_inc(pads_ready, 1)

            def dt_abs():
                evacuated(dve, T0)
                x = c_buf[0][0:32, :]
                STT(out=c_buf[1][0:32, :], in0=x, scalar=-1.0, in1=x, op0=ALU.mult, op1=ALU.max).then_inc(dte_arg, 1)
                dve.wait_ge(dte_ready, L + 1)
                TS(c_buf[2][0:32, :], c_buf[1][0:32, :], 1.0, None, ALU.add).then_inc(dtu_ready, 1)

            def dt_finish():
                x, e, u, lu = (b[0:32, :] for b in c_buf[0:4])
                dve.wait_ge(dtu_ready, L + 1)
                STT(out=e, in0=u, scalar=1.0, in1=e, op0=ALU.subtract, op1=ALU.subtract)
                own.link(nc.vector.reciprocal(dta[0:32, :], u))
                own.link(TT(e, e, dta[0:32, :], ALU.mult))
                dve.wait_ge(dtl_ready, L + 1)
                own.link(TT(lu, lu, e, ALU.subtract))
                own.link(STT(out=dta[0:32, :], in0=x, scalar=0.0, in1=lu, op0=ALU.max, op1=ALU.add))
                TS(dta[32:64, :], dta[0:32, :], ea[:, L:L + 1], -1.0, ALU.mult, ALU.mult).then_inc(dta_ready, 1)

            def dup_a():
                dve.wait_ge(tm_ready, L + 1)
                for r in range(4):
                    last = nc.vector.tensor_copy(adup[:, :, r, :], tm[:, :, 32 + NH * (r // 2):48 + NH * (r // 2)])
                last.then_inc(adup_ready, 1)

            def decay_args():
                dve.wait_ge(cum_mm, L + 1)
                cf = X[3][:, 0:80].rearrange("p (c h) -> p c h", h=NH)
                eb = X[3][:, 80:160].rearrange("p (c h) -> p c h", h=NH)
                tot = X[3][:, 160:320].rearrange("p (c d h) -> p d c h", d=2, h=NH)
                TS(ncf[:, :, :], cf, -1.0, None, ALU.mult)
                nc.vector.tensor_copy(ebs[:, :, :], eb)
                nc.vector.tensor_copy(ex[:, 1, :, :], eb)
                nc.vector.tensor_copy(ex[:, 2, :, :], cf)
                nc.vector.tensor_copy(ex[:, 4, :, :], tot[:, 0])
                own.link(nc.vector.tensor_copy(ex[:, 5, :, :], tot[:, 1]))
                TT(ex[:, 0, :, :], ex[:, 4, :, :], ncf[:, :, :], ALU.add)
                TT(ex[:, 3, :, :], ex[:, 5, :, :], ebs[:, :, :], ALU.subtract).then_inc(ex_arg, 1)

            def cum_rows():
                dve.wait_ge(cumT_mm, L + 1)
                lat, cx = slice(P, TOK), slice(0, P)
                nc.vector.tensor_copy(cum_r[:, lat], X[0][0:64, :])
                own.link(nc.vector.tensor_copy(cum_r[:, cx], X[1][0:64, 0:P]))
                STT(out=cum_t[:, lat], in0=f(cum_r[:, lat]), scalar=m64[:, 0:1], in1=X[0][0:64, :],
                    op0=ALU.mult, op1=ALU.add)
                STT(out=cum_t[:, cx], in0=f(cum_r[:, cx]), scalar=m64[:, 0:1], in1=X[1][0:64, 0:P],
                    op0=ALU.mult, op1=ALU.add).then_inc(cum_ready, 1)

            def state_weights():
                dve.wait_ge(ex_ready, L + 1)
                for d in range(2):
                    last = TT(ex[:, d, :, :], ex[:, d, :, :], tm[:, :, NH * d:NH * (d + 1)], ALU.mult)
                own.link(last)

            dt_abs()
            for i in range(NCONV + 1):
                if i < NCONV:
                    evacuated(dve, T0 + T_CONV + i)
                    ch = (i + 8) % NCONV
                    w = convw_sb[:, L, ch, :]
                    r, o = raw[:, i % 2, :], cv[:, i % 2, 0:CW]
                    if NCONV * L + i > 1:
                        dve.wait_ge(conv_done, NCONV * L + i - 1)
                    own.link(TS(o, r[:, PAD:PAD + CW], w[:, PAD:PAD + 1], w[:, TAPS:TAPS + 1], ALU.mult, ALU.add))
                    for tap in (0, 1, 3, 4):
                        ins = STT(out=o, in0=r[:, tap:tap + CW], scalar=w[:, tap:tap + 1], in1=o,
                                  op0=ALU.mult, op1=ALU.add)
                        if tap < 4:
                            own.link(ins)
                        else:
                            ins.then_inc(cv_ready, 1)
                if i > 0:
                    n = i - 1
                    dve.wait_ge(cvt_ready, NCONV * L + i)
                    if n < 8:
                        dst = bc[:, n, :]
                    else:
                        dst = xo[:, n % 2, 0:CW]
                        if n >= 10:
                            dve.wait_ge(tp_ready, 16 * L + n - 9)
                    STT(out=dst, in0=cvt[:, 0:CW], scalar=1.0, in1=cv[:, n % 2, 0:CW],
                        op0=ALU.add, op1=ALU.mult).then_inc(conv_done, 1)
                if i == 0:
                    dt_finish()
                if i == 4:
                    dup_a()
                if i == 5:
                    decay_args()
                if i == 6:
                    cum_rows()
                if i == 8:
                    state_weights()

            for a, (c, g) in enumerate(A_UNITS):
                n = NU * L + a
                dve.wait_ge(tp_out, 16 * L + 2 * (g + 1))
                if a >= 2:
                    dve.wait_ge(s_mm, n - 1)
                xg = x_tok[:, c, g * GC:(g + 1) * GC].rearrange("p (h w) -> p h w", w=HD)
                for d in range(2):
                    last = TT(xw[:, a % 2, d, :, :], xg, per_head(ex[:, d, c, HPG * g:HPG * (g + 1)], HD), ALU.mult)
                last.then_inc(xw_ready, 1)

            dve.wait_ge(st_in, 32 * (L + 1))
            dve.wait_ge(s_out, NU * (L + 1))
            for i in range(NCH - 2):
                for d in range(2):
                    c = 1 + i if d == 0 else NCH - 1 - i
                    frm = states[2 * (c - 1) + d]
                    to = states[2 * c] if d == 0 else states[2 * (c - 2) + 1]
                    own.link(TT(scan_tmp[:, :].rearrange("p (h w) -> p h w", w=HD),
                                frm[:, :].rearrange("p (h w) -> p h w", w=HD),
                                per_head(ex[:, 4 + d, c, :], HD), ALU.mult))
                    ins = TT(to[:, :], to[:, :], scan_tmp[:, :], ALU.add)
                    if i == NCH - 3 and d == 1:
                        ins.then_inc(scan_done, 1)
                    else:
                        own.link(ins)

            def layer_norm():
                dve.wait_ge(tp_out, 16 * (L + 1))
                for c in range(NCH):
                    for hf in range(2):
                        last = nc.vector.bn_stats(bst[:, c, 6 * hf:6 * hf + 6], v_tok[:, c, 512 * hf:512 * (hf + 1)])
                own.link(last)
                for c in range(NCH):
                    last = nc.vector.bn_aggr(mv[:, c, :], bst[:, c, :])
                last.then_inc(vvar, 1)

            def layer_norm2():
                dve.wait_ge(vroot, L + 1)
                own.link(nc.vector.reciprocal(rv[:, :, :], rv[:, :, :]))
                for c in range(NCH):
                    TS(v_tok[:, c, :], v_tok[:, c, :], mv[:, c, 0:1], rv[:, c, 0:1], ALU.subtract, ALU.mult)\
                        .then_inc(ln_ready, 1)

            def b_unit(b):
                if b < NU:
                    c, g = B_UNITS[b]
                    hs = slice(HPG * g, HPG * (g + 1))
                    xg = x_tok[:, c, g * GC:(g + 1) * GC].rearrange("p (h w) -> p h w", w=HD)
                    dve.wait_ge(fbg_ready, (NU + 1) * L + b + 1)
                    TT(gm[:, 0, :], X[2][:, 0:P], tri[:, 0, :], ALU.mult)
                    TT(gm[:, 1, :], X[2][:, 0:P], maskb[:, :], ALU.mult)
                    for d in range(2):
                        TT(xfb[:, d, :, :], xg, per_head(tm[:, c, NH * d + HPG * g:NH * d + HPG * (g + 1)], HD), ALU.mult)
                    dve.wait_ge(t_ready, NU * L + b + 1)
                    for h in range(HPG):
                        j = HPG * g + h
                        last = STT(out=dmat[:, h, :], in0=X[1][:, P * h:P * (h + 1)], scalar=ebs[:, c, j:j + 1],
                                   in1=dmat[:, h, :], op0=ALU.add, op1=ALU.min)
                    last.then_inc(d_ready, 1)
                if b > 0:
                    c, g = B_UNITS[b - 1]
                    xf = x_tok[:, c, g * GC:(g + 1) * GC]
                    xg = xf.rearrange("p (h w) -> p h w", w=HD)
                    hs = slice(HPG * g, HPG * (g + 1))
                    ya, yb = yab[:, 0, :, :], yab[:, 1, :, :]
                    flat = [yab[:, i, :, :].rearrange("p h w -> p (h w)") for i in range(2)]
                    if b == NU:
                        dve.wait_ge(fbg_ready, (NU + 1) * (L + 1))
                    if c > 0:
                        TT(ya, X[2][:, P:P + GC].rearrange("p (h w) -> p h w", w=HD), per_head(ex[:, 2, c, hs], HD), ALU.mult)
                        own.link(TT(yb, X[3][:, GC:2 * GC].rearrange("p (h w) -> p h w", w=HD),
                                    per_head(ex[:, 3, c, hs], HD), ALU.mult))
                        own.link(TT(flat[0], flat[0], flat[1], ALU.add))
                        TT(yb, xg, per_head(dskip_sb[:, L, hs], HD), ALU.mult)
                        own.link(TT(flat[0], flat[0], X[3][:, 0:GC], ALU.add))
                        TT(xf, flat[0], flat[1], ALU.add).then_inc(y_ready, 1)
                    else:
                        own.link(TT(yb, xg, per_head(dskip_sb[:, L, hs], HD), ALU.mult))
                        TT(xf, flat[1], X[3][:, 0:GC], ALU.add).then_inc(y_ready, 1)
                if b < NU:
                    dve.wait_ge(e_ready, NU * L + b + 1)
                    for d in range(2):
                        last = TT(mmat[:, d, :, :], dmat[:, :, :],
                                  gm[:, d, :].unsqueeze(1).broadcast_to([P, HPG, P]), ALU.mult)
                    last.then_inc(m_ready, 1)

            for what, n in order_uz():
                if what == "burst":
                    b_unit(n)
                    continue
                t, j = T0 + T_UZ + n, n // 2
                if n % 2 == 1:
                    dve.wait_ge(zt_ready, 16 * L + j + 1)
                    if n == 1:
                        dve.wait_ge(tp_ready, 16 * (L + 1))
                    free(t, STT(out=halves(c_buf[1]), in0=halves(c_buf[0]), scalar=1.0,
                                in1=acc_of(t)[:, :, 0:HALF], op0=ALU.add, op1=ALU.mult))
                    evacuated(dve, t)
                    evacuated(dve, t - 1)
                    own.mark(TT(uz[:, j, :], uz[:, j, :], c_buf[1][:, :], ALU.mult))
                if n == 3:
                    layer_norm()
                if n == 5:
                    layer_norm2()

            own.wait()
            for j in range(8):
                t = T0 + T_ZM + j
                n = 8 * L + j
                dve.wait_ge(zt_ready, 16 * L + 8 + j + 1)
                if j > 0:
                    dve.wait_ge(ymhi_ready, n)
                    dve.wait_ge(ym_ready, n)
                free(t, STT(out=halves(c_buf[1]), in0=halves(c_buf[0]), scalar=1.0,
                            in1=acc_of(t)[:, :, 0:HALF], op0=ALU.add, op1=ALU.mult))
                evacuated(dve, t)
                dve.wait_ge(yT_mm, n + 1)
                cx = c_buf[1][:, 0:CTX]
                STT(out=cx, in0=X[1][:, 0:P], scalar=0.5, in1=cx, op0=ALU.mult, op1=ALU.mult)
                lat = c_buf[1][:, CTX:TOK].rearrange("p (r w) -> p r w", w=GW)
                src = X[0][:, :].rearrange("p (r w) -> p r w", w=GW) if L % 2 == 0 else \
                    X[0][:, :].rearrange("p (w r) -> p r w", r=GH)
                STT(out=lat, in0=src, scalar=0.5, in1=lat, op0=ALU.mult, op1=ALU.mult).then_inc(y2_ready, 1)
                dve.wait_ge(sp_mm, n + 1)
                if j > 0:
                    dve.wait_ge(yghi_ready, n)
                    dve.wait_ge(yg_ready, n)
                STT(out=c_buf[4][:, CTX:TOK].rearrange("p (c n) -> p c n", n=P),
                    in0=X[2][:, :].rearrange("p (c n) -> p c n", n=P), scalar=lnw_sb[:, L, j:j + 1],
                    in1=pbb[:, j, :].unsqueeze(1).broadcast_to([P, NCH - 1, P]), op0=ALU.mult, op1=ALU.add)
                STT(out=c_buf[4][:, 0:CTX], in0=X[3][:, 0:P], scalar=lnw_sb[:, L, j:j + 1], in1=pbb[:, j, :],
                    op0=ALU.mult, op1=ALU.add).then_inc(sp_used, 1)
                add_square(2 * L + 1, j)
                dve.wait_ge(sp_used, n + 1)
                STT(out=c_buf[4][:, :], in0=c_buf[4][:, :], scalar=0.5, in1=uz[:, j, :],
                    op0=ALU.mult, op1=ALU.mult).then_inc(ya_ready, 1)
                dve.wait_ge(ymhi_ready, n + 1)
                STT(out=ym_lo[:, j, :], in0=c_buf[1][:, :], scalar=ssmw_sb[:, L, j:j + 1], in1=f(ym_hi[:, j, :]),
                    op0=ALU.mult, op1=ALU.subtract).then_inc(ym_ready, 1)
                dve.wait_ge(yghi_ready, n + 1)
                TT(yg_lo[:, j, :], c_buf[4][:, :], f(yg_hi[:, j, :]), ALU.subtract).then_inc(yg_ready, 1)

            def merge_lo(k):
                dve.wait_ge(mhi_ready, 8 * L + k + 1)
                TT(h_lo[:, k, :], mg[:, k, :], f(h_hi[:, k, :]), ALU.subtract).then_inc(mh_ready, 1)

            for j in range(8):
                t = T0 + T_S5 + 4 * j
                if j == 0:
                    rstd(2 * L + 1)
                if L == 0:
                    ada(16 + 4 * j)
                for b, tt in ((0, t + 1), (1, t + 3)):
                    if b == 1 and j == 7:
                        for k in range(KC - 1):
                            merge_lo(k)
                    dve.wait_ge(tile_done, tt + 1)
                    evacuated(dve, tt - 1)
                    o = c_buf[4][:, :] if b == 0 else mg[:, j, :]
                    if b == 0 and j > 0:
                        dve.wait_ge(mg_ready, 8 * L + j)
                    free(tt, STT(out=halves(o), in0=halves(c_buf[b]), scalar=1.0, in1=acc_of(tt)[:, :, 0:HALF],
                                 op0=ALU.add, op1=ALU.mult))
                    if L == 0 and b == 0:
                        ada(17 + 4 * j)
                        if j > 0:
                            job_out(3 + j)
                        ada(18 + 4 * j)
                if j == 0:
                    dve.wait_ge(ry_ready, L + 1)
                evacuated(dve, t + 3)
                own.link(TT(mg[:, j, :], mg[:, j, :], c_buf[2][:, :], ALU.mult))
                STT(out=mg[:, j, :], in0=c_buf[4][:, :], scalar=0.5, in1=mg[:, j, :],
                    op0=ALU.mult, op1=ALU.add).then_inc(mg_ready, 1)
                if L == 0:
                    ada(19 + 4 * j)
            merge_lo(KC - 1)
            if L == 0:
                job_out(11)

            dve.wait_ge(x_in, 16 * (L + 2))
            for j in range(8):
                t = T0 + T_OUT + j
                dve.wait_ge(tile_done, t + 1)
                n0 = HALF
                for v, cols, src in ((0, slice(0, CTX), acc_of(t)[:, 0, 0:CTX]),
                                     (1, slice(CTX, n0), acc_of(t)[:, 0, CTX:HALF]),
                                     (1, slice(n0, TOK), acc_of(t)[:, 1, 0:HALF])):
                    last = STT(out=xr[:, j, cols], in0=src, scalar=mods[:, 3 * L + 2, v, j:j + 1],
                               in1=xr[:, j, cols], op0=ALU.mult, op1=ALU.add)
                free(t, last)
                if j > 0:
                    add_square(2 * L + 2, j - 1)
            add_square(2 * L + 2, 7)

        rstd(2 * DEPTH)
        dve.wait_ge(rbc_ready, 2 * DEPTH + 1)
        for k in range(KC):
            for cols, r in ((slice(0, CTX), X[1][:, 0:CTX]), (slice(CTX, TOK), X[0][:, 0:LAT])):
                last = STT(out=xr[:, k, cols], in0=xr[:, k, cols], scalar=finalw_sb[:, k:k + 1], in1=r,
                           op0=ALU.mult, op1=ALU.mult)
            last.then_inc(fin_ready, 1)

    ctx.close()


def kernel(**inputs):
    import numpy as np
    import concourse.bacc as bacc
    from concourse.bass_utils import run_bass_kernel_spmd

    a = {k: np.asarray(v) for k, v in inputs.items()}
    f32 = np.float32

    def tiles(w):
        L, _, n = w.shape
        return w.reshape(L, KC, P, n // P, P).transpose(0, 3, 2, 1, 4).reshape(L, n // P, P, KC * P)

    def cols(v):
        v = v.reshape(v.shape[:-1] + (v.shape[-1] // P, P))
        return np.ascontiguousarray(np.moveaxis(v, -1, 0))

    w_in = a["w_in"]
    s = np.cumsum([0, NCONV * P, DM, 32, DM, DM, DM, DM, DM])
    part = [w_in[:, :, s[i]:s[i + 1]] for i in range(8)]
    xbc, zm, dt, u, v, zg, glm, glg = part
    dt = np.concatenate([dt, np.zeros((DEPTH, DM, P - 32), f32)], axis=2)
    xbc_t, zm_t, u_t, v_t, zg_t, glm_t, glg_t = (tiles(w) for w in (xbc, zm, u, v, zg, glm, glg))
    om_t, og_t, out_t = tiles(a["w_out_m"]), tiles(a["w_out_g"]), tiles(a["w_out"])
    uz = np.stack([u_t, zg_t], axis=2).reshape(DEPTH, 16, P, KC * P)
    s5 = np.stack([glg_t, og_t, glm_t, om_t], axis=2).reshape(DEPTH, 32, P, KC * P)
    wts = np.concatenate([tiles(dt), xbc_t[:, 8:], xbc_t[:, :8], v_t, uz, zm_t, s5, out_t], axis=1)
    wts = wts.reshape(DEPTH * N_TILES, P, KC * P)
    wada = a["w_ada"].reshape(DEPTH, 4, 2, P, 3, 2, 512).transpose(0, 4, 5, 1, 3, 2, 6)
    x = np.concatenate([a["x_prompt"][0], a["x_sample"][0]], axis=0)
    xT = x.T.reshape(KC, P, TOK).transpose(1, 0, 2)
    conv = np.concatenate([a["conv_w"], a["conv_b"][:, None, :]], axis=1)
    conv = conv.reshape(DEPTH, TAPS + 1, NCONV, P).transpose(3, 0, 2, 1)
    h0 = a["state_ssm"][0].reshape(DEPTH, 2, DM, P).transpose(0, 1, 3, 2)
    ins = {
        "xT": xT, "wts": wts, "wada": wada,
        "cT": cols(np.stack([a["c_ctx"], a["c"][0]])).transpose(0, 2, 1),
        "bada": cols(a["b_ada"].reshape(DEPTH * 3, DM)), "normw": cols(a["norm_w"]),
        "finalw": cols(a["final_norm_w"]), "ssmw": cols(a["ssm_norm_w"]), "convw": conv,
        "dtb": a["dt_bias"].reshape(DEPTH, 32).T, "alog": a["a_log"].reshape(DEPTH, 32).T,
        "dskip": np.broadcast_to(a["d_skip"][None], (P, DEPTH, NH)), "lnw": cols(a["sgu_ln_w"]),
        "lnb": a["sgu_ln_b"], "wsp": a["w_sp"].transpose(0, 3, 1, 2), "bsp": a["b_sp"].reshape(DEPTH, DM),
        "h0": h0,
    }
    ins = {k: np.ascontiguousarray(v) for k, v in ins.items()}
    nc = bacc.Bacc("TRN2", target_bir_lowering=False, num_devices=1, dynamic_dma_scratch_size=1024)
    aps = {k: nc.dram_tensor(f"in_{k}", v.shape, F32, kind="ExternalInput").ap() for k, v in ins.items()}
    yT = nc.dram_tensor("yT", (P, KC, TOK), F32, kind="ExternalOutput").ap()
    st = nc.dram_tensor("st", (DEPTH, 2, P, DM), F32, kind="ExternalOutput").ap()
    x_mid = nc.dram_tensor("x_mid", (P, KC, TOK), F32, kind="Internal").ap()
    build(nc, **aps, yT=yT, st_out=st, x_mid=x_mid)
    r = run_bass_kernel_spmd(nc, [{f"in_{k}": v for k, v in ins.items()}], core_ids=[0])
    y = np.asarray(r.results[0]["yT"]).transpose(1, 0, 2).reshape(DM, TOK).T
    new = np.asarray(r.results[0]["st"]).transpose(0, 1, 3, 2).reshape(1, DEPTH, 2, NH, HD, P)
    return (np.ascontiguousarray(y[None, :CTX]), np.ascontiguousarray(y[None, CTX:]), np.ascontiguousarray(new))
```

```python
from contextlib import ExitStack

import concourse.bass as bass
from concourse import mybir

P = 128
DEPTH, DM = 2, 1024
KC = DM // P
CTX, LAT = 128, 512
TOK = CTX + LAT
HALF = TOK // 2
GW, GH = 64, LAT // 64
NCH = TOK // P
NH, HD, NG = 16, 64, 4
HPG = NH // NG
GC = HPG * HD
TAPS = 5
PAD = TAPS // 2
CW = CTX + PAD + LAT
LAT0 = CTX + PAD
RAW = CW + 2 * PAD
PITCH = (RAW + 7) // 8 * 8
NCONV = 16
EPS = 1e-6

N_TILES = 1 + NCONV + 8 + 16 + 8 + 32 + 8
T_CONV, T_V, T_UZ, T_ZM, T_S5, T_OUT = 1, 17, 25, 41, 49, 81

F32 = mybir.dt.float32
F32R = mybir.dt.float32r
ALU = mybir.AluOpType
ACT = mybir.ActivationFunctionType
AXX = mybir.AxisListType.X

A_UNITS = [(c, g) for g in range(NG) for c in range(NCH)]
B_UNITS = [(c, g) for c in range(NCH) for g in range(NG)]
NU = len(A_UNITS)
A_STEPS = (2, 5, 8)
B_STEPS = [8 + 40 * b // 7 for b in range(NU + 2)]
JOBS_FIRST = [(0, q, h) for q in (1, 0) for h in (0, 1)]
NF = len(JOBS_FIRST)
JOBS_LATER = [(0, 2, 0), (0, 2, 1)] + [(1, q, h) for q in range(3) for h in (0, 1)]


def order_uz():
    out = [((8 * (n + 1), 1), ("tile", n)) for n in range(16)]
    out += [((at, 0), ("burst", b)) for b, at in enumerate(B_STEPS)]
    return [x for _, x in sorted(out)]


class Chain:

    def __init__(self, eng, sem):
        self.eng, self.sem, self.n = eng, sem, 0

    def mark(self, ins):
        ins.then_inc(self.sem, 1)
        self.n += 1
        return self.n

    def wait(self, n=None):
        self.eng.wait_ge(self.sem, self.n if n is None else n)

    def link(self, ins):
        self.mark(ins)
        self.wait()


def build(nc, xT, wts, wada, cT, bada, normw, finalw, ssmw, convw, dtb, alog, dskip, lnw, lnb,
          wsp, bsp, h0, yT, st_out, x_mid):
    ctx = ExitStack()
    pos = [1152]

    def region(nbytes):
        at = pos[0]
        pos[0] += (nbytes + 31) // 32 * 32
        assert pos[0] <= nc.sbuf_usable_end, pos[0]
        return at

    def place(name, shape, at, dt=F32):
        return nc.alloc_sbuf_tensor_at(name, shape, dt, offset=at)

    def new(name, shape, dt=F32):
        n = 4
        for s in shape[1:]:
            n *= s
        return place(name, shape, region(n), dt)

    ACTB = KC * TOK * 4
    h_hi = new("h_hi", [P, KC, TOK], F32R)
    h_lo = new("h_lo", [P, KC, TOK], F32R)
    w_st = new("w_st", [P, 2, KC * P])
    w_hi = new("w_hi", [P, 2, KC * P], F32R)
    w_lo = new("w_lo", [P, 2, KC * P], F32R)
    r_v = region(ACTB)
    v_tok = place("v_tok", [P, NCH, DM], r_v)
    mg = place("mg", [P, KC, TOK], r_v)
    r_uz = region(ACTB)
    uz = place("uz", [P, KC, TOK], r_uz)
    yg_lo = place("yg_lo", [P, KC, TOK], r_uz, F32R)
    r_r = region(ACTB)
    yg_hi = place("yg_hi", [P, KC, TOK], r_r, F32R)
    bsp_row = place("bsp_row", [1, DM], r_r + 15360)
    r_x = region(ACTB)
    x_tok = place("x_tok", [P, NCH, DM], r_x)
    xr = place("xr", [P, KC, TOK], r_x)
    r_bc = region(8 * CW * 4)
    bc = place("bc", [P, 8, CW], r_bc)
    ym_lo = place("ym_lo", [P, KC, TOK], r_bc, F32R)
    r_t = region(ACTB)
    ym_hi = place("ym_hi", [P, KC, TOK], r_t, F32R)
    raw = place("raw", [P, 2, PITCH], r_t)
    cv = place("cv", [P, 2, PITCH], r_t + 8 * PITCH)
    cvt = place("cvt", [P, PITCH], r_t + 16 * PITCH)
    xo = place("xo", [P, 2, PITCH], r_t + 20 * PITCH)
    dmat = place("dmat", [P, 2, HPG, P], r_t)
    mmat = place("mmat", [P, 2, 2, HPG, P], r_t + 4096)
    xfb = place("xfb", [P, 2, 2, HPG, HD], r_t + 12288)
    gm = place("gm", [P, 2, 2, P], r_t + 16384)
    yab = place("yab", [P, 2, HPG, HD], r_t + 18432)
    scan_tmp = place("scan_tmp", [P, DM], r_t + 8192)
    r_wp = region(8 * DM)
    wsp_sb = place("wsp_sb", [P, 8, P], r_wp)
    lnb_sb = place("lnb_sb", [P, DM], r_wp + 4 * DM)
    pbb = place("pbb", [P, 8, P], r_wp + 4 * DM)
    ada_st = place("ada_st", [P, 2, 2, 512], r_wp)
    ada_pre = place("ada_pre", [P, 4 * NF - 1, 2, 512], r_v)
    r_c = region(5 * TOK * 4)
    c_buf = [place(f"c_buf{i}", [P, TOK], r_c + i * TOK * 4) for i in range(5)]
    xw = place("xw", [P, 2, 2, HPG, HD], r_c + 2 * TOK * 4)
    bt = place("bt", [P, 2, P], r_c + 2 * TOK * 4 + 4096)
    ctx_st = place("ctx_st", [P, 2 * GC], r_c + 4 * TOK * 4)
    dta = place("dta", [64, TOK], r_c + 4 * TOK * 4)
    adup = place("adup", [P, NCH, 4, NH], r_c + 3 * TOK * 4)
    cum_r = place("cum_r", [64, TOK], r_c, F32R)
    r_a0, r_a1 = region(4096), region(4096)
    ada_row = place("ada_row", [2, 2, 512], r_a0)
    ada_acc = [place(f"ada_acc{i}", [P, 2, 512], at) for i, at in enumerate((r_a0, r_a1))]
    st_at = [r_r + i * 4096 for i in range(5)] + [r_wp, r_wp + 4096, r_a0]
    states = [place(f"states{i}", [P, DM], at) for i, at in enumerate(st_at)]
    tm = place("tm", [P, NCH, 64], r_a1)
    ex = place("ex", [P, 6, NCH, NH], r_a1 + 1280)
    ncf = place("ncf", [P, NCH, NH], r_a1 + 3200)
    ebs = place("ebs", [P, NCH, NH], r_a1 + 3520)
    r_cum = region(TOK * 4)
    cum_t = place("cum_t", [64, TOK], r_cum, F32R)
    ssq = place("ssq", [P, TOK], r_cum)
    tri = new("tri", [P, 2, P])
    maskb = new("maskb", [P, P])
    ident = new("ident", [P, P])
    ones = new("ones", [P, P])
    sel32 = new("sel32", [64, 32])
    sel = new("sel", [64, 32], F32R)
    dupm = new("dupm", [64, NH])
    m64 = new("m64", [64, 1])
    c_sb = new("c_sb", [P, KC, 2])
    sc = new("sc", [P, 2, KC, 2])
    mods = new("mods", [P, DEPTH * 3, 2, KC])
    amul = new("amul", [P, DEPTH, 2, KC])
    bada_sb = new("bada_sb", [P, DEPTH * 3, KC])
    normw_sb = new("normw_sb", [P, DEPTH, KC])
    finalw_sb = new("finalw_sb", [P, KC])
    ssmw_sb = new("ssmw_sb", [P, DEPTH, KC])
    convw_sb = new("convw_sb", [P, DEPTH, NCONV, TAPS + 1])
    dtb_sb = new("dtb_sb", [32, DEPTH])
    ea = new("ea", [32, DEPTH])
    dskip_sb = new("dskip_sb", [P, DEPTH, NH])
    lnw_sb = new("lnw_sb", [P, DEPTH, KC])
    bst = new("bst", [P, NCH, 12])
    mv = new("mv", [P, NCH, 2])
    rv = new("rv", [P, NCH, 1])
    rst = new("rst", [P, 2, NCH])
    eps_sb = new("eps_sb", [P, 1])

    acc = [ctx.enter_context(nc.psum_tensor(f"acc{i}", [P, 2, 512], F32)) for i in range(2)]
    X = [ctx.enter_context(nc.psum_tensor(f"X{i}", [P, 512], F32)) for i in range(4)]

    def sem(name):
        return ctx.enter_context(nc.semaphore(name))

    w_landed = [sem("w_landed0"), sem("w_landed1")]
    w_split, tile_done, w_go = sem("w_split"), sem("tile_done"), sem("w_go")
    acc_free = [sem("acc_free0"), sem("acc_free1")]
    consts_in, consts_made, x_in = sem("consts_in"), sem("consts_made"), sem("x_in")
    x_stored, out_done, wsp_in = sem("x_stored"), sem("out_done"), sem("wsp_in")
    st_in, st_stored = sem("st_in"), sem("st_stored")
    ada_in = [sem("ada_in0"), sem("ada_in1")]
    ada_used, ada_mm = sem("ada_used"), sem("ada_mm")
    pre_in = [sem(f"pre_in{i}") for i in range(2 * NF)]
    row_mm, row_out, job_read = sem("row_mm"), sem("row_out"), sem("job_read")
    c_in, ct_ready, sc_ready = sem("c_in"), sem("ct_ready"), sem("sc_ready")
    sq_ready, sq_used, ssq_ready, stat_ready = sem("sq_ready"), sem("sq_used"), sem("ssq_ready"), sem("stat_ready")
    root_ready, rstd_ready, rbc_ready = sem("root_ready"), sem("rstd_ready"), sem("rbc_ready")
    hpre_ready, hhi_ready, h_ready = sem("hpre_ready"), sem("hhi_ready"), sem("h_ready")
    dte_arg, dte_ready = sem("dte_arg"), sem("dte_ready")
    dtu_ready, dtl_ready, dta_ready = sem("dtu_ready"), sem("dtl_ready"), sem("dta_ready")
    tmT_ready, tm_ready, cum_mm, adup_ready = sem("tmT_ready"), sem("tm_ready"), sem("cum_mm"), sem("adup_ready")
    cumT_mm, cum_ready, ex_arg, ex_ready = sem("cumT_mm"), sem("cum_ready"), sem("ex_arg"), sem("ex_ready")
    pads_ready, cv_ready, cvt_ready, conv_done = sem("pads_ready"), sem("cv_ready"), sem("cvt_ready"), sem("conv_done")
    tp_ready, tp_out, ln_ready = sem("tp_ready"), sem("tp_out"), sem("ln_ready")
    bt_mm, bt_ready, xw_ready, s_mm, s_out = sem("bt_mm"), sem("bt_ready"), sem("xw_ready"), sem("s_mm"), sem("s_out")
    scan_done, vvar, vroot = sem("scan_done"), sem("vvar"), sem("vroot")
    fbg_ready, t_ready, d_ready, e_ready = sem("fbg_ready"), sem("t_ready"), sem("d_ready"), sem("e_ready")
    m_ready, y_out, y_ready = sem("m_ready"), sem("y_out"), sem("y_ready")
    zt_ready = sem("zt_ready")
    pbb_mm, pbb_ready, sp_mm, sp_used = sem("pbb_mm"), sem("pbb_ready"), sem("sp_mm"), sem("sp_used")
    ya_ready, yghi_ready, yg_ready = sem("ya_ready"), sem("yghi_ready"), sem("yg_ready")
    yT_mm, y2_ready, ymhi_ready, ym_ready = sem("yT_mm"), sem("y2_ready"), sem("ymhi_ready"), sem("ym_ready")
    ry_ready, gt_ready, mg_ready, mhi_ready, mh_ready = sem("ry_ready"), sem("gt_ready"), sem("mg_ready"), sem("mhi_ready"), sem("mh_ready")
    fin_ready = sem("fin_ready")
    s_act, s_dve, s_pool = sem("s_act"), sem("s_dve"), sem("s_pool")

    def ada_first(n):
        return ada_pre[:, n, :, :] if n < 4 * NF - 1 else ada_st[:, 0, :, :]

    def acc_of(t):
        return acc[t % 2]

    def f(ap):
        return ap.bitcast(F32)

    def chunk_off(c):
        return 0 if c == 0 else LAT0 + P * (c - 1)

    def xcols(pair, c):
        return pair[1][:, 0:P] if c == 0 else pair[0][:, P * (c - 1):P * c]

    def evacuated(eng, t):
        eng.wait_ge(acc_free[t % 2], t // 2 + 1)

    def halves(buf):
        return buf[:, 0:TOK].rearrange("p (b n) -> p b n", b=2)

    block = ctx.enter_context(nc.Block())

    @block.sync
    def _(sp):
        def weight(t, slot):
            sp.dma_start(w_st[:, slot, :], wts[t, :, :]).then_inc(w_landed[slot], 16)

        def ada(n):
            if n >= 2:
                sp.wait_ge(ada_used, n - 1)
            L, q, hf = JOBS_LATER[n // 4]
            sp.dma_start(ada_st[:, n % 2, :, :], wada[L, q, hf, n % 4, :, :, :]).then_inc(ada_in[n % 2], 16)

        sp.dma_start(c_sb[:, :, :], cT).then_inc(c_in, 16)
        for n in range(4 * NF):
            L, q, hf = JOBS_FIRST[n // 4]
            sp.dma_start(ada_first(n), wada[L, q, hf, n % 4, :, :, :]).then_inc(pre_in[n // 2], 16)
            if n in (7, 9):
                weight((n - 7) // 2, (n - 7) // 2)
        for dst, src in ((bada_sb, bada), (normw_sb, normw), (finalw_sb, finalw), (ssmw_sb, ssmw),
                         (convw_sb, convw), (dtb_sb, dtb), (ea, alog), (dskip_sb, dskip), (lnw_sb, lnw)):
            dst = dst[:]
            sp.dma_start(dst, src).then_inc(consts_in, 16)

        def stream(lo, hi):
            with sp.Fori(lo // 2, hi // 2) as i:
                for slot in range(2):
                    sp.wait_ge(w_split, 2 * i + slot - 1)
                    weight(2 * i + slot, slot)

        stream(2, 50)
        for n in range(4 * len(JOBS_LATER)):
            t = 50 + n
            sp.wait_ge(w_split, t - 1)
            weight(t, t % 2)
            if n == 0:
                sp.wait_ge(sp_used, 8)
            ada(n)
        stream(82, DEPTH * N_TILES)
        for k in range(KC):
            sp.wait_ge(fin_ready, k + 1)
            sp.dma_start(yT[:, k, :], xr[:, k, :]).then_inc(out_done, 16)
        sp.wait_ge(out_done, 16 * KC)
        sp.wait_ge(st_stored, 32 * NG * DEPTH)
        sp.wait_ge(x_stored, 16)

    @block.gpsimd
    def _(pool):
        own = Chain(pool, s_pool)
        nc.gpsimd.memset(tri[:, :, :], 1.0)
        nc.gpsimd.memset(maskb[:, :], 1.0)
        nc.gpsimd.memset(ident[:, :], 0.0)
        nc.gpsimd.memset(ones[:, :], 1.0)
        nc.gpsimd.memset(sel32[:, :], 0.0)
        nc.gpsimd.memset(eps_sb[:, :], EPS)
        own.link(nc.gpsimd.memset(dupm[:, :], 0.0))
        for d in range(2):
            nc.gpsimd.affine_select(out=tri[:, d, :], in_=tri[:, d, :], compare_op=ALU.is_ge, fill=0.0,
                                    base=-d, pattern=[[1, P]], channel_multiplier=-1)
        nc.gpsimd.affine_select(out=maskb[:, :], in_=maskb[:, :], compare_op=ALU.is_ge, fill=0.0,
                                base=0, pattern=[[-1, P]], channel_multiplier=1)
        nc.gpsimd.affine_select(out=ident[:, :], in_=ident[:, :], compare_op=ALU.not_equal, fill=1.0,
                                base=0, pattern=[[-1, P]], channel_multiplier=1)
        for d, sign in ((0, 1.0), (1, -1.0)):
            for part in range(2):
                cols = sel32[:, NH * d:NH * (d + 1)]
                own.link(nc.gpsimd.affine_select(out=cols, in_=cols, compare_op=ALU.not_equal, fill=sign,
                                                 base=-(32 * d + 16 * part), pattern=[[-1, NH]],
                                                 channel_multiplier=1))
            own.link(nc.gpsimd.affine_select(out=dupm[:, :], in_=dupm[:, :], compare_op=ALU.not_equal, fill=-1.0,
                                             base=-(32 * d + 16), pattern=[[-1, NH]], channel_multiplier=1))
        nc.gpsimd.tensor_copy(sel[:, :], sel32[:, :]).then_inc(consts_made, 1)

        def split(slot, landed, done):
            pool.wait_ge(w_landed[slot], landed)
            if done is not None:
                pool.wait_ge(tile_done, done)
                pool.sem_inc(w_go, 1)
            nc.gpsimd.tensor_copy(w_hi[:, slot, :], w_st[:, slot, :]).then_inc(s_pool, 1)

        def split_lo(slot, n):
            pool.wait_ge(s_pool, n)
            nc.gpsimd.tensor_tensor(w_lo[:, slot, :], w_st[:, slot, :], f(w_hi[:, slot, :]),
                                    ALU.subtract).then_inc(w_split, 1)

        base = own.n
        for slot in range(2):
            split(slot, 16, None)
            split_lo(slot, base + slot + 1)
        with pool.Fori(1, DEPTH * N_TILES // 2) as i:
            for slot in range(2):
                split(slot, 16 * i + 16, 2 * i + slot - 1)
                split_lo(slot, 2 * i + (base + slot + 1))

    @block.tensor
    def _(pe):
        mm = nc.tensor.matmul

        def tile(t, hi, lo, ready=None, hooks=()):
            pe.wait_ge(w_split, t + 1)
            if t >= 2:
                pe.wait_ge(acc_free[t % 2], t // 2)
            a, s = acc_of(t), t % 2
            for k in range(KC):
                if ready is not None:
                    ready(k)
                cols = slice(k * P, (k + 1) * P)
                for n, (w, x) in enumerate(((w_hi, hi), (w_hi, lo), (w_lo, hi))):
                    for hf in range(2):
                        last = mm(a[:, hf, 0:HALF], w[:, s, cols], x[:, k, hf * HALF:(hf + 1) * HALF],
                                  start=(k == 0 and n == 0), stop=(k == KC - 1 and n == 2))
                if k == KC - 1:
                    last.then_inc(tile_done, 1)
                for at, hook in hooks:
                    if at == k + 1:
                        hook()

        def job_mm(n):
            pe.wait_ge(ada_used, 4 * (n - NF + 1))
            for v in range(2):
                for j in range(4):
                    last = mm(X[2][:, 4 * v + j:4 * v + j + 1], ada_acc[n % 2][:, v, P * j:P * (j + 1)],
                              ones[:, 0:1], start=True, stop=True)
            last.then_inc(ada_mm, 1)

        def first_mm(n):
            pe.wait_ge(sc_ready, 1)
            for k in range(KC):
                if k % 4 == 0:
                    pe.wait_ge(pre_in[(4 * n + k // 2) // 2], 32)
                last = mm(acc[n % 2][0:2, 0, :], sc[:, 1, k, :], ada_first(4 * n + k // 2)[:, k % 2, :],
                          start=(k == 0), stop=(k == KC - 1))
            last.then_inc(row_mm, 1)

        def first_tp(n):
            pe.wait_ge(row_out, n + 1)
            if n > 0:
                pe.wait_ge(job_read, n)
            for j in range(4):
                last = nc.tensor.transpose(X[2][:, 0:8].rearrange("p (v j) -> p j v", v=2)[:, j, :],
                                           ada_row[:, n % 2, P * j:P * (j + 1)], ident[0:2, 0:2])
            last.then_inc(ada_mm, 1)

        def stat_mm(n):
            pe.wait_ge(ssq_ready, n + 1)
            for c in range(NCH):
                last = mm(X[0][:, c:c + 1], ssq[:, P * c:P * (c + 1)], ones[:, 0:1], start=True, stop=True)
            last.then_inc(stat_ready, 1)

        def stat_bc(n):
            pe.wait_ge(rstd_ready, n + 1)
            for c in range(NCH):
                last = mm(xcols((X[0], X[1]), c), rst[:, 1, c:c + 1].broadcast_to([P, P]), ident[:, :],
                          start=True, stop=True)
            last.then_inc(rbc_ready, 1)

        def transposes(src, n):
            if n > 0:
                pe.wait_ge(tp_out, n)
            for c in range(NCH):
                last = nc.tensor.transpose(xcols((X[0], X[1]), c), src(c), ident[:, :])
            last.then_inc(tp_ready, 1)

        def dt_cums(L):
            pe.wait_ge(dta_ready, L + 1)
            for c in range(NCH):
                last = nc.tensor.transpose(X[2][:, 64 * c:64 * (c + 1)], dta[:, P * c:P * (c + 1)], ident[0:64, 0:64])
            last.then_inc(tmT_ready, 1)

        def dt_cums2(L):
            pe.wait_ge(tm_ready, L + 1)
            mm(X[3][:, 0:80], tri[:, 0, :], tm[:, :, 32:48], start=True, stop=True)
            mm(X[3][:, 80:160], tri[:, 1, :], tm[:, :, 48:64], start=True, stop=True)
            mm(X[3][:, 160:320], ones[:, :], tm[:, :, 32:64], start=True, stop=True).then_inc(cum_mm, 1)

        def dt_cums3(L):
            pe.wait_ge(adup_ready, L + 1)
            for d in range(2):
                for c in range(NCH):
                    last = mm(xcols((X[0], X[1]), c)[32 * d:32 * (d + 1), :],
                              adup[:, c, 2 * d:2 * d + 2, :].rearrange("p r h -> p (r h)"), tri[:, d, :], start=True, stop=True)
            last.then_inc(cumT_mm, 1)

        def a_burst(L, a):
            if a > 0:
                c, g = A_UNITS[a - 1]
                n = NU * L + a
                pe.wait_ge(bt_ready, n)
                pe.wait_ge(xw_ready, n)
                if n > 1:
                    pe.wait_ge(s_out, n - 1)
                s = (a - 1) % 2
                cols = slice(0, GC) if c == 1 else slice(GC, 2 * GC) if c == NCH - 1 else slice(0, 2 * GC)
                mm(X[3][:, cols], bt[:, s, :], xw[:, s, :, :, :].rearrange("p d h w -> p (d h w)")[:, cols],
                   start=True, stop=True).then_inc(s_mm, 1)
            if a < NU:
                c, g = A_UNITS[a]
                if c == 0:
                    pe.wait_ge(tp_out, 16 * L + 2 * (g + 1))
                off = chunk_off(c)
                nc.tensor.transpose(X[2][:, 0:P], bc[:, g, off:off + P], ident[:, :]).then_inc(bt_mm, 1)

        def b_burst(L, b):
            base = NU * L
            if b >= 2:
                u = b - 2
                c, g = B_UNITS[u]
                s = u % 2
                pe.wait_ge(m_ready, base + u + 1)
                if u > 0:
                    pe.wait_ge(y_out, base + u)
                if u == HPG:
                    pe.wait_ge(scan_done, L + 1)
                off = chunk_off(c)
                for h in range(HPG):
                    y = X[3][:, h * HD:(h + 1) * HD]
                    mm(y, mmat[:, s, 0, h, :], xfb[:, s, 0, h, :], start=True, stop=False)
                    last = mm(y, mmat[:, s, 1, h, :], xfb[:, s, 1, h, :], start=False, stop=True)
                if c > 0:
                    cg = bc[:, 4 + g, off:off + P]
                    cols = slice(g * GC, (g + 1) * GC)
                    mm(X[2][:, P:P + GC], cg, states[2 * (c - 1)][:, cols], start=True, stop=True)
                    last = mm(X[3][:, GC:2 * GC], cg, states[2 * (c - 1) + 1][:, cols], start=True, stop=True)
                if b >= NU:
                    last.then_inc(fbg_ready, 1)
            if b < NU:
                c, g = B_UNITS[b]
                off = chunk_off(c)
                if b == 0:
                    pe.wait_ge(tp_out, 16 * (L + 1))
                    pe.wait_ge(s_out, NU * (L + 1))
                else:
                    pe.wait_ge(d_ready, base + b)
                for d in range(2):
                    for h in range(HPG):
                        j = NH * d + HPG * g + h
                        mm(X[d][:, P * h:P * (h + 1)], sel[:, j:j + 1].broadcast_to([64, P]),
                           cum_t[:, P * c:P * (c + 1)], start=True, stop=True)
                mm(X[2][:, 0:P], bc[:, g, off:off + P], bc[:, 4 + g, off:off + P],
                   start=True, stop=True).then_inc(fbg_ready, 1)

        def pbb_products(L):
            pe.wait_ge(wsp_in, 48 * (L + 1))
            pe.wait_ge(y_ready, NU * (L + 1))
            for g in range(8):
                o = X[2 + g // 4][:, P * (g % 4):P * (g % 4 + 1)]
                mm(o, lnb_sb[:, P * g:P * (g + 1)], wsp_sb[:, g, :], start=True, stop=False)
                last = mm(o, ones[0:1, :], bsp_row[0:1, P * g:P * (g + 1)], start=False, stop=True)
            last.then_inc(pbb_mm, 1)

        def spatial(L, g):
            if g == 0:
                pe.wait_ge(ln_ready, NCH * (L + 1))
                pe.wait_ge(pbb_ready, 2 * (L + 1))
            else:
                pe.wait_ge(sp_used, 8 * L + g)
            for c in range(NCH):
                last = mm(xcols((X[2], X[3]), c), v_tok[:, c, P * g:P * (g + 1)], wsp_sb[:, g, :],
                          start=True, stop=True)
            last.then_inc(sp_mm, 1)

        def y_transposes(L, j):
            if j == 0:
                pe.wait_ge(y_ready, NU * (L + 1))
            else:
                pe.wait_ge(y2_ready, 8 * L + j)
            for c in range(NCH):
                last = nc.tensor.transpose(xcols((X[0], X[1]), c), x_tok[:, c, P * j:P * (j + 1)], ident[:, :])
            last.then_inc(yT_mm, 1)

        pe.wait_ge(consts_made, 1)
        first_mm(0)
        first_mm(1)
        first_tp(0)
        stat_mm(0)
        pe.wait_ge(row_out, 1)
        first_mm(2)
        first_tp(1)
        stat_bc(0)
        pe.wait_ge(row_out, 2)
        first_mm(3)
        first_tp(2)
        first_tp(3)
        for L in range(DEPTH):
            T0 = L * N_TILES
            if L > 0:
                stat_mm(2 * L)
                stat_bc(2 * L)
            h = (h_hi, h_lo)
            tile(T0, *h, ready=lambda k: pe.wait_ge(h_ready, 8 * L + k + 1))
            def x_transposes(j):
                pe.wait_ge(conv_done, NCONV * L + 9 + j)
                if j == 0:
                    pe.wait_ge(cum_ready, L + 1)
                transposes(lambda c: xo[:, j % 2, chunk_off(c):chunk_off(c) + P], 16 * L + j)

            def v_transposes(j):
                evacuated(pe, T0 + T_V + j)
                transposes(lambda c: c_buf[j % 2][:, P * c:P * (c + 1)], 16 * L + 8 + j)

            for i in range(NCONV):
                tile(T0 + T_CONV + i, *h, hooks=[(2, lambda: x_transposes(i - 11))] if i >= 11 else [])
                if i == 2:
                    dt_cums(L)
                if i == 4:
                    dt_cums2(L)
                if i == 5:
                    dt_cums3(L)
            for i in range(8):
                def bursts(n):
                    return lambda: a_burst(L, n)
                hooks = [(s, bursts(3 * i + n)) for n, s in enumerate(A_STEPS) if 3 * i + n <= NU]
                if i < 2:
                    hooks.append((1, lambda: x_transposes(5 + 2 * i)))
                hooks.append((6, (lambda: v_transposes(i - 1)) if i >= 1 else (lambda: x_transposes(6))))
                tile(T0 + T_V + i, *h, hooks=hooks)
            for n in range(16):
                hooks = []
                for b, at in enumerate(B_STEPS):
                    if 8 * n < at <= 8 * (n + 1):
                        hooks.append((at - 8 * n, (lambda b=b: b_burst(L, b))))
                if n == 0:
                    hooks.append((6, lambda: v_transposes(7)))
                tile(T0 + T_UZ + n, *h, hooks=hooks)
            for j in range(8):
                hooks = [(5, lambda: pbb_products(L))] if j == 0 else []
                tile(T0 + T_ZM + j, *h, hooks=hooks)
                y_transposes(L, j)
                spatial(L, j)
            for j in range(8):
                t = T0 + T_S5 + 4 * j
                job = 4 + j
                tile(t, *h)
                if j == 0:
                    stat_mm(2 * L + 1)
                tile(t + 1, yg_hi, yg_lo,
                     ready=(lambda k: pe.wait_ge(yg_ready, 8 * L + k + 1)) if j == 0 else None)
                if j == 0:
                    stat_bc(2 * L + 1)
                tile(t + 2, *h)
                if L == 0 and j > 0:
                    job_mm(job - 1)
                tile(t + 3, ym_hi, ym_lo,
                     ready=(lambda k: pe.wait_ge(ym_ready, 8 * L + k + 1)) if j == 0 else None)
            for j in range(8):
                tile(T0 + T_OUT + j, *h,
                     ready=(lambda k: pe.wait_ge(mh_ready, 8 * L + k + 1)) if j == 0 else None)
                if L == 0 and j == 0:
                    job_mm(11)
        stat_mm(2 * DEPTH)
        stat_bc(2 * DEPTH)

    @block.scalar
    def _(act):
        own = Chain(act, s_act)
        A = nc.scalar.activation

        def free(t, ins):
            ins.then_inc(acc_free[t % 2], 1)

        def pieces(a, dst_ctx, dst_lat, L, parts=P):
            n0 = (HALF - CTX) // GW
            if L % 2 == 0:
                lat = dst_lat.rearrange("p (r w) -> p r w", w=GW)
            else:
                lat = dst_lat.rearrange("p (w r) -> p r w", r=GH)
            return [(dst_ctx, a[0:parts, 0, 0:CTX]),
                    (lat[:, 0:n0, :], a[0:parts, 0, CTX:HALF].rearrange("p (r w) -> p r w", w=GW)),
                    (lat[:, n0:GH, :], a[0:parts, 1, 0:HALF].rearrange("p (r w) -> p r w", w=GW))]

        def root(n):
            act.wait_ge(stat_ready, n + 1)
            A(rst[:, 0, :], X[0][:, 0:NCH], ACT.Sqrt, scale=1.0 / DM, bias=eps_sb[:, 0:1]).then_inc(root_ready, 1)

        def square(n, k, src):
            if k >= 2:
                act.wait_ge(sq_used, 7 * n + k - 1)
            elif n > 0:
                act.wait_ge(ssq_ready, n)
            A(c_buf[2 + k % 2][:, :], src, ACT.Square).then_inc(sq_ready, 1)

        def tp_copy(dst, n):
            act.wait_ge(tp_ready, n + 1)
            A(dst[:, 1:NCH, :], X[0][:, :].rearrange("p (c n) -> p c n", n=P), ACT.Copy)
            A(dst[:, 0, :], X[1][:, 0:P], ACT.Copy).then_inc(tp_out, 1)

        act.dma_start(xr[:, :, :], xT).then_inc(x_in, 16)
        act.wait_ge(c_in, 16)
        A(sc[:, 0, :, :], c_sb[:, :, :], ACT.Tanh, scale=0.5).then_inc(ct_ready, 1)
        act.wait_ge(x_in, 16)
        for k in range(KC):
            square(0, k, xr[:, k, :])

        def row_copy(n):
            act.wait_ge(row_mm, n + 1)
            if n >= 2:
                act.wait_ge(ada_mm, n - 1)
            A(ada_row[:, n % 2, :], acc[n % 2][0:2, 0, :], ACT.Copy).then_inc(row_out, 1)

        row_copy(0)
        row_copy(1)
        root(0)
        row_copy(2)
        row_copy(3)
        act.wait_ge(consts_in, 16 * 9)
        own.link(A(ea[:, :], ea[:, :], ACT.Exp))
        act.wait_ge(job_read, NF)

        for L in range(DEPTH):
            T0 = L * N_TILES

            if L > 0:
                root(2 * L)
            for k in range(KC):
                act.wait_ge(hpre_ready, 8 * L + k + 1)
                for v, cols in ((0, slice(0, CTX)), (1, slice(CTX, TOK))):
                    last = A(h_hi[:, k, cols], c_buf[k % 4][:, cols], ACT.Identity, bias=mods[:, 3 * L, v, k:k + 1])
                last.then_inc(hhi_ready, 1)

            act.wait_ge(tile_done, T0 + 1)
            for dst, src in pieces(acc_of(T0), c_buf[0][0:32, 0:CTX], c_buf[0][0:32, CTX:TOK], L, 32):
                last = A(dst, src, ACT.Identity, bias=dtb_sb[:, L:L + 1])
            free(T0, last)

            def x_copy(j):
                tp_copy(x_tok[:, :, P * j:P * (j + 1)], 16 * L + j)

            def v_copy(j):
                tp_copy(v_tok[:, :, P * j:P * (j + 1)], 16 * L + 8 + j)

            for i in range(NCONV + 1):
                if 11 <= i < NCONV:
                    if L > 0 and i == 11:
                        act.wait_ge(x_stored, 16)
                    x_copy(i - 11)
                if i < NCONV:
                    t = T0 + T_CONV + i
                    act.wait_ge(tile_done, t + 1)
                    if i >= 2:
                        act.wait_ge(cv_ready, NCONV * L + i - 1)
                    else:
                        act.wait_ge(pads_ready, L + 1)
                    r = raw[:, i % 2, :]
                    for dst, src in pieces(acc_of(t), r[:, PAD:PAD + CTX], r[:, PAD + LAT0:PAD + LAT0 + LAT], L):
                        last = A(dst, src, ACT.Copy)
                    free(t, last)
                if i == 0:
                    act.wait_ge(dte_arg, L + 1)
                    A(c_buf[1][0:32, :], c_buf[1][0:32, :], ACT.Exp, scale=-1.0).then_inc(dte_ready, 1)
                    act.wait_ge(dtu_ready, L + 1)
                    A(c_buf[3][0:32, :], c_buf[2][0:32, :], ACT.Ln).then_inc(dtl_ready, 1)
                if i == 3:
                    act.wait_ge(tmT_ready, L + 1)
                    A(tm[:, :, :], X[2][:, 0:NCH * 64].rearrange("p (c r) -> p c r", r=64), ACT.Copy)\
                        .then_inc(tm_ready, 1)
                if i == 7:
                    act.wait_ge(ex_arg, L + 1)
                    A(ex[:, :, :, :], ex[:, :, :, :], ACT.Exp).then_inc(ex_ready, 1)
                if i >= 1:
                    n = NCONV * L + i - 1
                    act.wait_ge(cv_ready, n + 1)
                    if n > 0:
                        act.wait_ge(conv_done, n)
                    A(cvt[:, 0:CW], cv[:, (i - 1) % 2, 0:CW], ACT.Tanh).then_inc(cvt_ready, 1)

            def a_copies(a):
                if a > 0:
                    c, g = A_UNITS[a - 1]
                    n = NU * L + a
                    act.wait_ge(s_mm, n)
                    cols = slice(g * GC, (g + 1) * GC)
                    if c == 0:
                        if g > 0 or L > 0:
                            act.wait_ge(st_stored, 32 * (NG * L + g))
                        A(ctx_st[:, :], X[3][:, :], ACT.Copy).then_inc(s_out, 1)
                        act.wait_ge(s_out, n)
                        for d in range(2):
                            act.dma_start(st_out[L, d, :, cols], ctx_st[:, d * GC:(d + 1) * GC])\
                                .then_inc(st_stored, 16)
                    else:
                        if c < NCH - 1:
                            last = A(states[2 * c][:, cols], X[3][:, 0:GC], ACT.Copy)
                        if c > 1:
                            last = A(states[2 * (c - 2) + 1][:, cols], X[3][:, GC:2 * GC], ACT.Copy)
                        last.then_inc(s_out, 1)
                if a < NU:
                    n = NU * L + a
                    act.wait_ge(bt_mm, n + 1)
                    if a >= 2:
                        act.wait_ge(s_mm, n - 1)
                    A(bt[:, a % 2, :], X[2][:, 0:P], ACT.Copy).then_inc(bt_ready, 1)

            act.dma_start(states[0][:, :], h0[L, 0, :, :]).then_inc(st_in, 16)
            act.dma_start(states[2 * (NCH - 2) + 1][:, :], h0[L, 1, :, :]).then_inc(st_in, 16)
            for i in range(8):
                t = T0 + T_V + i
                if i < 2:
                    x_copy(5 + 2 * i)
                for n in range(3):
                    if n == 2:
                        v_copy(i - 1) if i >= 1 else x_copy(6)
                    if 3 * i + n <= NU:
                        a_copies(3 * i + n)
                act.wait_ge(tile_done, t + 1)
                if i >= 2:
                    act.wait_ge(tp_ready, 16 * L + 8 + i - 1)
                free(t, A(halves(c_buf[i % 2]), acc_of(t)[:, :, 0:HALF], ACT.Gelu_apprx_tanh))

            v_copy(7)
            for what, n in order_uz():
                if what == "burst":
                    if 1 <= n <= NU:
                        act.wait_ge(d_ready, NU * L + n)
                        d = dmat[:, (n - 1) % 2, :, :]
                        A(d, d, ACT.Exp).then_inc(e_ready, 1)
                    if n < NU:
                        c, g = B_UNITS[n]
                        act.wait_ge(fbg_ready, (NU + 2) * L + n + 1)
                        if n >= 2:
                            act.wait_ge(m_ready, NU * L + n - 1)
                        for h in range(HPG):
                            j = HPG * g + h
                            last = A(dmat[:, n % 2, h, :], X[0][:, P * h:P * (h + 1)], ACT.Identity,
                                     bias=ncf[:, c, j:j + 1])
                        last.then_inc(t_ready, 1)
                    if n == NCH + 2:
                        act.wait_ge(vvar, L + 1)
                        A(rv[:, :, :], mv[:, :, 1:2], ACT.Sqrt, bias=eps_sb[:, 0:1]).then_inc(vroot, 1)
                    continue
                t = T0 + T_UZ + n
                act.wait_ge(tile_done, t + 1)
                if n % 2 == 0:
                    free(t, A(halves(uz[:, n // 2, :]), acc_of(t)[:, :, 0:HALF], ACT.Gelu_apprx_tanh))
                else:
                    if n > 1:
                        evacuated(act, t - 2)
                    A(halves(c_buf[0]), acc_of(t)[:, :, 0:HALF], ACT.Tanh, scale=0.5).then_inc(zt_ready, 1)

            act.wait_ge(y_ready, NU * (L + 1))
            act.dma_start(wsp_sb[:, :, :], wsp[L, :, :, :]).then_inc(wsp_in, 16)
            act.dma_start(lnb_sb[:, :], lnb[L:L + 1, :].partition_broadcast(P)).then_inc(wsp_in, 16)
            act.dma_start(bsp_row[:, :], bsp[L:L + 1, :]).then_inc(wsp_in, 16)
            for j in range(8):
                t = T0 + T_ZM + j
                if j == 0:
                    act.wait_ge(pbb_mm, L + 1)
                    for i in range(2):
                        A(pbb[:, 4 * i:4 * i + 4, :], X[2 + i][:, :].rearrange("p (g n) -> p g n", n=P), ACT.Copy)\
                            .then_inc(pbb_ready, 1)
                act.wait_ge(tile_done, t + 1)
                if j > 0:
                    evacuated(act, t - 1)
                else:
                    evacuated(act, T0 + T_UZ + 15)
                A(halves(c_buf[0]), acc_of(t)[:, :, 0:HALF], ACT.Tanh, scale=0.5).then_inc(zt_ready, 1)
                act.wait_ge(y2_ready, 8 * L + j + 1)
                square(2 * L + 1, j, c_buf[1][:, :])
                A(ym_hi[:, j, :], c_buf[1][:, :], ACT.Copy, scale=ssmw_sb[:, L, j:j + 1]).then_inc(ymhi_ready, 1)
                act.wait_ge(ya_ready, 8 * L + j + 1)
                A(yg_hi[:, j, :], c_buf[4][:, :], ACT.Copy).then_inc(yghi_ready, 1)

            act.dma_start(xr[:, :, :], xT if L == 0 else x_mid).then_inc(x_in, 16)
            for j in range(8):
                t = T0 + T_S5 + 4 * j
                for b, tt in ((0, t), (1, t + 2)):
                    act.wait_ge(tile_done, tt + 1)
                    if j > 0:
                        evacuated(act, t - 3 + 2 * b)
                    free(tt, A(halves(c_buf[b]), acc_of(tt)[:, :, 0:HALF], ACT.Tanh, scale=0.5))
                    if j == 0 and b == 0:
                        root(2 * L + 1)
                        act.wait_ge(rbc_ready, 2 * L + 2)
                        A(c_buf[2][:, CTX:TOK], X[0][:, :], ACT.Copy, scale=0.5)
                        A(c_buf[2][:, 0:CTX], X[1][:, 0:P], ACT.Copy, scale=0.5).then_inc(ry_ready, 1)
            for k in range(KC):
                act.wait_ge(mg_ready, 8 * L + k + 1)
                A(h_hi[:, k, :], mg[:, k, :], ACT.Copy).then_inc(mhi_ready, 1)
            for j in range(8):
                evacuated(act, T0 + T_OUT + j)
                square(2 * L + 2, j, xr[:, j, :])
            if L < DEPTH - 1:
                act.dma_start(x_mid, xr[:, :, :]).then_inc(x_stored, 16)
        root(2 * DEPTH)

    @block.vector
    def _(dve):
        own = Chain(dve, s_dve)
        TT, STT, TS = nc.vector.tensor_tensor, nc.vector.scalar_tensor_tensor, nc.vector.tensor_scalar

        def free(t, ins):
            ins.then_inc(acc_free[t % 2], 1)

        def per_head(ap, w):
            return ap.unsqueeze(2).broadcast_to([P, ap.shape[1], w])

        def ada(n):
            job, part = n // 4, n % 4
            dve.wait_ge(ada_in[n % 2], 16 * (n // 2 + 1))
            if part == 0 and job >= 2:
                dve.wait_ge(ada_mm, NF + job - 1)
            if part > 0:
                dve.wait_ge(ada_used, n)
            for kk in range(2):
                k = 2 * part + kk
                for v in range(2):
                    o, w, s = ada_acc[job % 2][:, v, :], ada_st[:, n % 2, kk, :], sc[:, 1, k, v:v + 1]
                    ins = TS(o, w, s, None, ALU.mult) if k == 0 else \
                        STT(out=o, in0=w, scalar=s, in1=o, op0=ALU.mult, op1=ALU.add)
                    if kk == 1 and v == 1:
                        ins.then_inc(ada_used, 1)
                    else:
                        own.mark(ins)
                if kk == 0:
                    own.wait()

        def job_out(n):
            L, q, hf = (JOBS_FIRST + JOBS_LATER)[n]
            dve.wait_ge(ada_mm, n + 1)
            cols = slice(4 * hf, 4 * hf + 4)
            TT(mods[:, 3 * L + q, :, cols], X[2][:, 0:8].rearrange("p (v j) -> p v j", v=2),
               bada_sb[:, 3 * L + q, cols].unsqueeze(1).broadcast_to([P, 2, 4]), ALU.add).then_inc(job_read, 1)
            dve.wait_ge(job_read, n + 1)
            if q == 1 and hf == 1:
                own.link(STT(out=amul[:, L, :, :], in0=mods[:, 3 * L + 1, :, :], scalar=1.0,
                             in1=normw_sb[:, L, :].unsqueeze(1).broadcast_to([P, 2, KC]),
                             op0=ALU.add, op1=ALU.mult))

        def add_square(n, k):
            dve.wait_ge(sq_ready, 8 * n + k + 1)
            src = c_buf[2 + k % 2][:, :]
            ins = nc.vector.tensor_copy(ssq[:, :], src) if k == 0 else TT(ssq[:, :], ssq[:, :], src, ALU.add)
            if k < KC - 1:
                ins.then_inc(sq_used, 1)
                dve.wait_ge(sq_used, 7 * n + k + 1)
            else:
                ins.then_inc(ssq_ready, 1)

        def rstd(n):
            dve.wait_ge(root_ready, n + 1)
            nc.vector.reciprocal(rst[:, 1, :], rst[:, 0, :]).then_inc(rstd_ready, 1)

        dve.wait_ge(ct_ready, 1)
        own.link(STT(out=sc[:, 1, :, :], in0=sc[:, 0, :, :], scalar=1.0, in1=c_sb[:, :, :], op0=ALU.add, op1=ALU.mult))
        TS(sc[:, 1, :, :], sc[:, 1, :, :], 0.5, None, ALU.mult).then_inc(sc_ready, 1)
        for k in range(KC):
            add_square(0, k)
        dve.wait_ge(consts_in, 16 * 9)
        dve.wait_ge(consts_made, 1)
        own.link(nc.vector.tensor_reduce(m64[:, :], dupm[:, :], AXX, ALU.add))
        own.link(TS(convw_sb[:, :, :, :], convw_sb[:, :, :, :], 0.5, None, ALU.mult))
        job_out(0)
        rstd(0)
        job_out(1)

        for L in range(DEPTH):
            T0 = L * N_TILES

            if L > 0:
                rstd(2 * L)
            lag = 1 if L > 0 else 3
            dve.wait_ge(rbc_ready, 2 * L + 1)
            SEG = ((0, slice(0, CTX), X[1][:, 0:CTX]), (1, slice(CTX, TOK), X[0][:, 0:LAT]))
            for k in range(KC + lag):
                if k < KC:
                    if k >= 4:
                        dve.wait_ge(h_ready, 8 * L + k - 3)
                    for v, cols, r in SEG:
                        last = STT(out=c_buf[k % 4][:, cols], in0=xr[:, k, cols], scalar=amul[:, L, v, k:k + 1],
                                   in1=r, op0=ALU.mult, op1=ALU.mult)
                    last.then_inc(hpre_ready, 1)
                if L == 0 and k == lag - 1:
                    job_out(2)
                    job_out(3)
                if k >= lag:
                    kk = k - lag
                    dve.wait_ge(hhi_ready, 8 * L + kk + 1)
                    for v, cols, r in SEG:
                        last = STT(out=h_lo[:, kk, cols], in0=c_buf[kk % 4][:, cols],
                                   scalar=mods[:, 3 * L, v, kk:kk + 1], in1=f(h_hi[:, kk, cols]),
                                   op0=ALU.add, op1=ALU.subtract)
                    last.then_inc(h_ready, 1)

            dve.wait_ge(h_ready, 8 * (L + 1))
            for at in (0, PAD + CTX, RAW - PAD):
                last = nc.vector.memset(raw[:, :, at:at + PAD], 0.0)
            last.then_inc(pads_ready, 1)

            def dt_abs():
                evacuated(dve, T0)
                x = c_buf[0][0:32, :]
                STT(out=c_buf[1][0:32, :], in0=x, scalar=-1.0, in1=x, op0=ALU.mult, op1=ALU.max).then_inc(dte_arg, 1)
                dve.wait_ge(dte_ready, L + 1)
                TS(c_buf[2][0:32, :], c_buf[1][0:32, :], 1.0, None, ALU.add).then_inc(dtu_ready, 1)

            def dt_finish():
                x, e, u, lu = (b[0:32, :] for b in c_buf[0:4])
                dve.wait_ge(dtu_ready, L + 1)
                STT(out=e, in0=u, scalar=1.0, in1=e, op0=ALU.subtract, op1=ALU.subtract)
                own.link(nc.vector.reciprocal(dta[0:32, :], u))
                own.link(TT(e, e, dta[0:32, :], ALU.mult))
                dve.wait_ge(dtl_ready, L + 1)
                own.link(TT(lu, lu, e, ALU.subtract))
                own.link(STT(out=dta[0:32, :], in0=x, scalar=0.0, in1=lu, op0=ALU.max, op1=ALU.add))
                TS(dta[32:64, :], dta[0:32, :], ea[:, L:L + 1], -1.0, ALU.mult, ALU.mult).then_inc(dta_ready, 1)

            def dup_a():
                dve.wait_ge(tm_ready, L + 1)
                for r in range(4):
                    last = nc.vector.tensor_copy(adup[:, :, r, :], tm[:, :, 32 + NH * (r // 2):48 + NH * (r // 2)])
                last.then_inc(adup_ready, 1)

            def decay_args():
                dve.wait_ge(cum_mm, L + 1)
                cf = X[3][:, 0:80].rearrange("p (c h) -> p c h", h=NH)
                eb = X[3][:, 80:160].rearrange("p (c h) -> p c h", h=NH)
                tot = X[3][:, 160:320].rearrange("p (c d h) -> p d c h", d=2, h=NH)
                TS(ncf[:, :, :], cf, -1.0, None, ALU.mult)
                nc.vector.tensor_copy(ebs[:, :, :], eb)
                nc.vector.tensor_copy(ex[:, 1, :, :], eb)
                nc.vector.tensor_copy(ex[:, 2, :, :], cf)
                nc.vector.tensor_copy(ex[:, 4, :, :], tot[:, 0])
                own.link(nc.vector.tensor_copy(ex[:, 5, :, :], tot[:, 1]))
                TT(ex[:, 0, :, :], ex[:, 4, :, :], ncf[:, :, :], ALU.add)
                TT(ex[:, 3, :, :], ex[:, 5, :, :], ebs[:, :, :], ALU.subtract).then_inc(ex_arg, 1)

            def cum_rows():
                dve.wait_ge(cumT_mm, L + 1)
                lat, cx = slice(P, TOK), slice(0, P)
                nc.vector.tensor_copy(cum_r[:, lat], X[0][0:64, :])
                own.link(nc.vector.tensor_copy(cum_r[:, cx], X[1][0:64, 0:P]))
                STT(out=cum_t[:, lat], in0=f(cum_r[:, lat]), scalar=m64[:, 0:1], in1=X[0][0:64, :],
                    op0=ALU.mult, op1=ALU.add)
                STT(out=cum_t[:, cx], in0=f(cum_r[:, cx]), scalar=m64[:, 0:1], in1=X[1][0:64, 0:P],
                    op0=ALU.mult, op1=ALU.add).then_inc(cum_ready, 1)

            def state_weights():
                dve.wait_ge(ex_ready, L + 1)
                for d in range(2):
                    last = TT(ex[:, d, :, :], ex[:, d, :, :], tm[:, :, NH * d:NH * (d + 1)], ALU.mult)
                own.link(last)

            dt_abs()
            for i in range(NCONV + 1):
                if i < NCONV:
                    evacuated(dve, T0 + T_CONV + i)
                    ch = (i + 8) % NCONV
                    w = convw_sb[:, L, ch, :]
                    r, o = raw[:, i % 2, :], cv[:, i % 2, 0:CW]
                    if NCONV * L + i > 1:
                        dve.wait_ge(conv_done, NCONV * L + i - 1)
                    own.link(TS(o, r[:, PAD:PAD + CW], w[:, PAD:PAD + 1], w[:, TAPS:TAPS + 1], ALU.mult, ALU.add))
                    for tap in (0, 1, 3, 4):
                        ins = STT(out=o, in0=r[:, tap:tap + CW], scalar=w[:, tap:tap + 1], in1=o,
                                  op0=ALU.mult, op1=ALU.add)
                        if tap < 4:
                            own.link(ins)
                        else:
                            ins.then_inc(cv_ready, 1)
                if i > 0:
                    n = i - 1
                    dve.wait_ge(cvt_ready, NCONV * L + i)
                    if n < 8:
                        dst = bc[:, n, :]
                    else:
                        dst = xo[:, n % 2, 0:CW]
                        if n >= 10:
                            dve.wait_ge(tp_ready, 16 * L + n - 9)
                    STT(out=dst, in0=cvt[:, 0:CW], scalar=1.0, in1=cv[:, n % 2, 0:CW],
                        op0=ALU.add, op1=ALU.mult).then_inc(conv_done, 1)
                if i == 0:
                    dt_finish()
                if i == 4:
                    dup_a()
                if i == 5:
                    decay_args()
                if i == 6:
                    cum_rows()
                if i == 8:
                    state_weights()

            for a, (c, g) in enumerate(A_UNITS):
                n = NU * L + a
                dve.wait_ge(tp_out, 16 * L + 2 * (g + 1))
                if a >= 2:
                    dve.wait_ge(s_mm, n - 1)
                xg = x_tok[:, c, g * GC:(g + 1) * GC].rearrange("p (h w) -> p h w", w=HD)
                for d in range(2):
                    last = TT(xw[:, a % 2, d, :, :], xg, per_head(ex[:, d, c, HPG * g:HPG * (g + 1)], HD), ALU.mult)
                last.then_inc(xw_ready, 1)

            dve.wait_ge(st_in, 32 * (L + 1))
            dve.wait_ge(s_out, NU * (L + 1))
            for i in range(NCH - 2):
                for d in range(2):
                    c = 1 + i if d == 0 else NCH - 1 - i
                    frm = states[2 * (c - 1) + d]
                    to = states[2 * c] if d == 0 else states[2 * (c - 2) + 1]
                    own.link(TT(scan_tmp[:, :].rearrange("p (h w) -> p h w", w=HD),
                                frm[:, :].rearrange("p (h w) -> p h w", w=HD),
                                per_head(ex[:, 4 + d, c, :], HD), ALU.mult))
                    ins = TT(to[:, :], to[:, :], scan_tmp[:, :], ALU.add)
                    if i == NCH - 3 and d == 1:
                        ins.then_inc(scan_done, 1)
                    else:
                        own.link(ins)

            def layer_norm(b):
                if 1 <= b <= NCH:
                    c = b - 1
                    for hf in range(2):
                        ins = nc.vector.bn_stats(bst[:, c, 6 * hf:6 * hf + 6], v_tok[:, c, 512 * hf:512 * (hf + 1)])
                    own.mark(ins)
                if b == NCH + 1:
                    own.wait()
                    for c in range(NCH):
                        last = nc.vector.bn_aggr(mv[:, c, :], bst[:, c, :])
                    last.then_inc(vvar, 1)
                if b == NCH + 4:
                    dve.wait_ge(vroot, L + 1)
                    own.link(nc.vector.reciprocal(rv[:, :, :], rv[:, :, :]))
                if NCH + 5 <= b < 2 * NCH + 5:
                    c = b - NCH - 5
                    TS(v_tok[:, c, :], v_tok[:, c, :], mv[:, c, 0:1], rv[:, c, 0:1], ALU.subtract, ALU.mult)\
                        .then_inc(ln_ready, 1)

            def b_unit(b):
                if 1 <= b <= NU:
                    s = (b - 1) % 2
                    dve.wait_ge(e_ready, NU * L + b)
                    if b >= 3:
                        dve.wait_ge(fbg_ready, (NU + 2) * L + b)
                    for d in range(2):
                        last = TT(mmat[:, s, d, :, :], dmat[:, s, :, :],
                                  gm[:, s, d, :].unsqueeze(1).broadcast_to([P, HPG, P]), ALU.mult)
                    last.then_inc(m_ready, 1)
                dve.wait_ge(fbg_ready, (NU + 2) * L + b + 1)
                if b < NU:
                    s = b % 2
                    if b >= 2:
                        dve.wait_ge(m_ready, NU * L + b - 1)
                    TT(gm[:, s, 0, :], X[2][:, 0:P], tri[:, 0, :], ALU.mult)
                    TT(gm[:, s, 1, :], X[2][:, 0:P], maskb[:, :], ALU.mult)
                if b >= 2:
                    c, g = B_UNITS[b - 2]
                    xf = x_tok[:, c, g * GC:(g + 1) * GC]
                    xg = xf.rearrange("p (h w) -> p h w", w=HD)
                    hs = slice(HPG * g, HPG * (g + 1))
                    ya, yb = yab[:, 0, :, :], yab[:, 1, :, :]
                    flat = [yab[:, i, :, :].rearrange("p h w -> p (h w)") for i in range(2)]
                    if b > 2:
                        dve.wait_ge(y_ready, NU * L + b - 2)
                    if c > 0:
                        TT(ya, X[2][:, P:P + GC].rearrange("p (h w) -> p h w", w=HD), per_head(ex[:, 2, c, hs], HD), ALU.mult)
                        own.link(TT(yb, X[3][:, GC:2 * GC].rearrange("p (h w) -> p h w", w=HD),
                                    per_head(ex[:, 3, c, hs], HD), ALU.mult))
                        own.link(TT(flat[0], flat[0], flat[1], ALU.add))
                        own.mark(TT(yb, xg, per_head(dskip_sb[:, L, hs], HD), ALU.mult))
                        TT(flat[0], flat[0], X[3][:, 0:GC], ALU.add).then_inc(y_out, 1)
                    else:
                        own.link(nc.vector.tensor_copy(flat[0], X[3][:, 0:GC]))
                        TT(yb, xg, per_head(dskip_sb[:, L, hs], HD), ALU.mult).then_inc(y_out, 1)
                if b < NU:
                    c, g = B_UNITS[b]
                    s = b % 2
                    dve.wait_ge(t_ready, NU * L + b + 1)
                    for h in range(HPG):
                        j = HPG * g + h
                        last = STT(out=dmat[:, s, h, :], in0=X[1][:, P * h:P * (h + 1)], scalar=ebs[:, c, j:j + 1],
                                   in1=dmat[:, s, h, :], op0=ALU.add, op1=ALU.min)
                    last.then_inc(d_ready, 1)
                if b >= 2:
                    dve.wait_ge(y_out, NU * L + b - 1)
                    TT(xf, flat[0], flat[1], ALU.add).then_inc(y_ready, 1)
                if b < NU:
                    xg = x_tok[:, c, g * GC:(g + 1) * GC].rearrange("p (h w) -> p h w", w=HD)
                    for d in range(2):
                        TT(xfb[:, s, d, :, :], xg, per_head(tm[:, c, NH * d + HPG * g:NH * d + HPG * (g + 1)], HD), ALU.mult)

            for what, n in order_uz():
                if what == "burst":
                    if n == 0:
                        dve.wait_ge(tp_out, 16 * (L + 1))
                    b_unit(n)
                    layer_norm(n)
                    continue
                t, j = T0 + T_UZ + n, n // 2
                if n % 2 == 1:
                    dve.wait_ge(zt_ready, 16 * L + j + 1)
                    if n == 1:
                        dve.wait_ge(tp_ready, 16 * (L + 1))
                    free(t, STT(out=halves(c_buf[1]), in0=halves(c_buf[0]), scalar=1.0,
                                in1=acc_of(t)[:, :, 0:HALF], op0=ALU.add, op1=ALU.mult))
                    evacuated(dve, t)
                    evacuated(dve, t - 1)
                    own.mark(TT(uz[:, j, :], uz[:, j, :], c_buf[1][:, :], ALU.mult))

            own.wait()
            for j in range(8):
                t = T0 + T_ZM + j
                n = 8 * L + j
                dve.wait_ge(zt_ready, 16 * L + 8 + j + 1)
                if j > 0:
                    dve.wait_ge(ymhi_ready, n)
                    dve.wait_ge(ym_ready, n)
                free(t, STT(out=halves(c_buf[1]), in0=halves(c_buf[0]), scalar=1.0,
                            in1=acc_of(t)[:, :, 0:HALF], op0=ALU.add, op1=ALU.mult))
                evacuated(dve, t)
                dve.wait_ge(yT_mm, n + 1)
                cx = c_buf[1][:, 0:CTX]
                STT(out=cx, in0=X[1][:, 0:P], scalar=0.5, in1=cx, op0=ALU.mult, op1=ALU.mult)
                lat = c_buf[1][:, CTX:TOK].rearrange("p (r w) -> p r w", w=GW)
                src = X[0][:, :].rearrange("p (r w) -> p r w", w=GW) if L % 2 == 0 else \
                    X[0][:, :].rearrange("p (w r) -> p r w", r=GH)
                STT(out=lat, in0=src, scalar=0.5, in1=lat, op0=ALU.mult, op1=ALU.mult).then_inc(y2_ready, 1)
                dve.wait_ge(sp_mm, n + 1)
                if j > 0:
                    dve.wait_ge(yghi_ready, n)
                    dve.wait_ge(yg_ready, n)
                STT(out=c_buf[4][:, CTX:TOK].rearrange("p (c n) -> p c n", n=P),
                    in0=X[2][:, :].rearrange("p (c n) -> p c n", n=P), scalar=lnw_sb[:, L, j:j + 1],
                    in1=pbb[:, j, :].unsqueeze(1).broadcast_to([P, NCH - 1, P]), op0=ALU.mult, op1=ALU.add)
                STT(out=c_buf[4][:, 0:CTX], in0=X[3][:, 0:P], scalar=lnw_sb[:, L, j:j + 1], in1=pbb[:, j, :],
                    op0=ALU.mult, op1=ALU.add).then_inc(sp_used, 1)
                add_square(2 * L + 1, j)
                dve.wait_ge(sp_used, n + 1)
                STT(out=c_buf[4][:, :], in0=c_buf[4][:, :], scalar=0.5, in1=uz[:, j, :],
                    op0=ALU.mult, op1=ALU.mult).then_inc(ya_ready, 1)
                dve.wait_ge(ymhi_ready, n + 1)
                STT(out=ym_lo[:, j, :], in0=c_buf[1][:, :], scalar=ssmw_sb[:, L, j:j + 1], in1=f(ym_hi[:, j, :]),
                    op0=ALU.mult, op1=ALU.subtract).then_inc(ym_ready, 1)
                dve.wait_ge(yghi_ready, n + 1)
                TT(yg_lo[:, j, :], c_buf[4][:, :], f(yg_hi[:, j, :]), ALU.subtract).then_inc(yg_ready, 1)

            def merge_lo(k):
                dve.wait_ge(mhi_ready, 8 * L + k + 1)
                TT(h_lo[:, k, :], mg[:, k, :], f(h_hi[:, k, :]), ALU.subtract).then_inc(mh_ready, 1)

            for j in range(8):
                t = T0 + T_S5 + 4 * j
                if j == 0:
                    rstd(2 * L + 1)
                if L == 0:
                    ada(4 * j)
                for b, tt in ((0, t + 1), (1, t + 3)):
                    if b == 1 and j == 7:
                        for k in range(KC - 1):
                            merge_lo(k)
                    dve.wait_ge(tile_done, tt + 1)
                    evacuated(dve, tt - 1)
                    o = c_buf[4][:, :] if b == 0 else mg[:, j, :]
                    if b == 0 and j > 0:
                        dve.wait_ge(mg_ready, 8 * L + j)
                    free(tt, STT(out=halves(o), in0=halves(c_buf[b]), scalar=1.0, in1=acc_of(tt)[:, :, 0:HALF],
                                 op0=ALU.add, op1=ALU.mult))
                    if L == 0 and b == 0:
                        ada(4 * j + 1)
                        ada(4 * j + 2)
                if j == 0:
                    dve.wait_ge(ry_ready, L + 1)
                evacuated(dve, t + 3)
                own.link(TT(mg[:, j, :], mg[:, j, :], c_buf[2][:, :], ALU.mult))
                STT(out=mg[:, j, :], in0=c_buf[4][:, :], scalar=0.5, in1=mg[:, j, :],
                    op0=ALU.mult, op1=ALU.add).then_inc(mg_ready, 1)
                if L == 0:
                    if j > 0:
                        job_out(3 + j)
                    ada(4 * j + 3)
            merge_lo(KC - 1)

            dve.wait_ge(x_in, 16 * (L + 2))
            for j in range(8):
                t = T0 + T_OUT + j
                dve.wait_ge(tile_done, t + 1)
                n0 = HALF
                for v, cols, src in ((0, slice(0, CTX), acc_of(t)[:, 0, 0:CTX]),
                                     (1, slice(CTX, n0), acc_of(t)[:, 0, CTX:HALF]),
                                     (1, slice(n0, TOK), acc_of(t)[:, 1, 0:HALF])):
                    last = STT(out=xr[:, j, cols], in0=src, scalar=mods[:, 3 * L + 2, v, j:j + 1],
                               in1=xr[:, j, cols], op0=ALU.mult, op1=ALU.add)
                free(t, last)
                if j > 0:
                    add_square(2 * L + 2, j - 1)
                if L == 0 and j == 1:
                    job_out(11)
            add_square(2 * L + 2, 7)

        rstd(2 * DEPTH)
        dve.wait_ge(rbc_ready, 2 * DEPTH + 1)
        for k in range(KC):
            for cols, r in ((slice(0, CTX), X[1][:, 0:CTX]), (slice(CTX, TOK), X[0][:, 0:LAT])):
                last = STT(out=xr[:, k, cols], in0=xr[:, k, cols], scalar=finalw_sb[:, k:k + 1], in1=r,
                           op0=ALU.mult, op1=ALU.mult)
            last.then_inc(fin_ready, 1)

    ctx.close()


def kernel(**inputs):
    import numpy as np
    import concourse.bacc as bacc
    from concourse.bass_utils import run_bass_kernel_spmd

    a = {k: np.asarray(v) for k, v in inputs.items()}
    f32 = np.float32

    def tiles(w):
        L, _, n = w.shape
        return w.reshape(L, KC, P, n // P, P).transpose(0, 3, 2, 1, 4).reshape(L, n // P, P, KC * P)

    def cols(v):
        v = v.reshape(v.shape[:-1] + (v.shape[-1] // P, P))
        return np.ascontiguousarray(np.moveaxis(v, -1, 0))

    w_in = a["w_in"]
    s = np.cumsum([0, NCONV * P, DM, 32, DM, DM, DM, DM, DM])
    part = [w_in[:, :, s[i]:s[i + 1]] for i in range(8)]
    xbc, zm, dt, u, v, zg, glm, glg = part
    dt = np.concatenate([dt, np.zeros((DEPTH, DM, P - 32), f32)], axis=2)
    xbc_t, zm_t, u_t, v_t, zg_t, glm_t, glg_t = (tiles(w) for w in (xbc, zm, u, v, zg, glm, glg))
    om_t, og_t, out_t = tiles(a["w_out_m"]), tiles(a["w_out_g"]), tiles(a["w_out"])
    uz = np.stack([u_t, zg_t], axis=2).reshape(DEPTH, 16, P, KC * P)
    s5 = np.stack([glg_t, og_t, glm_t, om_t], axis=2).reshape(DEPTH, 32, P, KC * P)
    wts = np.concatenate([tiles(dt), xbc_t[:, 8:], xbc_t[:, :8], v_t, uz, zm_t, s5, out_t], axis=1)
    wts = wts.reshape(DEPTH * N_TILES, P, KC * P)
    wada = a["w_ada"].reshape(DEPTH, 4, 2, P, 3, 2, 512).transpose(0, 4, 5, 1, 3, 2, 6)
    x = np.concatenate([a["x_prompt"][0], a["x_sample"][0]], axis=0)
    xT = x.T.reshape(KC, P, TOK).transpose(1, 0, 2)
    conv = np.concatenate([a["conv_w"], a["conv_b"][:, None, :]], axis=1)
    conv = conv.reshape(DEPTH, TAPS + 1, NCONV, P).transpose(3, 0, 2, 1)
    h0 = a["state_ssm"][0].reshape(DEPTH, 2, DM, P).transpose(0, 1, 3, 2)
    ins = {
        "xT": xT, "wts": wts, "wada": wada,
        "cT": cols(np.stack([a["c_ctx"], a["c"][0]])).transpose(0, 2, 1),
        "bada": cols(a["b_ada"].reshape(DEPTH * 3, DM)), "normw": cols(a["norm_w"]),
        "finalw": cols(a["final_norm_w"]), "ssmw": cols(a["ssm_norm_w"]), "convw": conv,
        "dtb": a["dt_bias"].reshape(DEPTH, 32).T, "alog": a["a_log"].reshape(DEPTH, 32).T,
        "dskip": np.broadcast_to(a["d_skip"][None], (P, DEPTH, NH)), "lnw": cols(a["sgu_ln_w"]),
        "lnb": a["sgu_ln_b"], "wsp": a["w_sp"].transpose(0, 3, 1, 2), "bsp": a["b_sp"].reshape(DEPTH, DM),
        "h0": h0,
    }
    ins = {k: np.ascontiguousarray(v) for k, v in ins.items()}
    nc = bacc.Bacc("TRN2", target_bir_lowering=False, num_devices=1, dynamic_dma_scratch_size=1024)
    aps = {k: nc.dram_tensor(f"in_{k}", v.shape, F32, kind="ExternalInput").ap() for k, v in ins.items()}
    yT = nc.dram_tensor("yT", (P, KC, TOK), F32, kind="ExternalOutput").ap()
    st = nc.dram_tensor("st", (DEPTH, 2, P, DM), F32, kind="ExternalOutput").ap()
    x_mid = nc.dram_tensor("x_mid", (P, KC, TOK), F32, kind="Internal").ap()
    build(nc, **aps, yT=yT, st_out=st, x_mid=x_mid)
    r = run_bass_kernel_spmd(nc, [{f"in_{k}": v for k, v in ins.items()}], core_ids=[0])
    y = np.asarray(r.results[0]["yT"]).transpose(1, 0, 2).reshape(DM, TOK).T
    new = np.asarray(r.results[0]["st"]).transpose(0, 1, 3, 2).reshape(1, DEPTH, 2, NH, HD, P)
    return (np.ascontiguousarray(y[None, :CTX]), np.ascontiguousarray(y[None, CTX:]), np.ascontiguousarray(new))
```

```python
from contextlib import ExitStack

import concourse.bass as bass
from concourse import mybir

P = 128
DEPTH, DM = 2, 1024
KC = DM // P
CTX, LAT = 128, 512
TOK = CTX + LAT
HALF = TOK // 2
GW, GH = 64, LAT // 64
NCH = TOK // P
NH, HD, NG = 16, 64, 4
HPG = NH // NG
GC = HPG * HD
TAPS = 5
PAD = TAPS // 2
CW = CTX + PAD + LAT
LAT0 = CTX + PAD
RAW = CW + 2 * PAD
PITCH = (RAW + 7) // 8 * 8
NCONV = 16
EPS = 1e-6

N_TILES = 1 + NCONV + 8 + 16 + 8 + 32 + 8
T_CONV, T_V, T_UZ, T_ZM, T_S5, T_OUT = 1, 17, 25, 41, 49, 81

F32 = mybir.dt.float32
F32R = mybir.dt.float32r
ALU = mybir.AluOpType
ACT = mybir.ActivationFunctionType
AXX = mybir.AxisListType.X

A_UNITS = [(c, g) for g in range(NG) for c in range(NCH)]
B_UNITS = [(c, g) for c in range(NCH) for g in range(NG)]
NU = len(A_UNITS)
A_STEPS = (2, 5, 8)
B_STEPS = [9 + 28 * b // 5 for b in range(NU + 2)]
JOBS_FIRST = [(0, q, h) for q in (1, 0) for h in (0, 1)]
NF = len(JOBS_FIRST)
DVE_FIRST = 2
JOBS_LATER = [(0, 2, 0), (0, 2, 1)] + [(1, q, h) for q in range(3) for h in (0, 1)]


def order_uz():
    out = [((8 * (n + 1), 1), ("tile", n)) for n in range(16)]
    out += [((at, 0), ("burst", b)) for b, at in enumerate(B_STEPS)]
    return [x for _, x in sorted(out)]


class Chain:

    def __init__(self, eng, sem):
        self.eng, self.sem, self.n = eng, sem, 0

    def mark(self, ins):
        ins.then_inc(self.sem, 1)
        self.n += 1
        return self.n

    def wait(self, n=None):
        self.eng.wait_ge(self.sem, self.n if n is None else n)

    def link(self, ins):
        self.mark(ins)
        self.wait()


def build(nc, xT, wts, wada, cT, bada, normw, finalw, ssmw, convw, dtb, alog, dskip, lnw, lnb,
          wsp, bsp, h0, yT, st_out, x_mid, cum_dram):
    ctx = ExitStack()
    pos = [1152]

    def region(nbytes):
        at = pos[0]
        pos[0] += (nbytes + 31) // 32 * 32
        assert pos[0] <= nc.sbuf_usable_end, pos[0]
        return at

    def place(name, shape, at, dt=F32):
        return nc.alloc_sbuf_tensor_at(name, shape, dt, offset=at)

    def new(name, shape, dt=F32):
        n = 4
        for s in shape[1:]:
            n *= s
        return place(name, shape, region(n), dt)

    ACTB = KC * TOK * 4
    h_hi = new("h_hi", [P, KC, TOK], F32R)
    h_lo = new("h_lo", [P, KC, TOK], F32R)
    w_st = new("w_st", [P, 2, KC * P])
    w_hi = new("w_hi", [P, 2, KC * P], F32R)
    w_lo = new("w_lo", [P, 2, KC * P], F32R)
    r_v = region(ACTB)
    v_tok = place("v_tok", [P, NCH, DM], r_v)
    mg = place("mg", [P, KC, TOK], r_v)
    r_uz = region(ACTB)
    uz = place("uz", [P, KC, TOK], r_uz)
    yg_lo = place("yg_lo", [P, KC, TOK], r_uz, F32R)
    r_r = region(ACTB)
    yg_hi = place("yg_hi", [P, KC, TOK], r_r, F32R)
    bsp_row = place("bsp_row", [1, DM], r_r + 15360)
    r_x = region(ACTB)
    x_tok = place("x_tok", [P, NCH, DM], r_x)
    xr = place("xr", [P, KC, TOK], r_x)
    r_bc = region(8 * CW * 4)
    bc = place("bc", [P, 8, CW], r_bc)
    ym_lo = place("ym_lo", [P, KC, TOK], r_bc, F32R)
    r_t = region(ACTB)
    ym_hi = place("ym_hi", [P, KC, TOK], r_t, F32R)
    raw = place("raw", [P, 2, PITCH], r_t)
    cv = place("cv", [P, 2, PITCH], r_t + 8 * PITCH)
    cvt = place("cvt", [P, PITCH], r_t + 16 * PITCH)
    xo = place("xo", [P, 2, PITCH], r_t + 20 * PITCH)
    dmat = place("dmat", [P, 2, HPG, P], r_t)
    mmat = place("mmat", [P, 2, HPG, P], r_t + 8192)
    gdt = place("gdt", [P, 2, HPG, P], r_t + 12288)
    gm = place("gm", [P, 2, 2, P], r_t + 16384)
    yab = place("yab", [P, 2, HPG, HD], r_t + 18432)
    scan_tmp = place("scan_tmp", [P, DM], r_t + 4096)
    r_wp = region(8 * DM)
    wsp_sb = place("wsp_sb", [P, 8, P], r_wp)
    lnb_sb = place("lnb_sb", [P, DM], r_wp + 4 * DM)
    pbb = place("pbb", [P, 8, P], r_wp + 4 * DM)
    ada_st = place("ada_st", [P, 2, 2, 512], r_wp)
    ada_pre = place("ada_pre", [P, 4 * NF - 1, 2, 512], r_v)
    r_c = region(5 * TOK * 4)
    c_buf = [place(f"c_buf{i}", [P, TOK], r_c + i * TOK * 4) for i in range(5)]
    xw = place("xw", [P, 2, 2, HPG, HD], r_c + 2 * TOK * 4)
    bt = place("bt", [P, 2, P], r_c + 2 * TOK * 4 + 4096)
    ctx_st = place("ctx_st", [P, 2 * GC], r_c + 4 * TOK * 4)
    dta = place("dta", [64, TOK], r_c + 4 * TOK * 4)
    cum_bc = [place(f"cum_bc{i}", [P, 2, HPG, P], at) for i, at in enumerate((r_t + 4096, r_c + 2 * TOK * 4))]
    r_a0, r_a1 = region(4096), region(4096)
    ada_row = place("ada_row", [2, 2, 512], r_a1)
    ada_acc = [place(f"ada_acc{i}", [P, 2, 512], at) for i, at in enumerate((r_a0, r_a1))]
    st_at = [r_r + i * 4096 for i in range(5)] + [r_wp, r_wp + 4096, r_a0]
    states = [place(f"states{i}", [P, DM], at) for i, at in enumerate(st_at)]
    tm = place("tm", [P, NCH, 64], r_a1)
    ex = place("ex", [P, 6, NCH, NH], r_a1 + 1280)
    ncf = place("ncf", [P, NCH, NH], r_a1 + 3200)
    ebs = place("ebs", [P, NCH, NH], r_a1 + 3520)
    r_cum = region(TOK * 4)
    cum_t = place("cum_t", [64, TOK], r_cum)
    ssq = place("ssq", [P, TOK], r_cum)
    tri = new("tri", [P, 2, P])
    maskb = new("maskb", [P, P])
    ident = new("ident", [P, P])
    ones = new("ones", [P, P])
    c_sb = new("c_sb", [P, KC, 2])
    sc = new("sc", [P, 2, KC, 2])
    mods = new("mods", [P, DEPTH * 3, 2, KC])
    amul = new("amul", [P, DEPTH, 2, KC])
    bada_sb = new("bada_sb", [P, DEPTH * 3, KC])
    normw_sb = new("normw_sb", [P, DEPTH, KC])
    finalw_sb = new("finalw_sb", [P, KC])
    ssmw_sb = new("ssmw_sb", [P, DEPTH, KC])
    convw_sb = new("convw_sb", [P, DEPTH, NCONV, TAPS + 1])
    dtb_sb = new("dtb_sb", [32, DEPTH])
    ea = new("ea", [32, DEPTH])
    dskip_sb = new("dskip_sb", [P, DEPTH, NH])
    lnw_sb = new("lnw_sb", [P, DEPTH, KC])
    bst = new("bst", [P, NCH, 12])
    mv = new("mv", [P, NCH, 2])
    rv = new("rv", [P, NCH, 1])
    rst = new("rst", [P, 2, NCH])
    eps_sb = new("eps_sb", [P, 1])
    warm = new("warm", [P, 1])
    job_sum = new("job_sum", [P, 2, 4])

    acc = [ctx.enter_context(nc.psum_tensor(f"acc{i}", [P, 2, 512], F32)) for i in range(2)]
    X = [ctx.enter_context(nc.psum_tensor(f"X{i}", [P, 512], F32)) for i in range(4)]

    def sem(name):
        return ctx.enter_context(nc.semaphore(name))

    w_landed = [sem("w_landed0"), sem("w_landed1")]
    w_split, tile_done, w_go = sem("w_split"), sem("tile_done"), sem("w_go")
    acc_free = [sem("acc_free0"), sem("acc_free1")]
    consts_in, consts_made, x_in = sem("consts_in"), sem("consts_made"), sem("x_in")
    x_stored, out_done, wsp_in = sem("x_stored"), sem("out_done"), sem("wsp_in")
    st_in, st_stored = sem("st_in"), sem("st_stored")
    ada_in = [sem("ada_in0"), sem("ada_in1")]
    ada_used, ada_mm = sem("ada_used"), sem("ada_mm")
    pre_in = [sem(f"pre_in{i}") for i in range(2 * NF)]
    row_mm, row_out, job_read = sem("row_mm"), sem("row_out"), sem("job_read")
    c_in, ct_ready, sc_ready = sem("c_in"), sem("ct_ready"), sem("sc_ready")
    sq_ready, sq_used, ssq_ready, stat_ready = sem("sq_ready"), sem("sq_used"), sem("ssq_ready"), sem("stat_ready")
    root_ready, rstd_ready, rbc_ready = sem("root_ready"), sem("rstd_ready"), sem("rbc_ready")
    hpre_ready, hhi_ready, h_ready = sem("hpre_ready"), sem("hhi_ready"), sem("h_ready")
    dte_arg, dte_ready = sem("dte_arg"), sem("dte_ready")
    dtu_ready, dtl_ready, dta_ready = sem("dtu_ready"), sem("dtl_ready"), sem("dta_ready")
    tmT_ready, tm_ready, cum_mm = sem("tmT_ready"), sem("tm_ready"), sem("cum_mm")
    cum_stored, cum_in = sem("cum_stored"), [sem("cum_in0"), sem("cum_in1")]
    cumT_mm, cum_ready, ex_arg, ex_ready = sem("cumT_mm"), sem("cum_ready"), sem("ex_arg"), sem("ex_ready")
    pads_ready, cv_ready, cvt_ready, conv_done = sem("pads_ready"), sem("cv_ready"), sem("cvt_ready"), sem("conv_done")
    tp_ready, tp_out, ln_ready = sem("tp_ready"), sem("tp_out"), sem("ln_ready")
    bt_mm, bt_ready, xw_ready, s_mm, s_out = sem("bt_mm"), sem("bt_ready"), sem("xw_ready"), sem("s_mm"), sem("s_out")
    scan_done, vvar, vroot = sem("scan_done"), sem("vvar"), sem("vroot")
    fbg_ready, t_ready, d_ready, e_ready = sem("fbg_ready"), sem("t_ready"), sem("d_ready"), sem("e_ready")
    gm_ready, gb_ready = sem("gm_ready"), sem("gb_ready")
    m_ready, y_out, y_ready = sem("m_ready"), sem("y_out"), sem("y_ready")
    zt_ready = sem("zt_ready")
    pbb_mm, pbb_ready, sp_mm, sp_used = sem("pbb_mm"), sem("pbb_ready"), sem("sp_mm"), sem("sp_used")
    ya_ready, yghi_ready, yg_ready = sem("ya_ready"), sem("yghi_ready"), sem("yg_ready")
    yT_mm, y2_ready, ymhi_ready, ym_ready = sem("yT_mm"), sem("y2_ready"), sem("ymhi_ready"), sem("ym_ready")
    ry_ready, gt_ready, mg_ready, mhi_ready, mh_ready = sem("ry_ready"), sem("gt_ready"), sem("mg_ready"), sem("mhi_ready"), sem("mh_ready")
    fin_ready = sem("fin_ready")
    s_act, s_dve, s_pool = sem("s_act"), sem("s_dve"), sem("s_pool")

    def ada_first(n):
        return ada_pre[:, n, :, :] if n < 4 * NF - 1 else ada_st[:, 0, :, :]

    def acc_of(t):
        return acc[t % 2]

    def f(ap):
        return ap.bitcast(F32)

    def chunk_off(c):
        return 0 if c == 0 else LAT0 + P * (c - 1)

    def xcols(pair, c):
        return pair[1][:, 0:P] if c == 0 else pair[0][:, P * (c - 1):P * c]

    def evacuated(eng, t):
        eng.wait_ge(acc_free[t % 2], t // 2 + 1)

    def halves(buf):
        return buf[:, 0:TOK].rearrange("p (b n) -> p b n", b=2)

    block = ctx.enter_context(nc.Block())

    @block.sync
    def _(sp):
        def weight(t, slot):
            sp.dma_start(w_st[:, slot, :], wts[t, :, :]).then_inc(w_landed[slot], 16)

        def ada(n):
            if n >= 2:
                sp.wait_ge(ada_used, 4 + n - 1)
            L, q, hf = JOBS_LATER[n // 4]
            sp.dma_start(ada_st[:, n % 2, :, :], wada[L, q, hf, n % 4, :, :, :]).then_inc(ada_in[n % 2], 16)

        def load_consts():
            for dst, src in ((bada_sb, bada), (normw_sb, normw), (finalw_sb, finalw), (ssmw_sb, ssmw),
                             (convw_sb, convw), (dtb_sb, dtb), (ea, alog), (dskip_sb, dskip), (lnw_sb, lnw)):
                dst = dst[:]
                sp.dma_start(dst, src).then_inc(consts_in, 16)

        sp.dma_start(c_sb[:, :, :], cT).then_inc(c_in, 16)
        for n in range(4 * NF):
            L, q, hf = JOBS_FIRST[n // 4]
            sp.dma_start(ada_first(n), wada[L, q, hf, n % 4, :, :, :]).then_inc(pre_in[n // 2], 16)
            if n == 3:
                sp.dma_start(xr[:, :, :], xT).then_inc(x_in, 16)
                load_consts()
            if n in (7, 11):
                weight(n // 11, n // 11)
 
        def stream(lo, hi):
            with sp.Fori(lo // 2, hi // 2) as i:
                for slot in range(2):
                    sp.wait_ge(w_split, 2 * i + slot - 1)
                    weight(2 * i + slot, slot)

        stream(2, 50)
        for n in range(4 * len(JOBS_LATER)):
            t = 50 + n
            sp.wait_ge(w_split, t - 1)
            weight(t, t % 2)
            if n == 0:
                sp.wait_ge(sp_used, 8)
            ada(n)
        stream(82, DEPTH * N_TILES)
        for k in range(KC):
            sp.wait_ge(fin_ready, k + 1)
            sp.dma_start(yT[:, k, :], xr[:, k, :]).then_inc(out_done, 16)
        sp.wait_ge(out_done, 16 * KC)
        sp.wait_ge(st_stored, 32 * NG * DEPTH)
        sp.wait_ge(x_stored, 16)

    @block.gpsimd
    def _(pool):
        own = Chain(pool, s_pool)
        nc.gpsimd.memset(tri[:, :, :], 1.0)
        nc.gpsimd.memset(maskb[:, :], 1.0)
        nc.gpsimd.memset(ident[:, :], 0.0)
        nc.gpsimd.memset(ones[:, :], 1.0)
        own.link(nc.gpsimd.memset(eps_sb[:, :], EPS))
        for d in range(2):
            nc.gpsimd.affine_select(out=tri[:, d, :], in_=tri[:, d, :], compare_op=ALU.is_ge, fill=0.0,
                                    base=-d, pattern=[[1, P]], channel_multiplier=-1)
        nc.gpsimd.affine_select(out=maskb[:, :], in_=maskb[:, :], compare_op=ALU.is_ge, fill=0.0,
                                base=0, pattern=[[-1, P]], channel_multiplier=1)
        nc.gpsimd.affine_select(out=ident[:, :], in_=ident[:, :], compare_op=ALU.not_equal, fill=1.0,
                                base=0, pattern=[[-1, P]], channel_multiplier=1).then_inc(consts_made, 1)

        def split(slot, landed, done):
            pool.wait_ge(w_landed[slot], landed)
            if done is not None:
                pool.wait_ge(tile_done, done)
                pool.sem_inc(w_go, 1)
            nc.gpsimd.tensor_copy(w_hi[:, slot, :], w_st[:, slot, :]).then_inc(s_pool, 1)

        def split_lo(slot, n):
            pool.wait_ge(s_pool, n)
            nc.gpsimd.tensor_tensor(w_lo[:, slot, :], w_st[:, slot, :], f(w_hi[:, slot, :]),
                                    ALU.subtract).then_inc(w_split, 1)

        base = own.n
        for slot in range(2):
            split(slot, 16, None)
            split_lo(slot, base + slot + 1)
        with pool.Fori(1, DEPTH * N_TILES // 2) as i:
            for slot in range(2):
                split(slot, 16 * i + 16, 2 * i + slot - 1)
                split_lo(slot, 2 * i + (base + slot + 1))

    @block.tensor
    def _(pe):
        mm = nc.tensor.matmul

        def tile(t, hi, lo, ready=None, hooks=()):
            pe.wait_ge(w_split, t + 1)
            if t >= 2:
                pe.wait_ge(acc_free[t % 2], t // 2)
            a, s = acc_of(t), t % 2
            for k in range(KC):
                cols = slice(k * P, (k + 1) * P)
                for n, (w, x) in enumerate(((w_hi, hi), (w_lo, hi), (w_hi, lo))):
                    if ready is not None and n != 1:
                        pe.wait_ge(ready[n // 2], 8 * ready[2] + k + 1)
                    for hf in range(2):
                        last = mm(a[:, hf, 0:HALF], w[:, s, cols], x[:, k, hf * HALF:(hf + 1) * HALF],
                                  start=(k == 0 and n == 0), stop=(k == KC - 1 and n == 2))
                if k == KC - 1:
                    last.then_inc(tile_done, 1)
                for at, hook in hooks:
                    if at == k + 1:
                        hook()

        def job_mm(n):
            pe.wait_ge(ada_used, 4 * (n + 1))
            if n == 0:
                pe.wait_ge(job_read, DVE_FIRST)
            for v in range(2):
                for j in range(4):
                    last = nc.tensor.transpose(X[2 + v][:, P * j:P * (j + 1)], ada_acc[n % 2][:, v, P * j:P * (j + 1)],
                                               ident[:, :])
            last.then_inc(ada_mm, 1)

        def first_mm(n):
            pe.wait_ge(sc_ready, 1)
            at = 4 * (n if n < DVE_FIRST else n + 1)
            if n >= 2:
                pe.wait_ge(row_out, n - 1)
            for k in range(KC):
                if k % 4 == 0:
                    pe.wait_ge(pre_in[(at + k // 2) // 2], 32)
                last = mm(acc[n % 2][0:2, 0, :], sc[:, 1, k, :], ada_first(at + k // 2)[:, k % 2, :],
                          start=(k == 0), stop=(k == KC - 1))
            last.then_inc(row_mm, 1)

        def first_tp(n):
            pe.wait_ge(row_out, n + 1)
            if n > 0:
                pe.wait_ge(job_read, n if n < DVE_FIRST else n + 1)
            for j in range(4):
                last = nc.tensor.transpose(X[2][:, 0:8].rearrange("p (v j) -> p j v", v=2)[:, j, :],
                                           ada_row[:, n % 2, P * j:P * (j + 1)], ident[0:2, 0:2])
            last.then_inc(ada_mm, 1)

        def stat_mm(n):
            pe.wait_ge(ssq_ready, n + 1)
            for c in range(NCH):
                last = mm(X[0][:, c:c + 1], ssq[:, P * c:P * (c + 1)], ones[:, 0:1], start=True, stop=True)
            last.then_inc(stat_ready, 1)

        def stat_bc(n):
            pe.wait_ge(rstd_ready, n + 1)
            for c in range(NCH):
                last = mm(xcols((X[0], X[1]), c), rst[:, 1, c:c + 1].broadcast_to([P, P]), ident[:, :],
                          start=True, stop=True)
            last.then_inc(rbc_ready, 1)

        def transposes(src, n):
            if n > 0:
                pe.wait_ge(tp_out, n)
            for c in range(NCH):
                last = nc.tensor.transpose(xcols((X[0], X[1]), c), src(c), ident[:, :])
            last.then_inc(tp_ready, 1)

        def dt_cums(L):
            pe.wait_ge(dta_ready, L + 1)
            for c in range(NCH):
                last = nc.tensor.transpose(X[2][:, 64 * c:64 * (c + 1)], dta[:, P * c:P * (c + 1)], ident[0:64, 0:64])
            last.then_inc(tmT_ready, 1)

        def dt_cums2(L):
            pe.wait_ge(tm_ready, L + 1)
            mm(X[3][:, 0:80], tri[:, 0, :], tm[:, :, 32:48], start=True, stop=True)
            mm(X[3][:, 80:160], tri[:, 1, :], tm[:, :, 48:64], start=True, stop=True)
            mm(X[3][:, 160:320], ones[:, :], tm[:, :, 32:64], start=True, stop=True).then_inc(cum_mm, 1)

        def dt_cums3(L):
            for d in range(2):
                for c in range(NCH):
                    last = mm(xcols((X[0], X[1]), c)[32 * d:32 * d + NH, :],
                              tm[:, c, 32 + NH * d:32 + NH * (d + 1)], tri[:, d, :], start=True, stop=True)
            last.then_inc(cumT_mm, 1)

        def a_burst(L, a):
            if a > 0:
                c, g = A_UNITS[a - 1]
                n = NU * L + a
                pe.wait_ge(bt_ready, n)
                pe.wait_ge(xw_ready, n)
                if n > 1:
                    pe.wait_ge(s_out, n - 1)
                s = (a - 1) % 2
                cols = slice(0, GC) if c == 1 else slice(GC, 2 * GC) if c == NCH - 1 else slice(0, 2 * GC)
                mm(X[3][:, cols], bt[:, s, :], xw[:, s, :, :, :].rearrange("p d h w -> p (d h w)")[:, cols],
                   start=True, stop=True).then_inc(s_mm, 1)
            if a < NU:
                c, g = A_UNITS[a]
                if c == 0:
                    pe.wait_ge(tp_out, 16 * L + 2 * (g + 1))
                off = chunk_off(c)
                nc.tensor.transpose(X[2][:, 0:P], bc[:, g, off:off + P], ident[:, :]).then_inc(bt_mm, 1)

        def b_burst(L, b):
            base = NU * L
            if b >= 2:
                u = b - 2
                c, g = B_UNITS[u]
                s = u % 2
                pe.wait_ge(m_ready, base + u + 1)
                if u > 0:
                    pe.wait_ge(y_out, base + u)
                if u == HPG:
                    pe.wait_ge(scan_done, L + 1)
                    pe.wait_ge(tp_out, 16 * (L + 1))
                off = chunk_off(c)
                for h in range(HPG):
                    y = X[3][:, h * HD:(h + 1) * HD]
                    last = mm(y, mmat[:, s, h, :], x_tok[:, c, g * GC + h * HD:g * GC + (h + 1) * HD],
                              start=True, stop=True)
                if c > 0:
                    cg = bc[:, 4 + g, off:off + P]
                    cols = slice(g * GC, (g + 1) * GC)
                    for d in range(2):
                        last = mm(X[u % 2][:, d * GC:(d + 1) * GC], cg, states[2 * (c - 1) + d][:, cols],
                                  start=True, stop=True)
                if b >= NU:
                    last.then_inc(fbg_ready, 1)
            if b < NU:
                c, g = B_UNITS[b]
                off = chunk_off(c)
                if b == 0:
                    pe.wait_ge(s_out, NU * (L + 1))
                else:
                    pe.wait_ge(gm_ready, base + b)
                mm(X[2][:, 0:P], bc[:, g, off:off + P], bc[:, 4 + g, off:off + P],
                   start=True, stop=True).then_inc(fbg_ready, 1)

        def pbb_products(L):
            pe.wait_ge(wsp_in, 48 * (L + 1))
            pe.wait_ge(y_ready, NU * (L + 1))
            for g in range(8):
                o = X[2 + g // 4][:, P * (g % 4):P * (g % 4 + 1)]
                mm(o, lnb_sb[:, P * g:P * (g + 1)], wsp_sb[:, g, :], start=True, stop=False)
                last = mm(o, ones[0:1, :], bsp_row[0:1, P * g:P * (g + 1)], start=False, stop=True)
            last.then_inc(pbb_mm, 1)

        def spatial(L, g):
            if g == 0:
                pe.wait_ge(ln_ready, NCH * (L + 1))
                pe.wait_ge(pbb_ready, 2 * (L + 1))
            else:
                pe.wait_ge(sp_used, 8 * L + g)
            for c in range(NCH):
                last = mm(xcols((X[2], X[3]), c), v_tok[:, c, P * g:P * (g + 1)], wsp_sb[:, g, :],
                          start=True, stop=True)
            last.then_inc(sp_mm, 1)

        def y_transposes(L, j):
            if j == 0:
                pe.wait_ge(y_ready, NU * (L + 1))
            else:
                pe.wait_ge(y2_ready, 8 * L + j)
            for c in range(NCH):
                last = nc.tensor.transpose(xcols((X[0], X[1]), c), x_tok[:, c, P * j:P * (j + 1)], ident[:, :])
            last.then_inc(yT_mm, 1)

        pe.wait_ge(consts_made, 1)
        first_mm(0)
        first_tp(0)
        first_mm(1)
        stat_mm(0)
        first_tp(1)
        stat_bc(0)
        first_mm(2)
        job_mm(0)
        first_tp(2)
        for L in range(DEPTH):
            T0 = L * N_TILES
            if L > 0:
                stat_mm(2 * L)
                stat_bc(2 * L)
            h = (h_hi, h_lo)
            tile(T0, *h, ready=(hhi_ready, h_ready, L))
            def x_transposes(j):
                pe.wait_ge(conv_done, NCONV * L + 9 + j)
                if j == 0:
                    pe.wait_ge(cum_ready, L + 1)
                transposes(lambda c: xo[:, j % 2, chunk_off(c):chunk_off(c) + P], 16 * L + j)

            def v_transposes(j):
                evacuated(pe, T0 + T_V + j)
                transposes(lambda c: c_buf[j % 2][:, P * c:P * (c + 1)], 16 * L + 8 + j)

            for i in range(NCONV):
                tile(T0 + T_CONV + i, *h, hooks=[(2, lambda: x_transposes(i - 11))] if i >= 11 else [])
                if i == 2:
                    dt_cums(L)
                if i == 4:
                    dt_cums2(L)
                if i == 5:
                    dt_cums3(L)
            for i in range(8):
                def bursts(n):
                    return lambda: a_burst(L, n)
                hooks = [(s, bursts(3 * i + n)) for n, s in enumerate(A_STEPS) if 3 * i + n <= NU]
                if i < 2:
                    hooks.append((1, lambda: x_transposes(5 + 2 * i)))
                hooks.append((6, (lambda: v_transposes(i - 1)) if i >= 1 else (lambda: x_transposes(6))))
                tile(T0 + T_V + i, *h, hooks=hooks)
            for n in range(16):
                hooks = []
                for b, at in enumerate(B_STEPS):
                    if 8 * n < at <= 8 * (n + 1):
                        hooks.append((at - 8 * n, (lambda b=b: b_burst(L, b))))
                if n == 0:
                    hooks.append((6, lambda: v_transposes(7)))
                tile(T0 + T_UZ + n, *h, hooks=hooks)
            for j in range(8):
                hooks = [(8, lambda: pbb_products(L))] if j == 0 else [(4, lambda: spatial(L, j - 1))]
                tile(T0 + T_ZM + j, *h, hooks=hooks)
                y_transposes(L, j)
            for j in range(8):
                t = T0 + T_S5 + 4 * j
                job = 1 + j
                tile(t, *h, hooks=[(3, lambda: spatial(L, 7))] if j == 0 else [])
                if j == 0:
                    stat_mm(2 * L + 1)
                tile(t + 1, yg_hi, yg_lo,
                     ready=(yghi_ready, yg_ready, L) if j == 0 else None)
                if j == 0:
                    stat_bc(2 * L + 1)
                tile(t + 2, *h)
                if L == 0 and j > 0:
                    job_mm(job - 1)
                tile(t + 3, ym_hi, ym_lo,
                     ready=(ymhi_ready, ym_ready, L) if j == 0 else None)
            for j in range(8):
                tile(T0 + T_OUT + j, *h,
                     ready=(mhi_ready, mh_ready, L) if j == 0 else None)
                if L == 0 and j == 0:
                    job_mm(8)
        stat_mm(2 * DEPTH)
        stat_bc(2 * DEPTH)

    @block.scalar
    def _(act):
        own = Chain(act, s_act)
        A = nc.scalar.activation

        def free(t, ins):
            ins.then_inc(acc_free[t % 2], 1)

        def pieces(a, dst_ctx, dst_lat, L, parts=P):
            n0 = (HALF - CTX) // GW
            if L % 2 == 0:
                lat = dst_lat.rearrange("p (r w) -> p r w", w=GW)
            else:
                lat = dst_lat.rearrange("p (w r) -> p r w", r=GH)
            return [(dst_ctx, a[0:parts, 0, 0:CTX]),
                    (lat[:, 0:n0, :], a[0:parts, 0, CTX:HALF].rearrange("p (r w) -> p r w", w=GW)),
                    (lat[:, n0:GH, :], a[0:parts, 1, 0:HALF].rearrange("p (r w) -> p r w", w=GW))]

        def root(n):
            act.wait_ge(stat_ready, n + 1)
            A(rst[:, 0, :], X[0][:, 0:NCH], ACT.Sqrt, scale=1.0 / DM, bias=eps_sb[:, 0:1]).then_inc(root_ready, 1)

        def warm_root():
            own.link(A(warm[:, :], eps_sb[:, :], ACT.Sqrt))

        def square(n, k, src):
            if k >= 2:
                act.wait_ge(sq_used, 7 * n + k - 1)
            elif n > 0:
                act.wait_ge(ssq_ready, n)
            A(c_buf[2 + k % 2][:, :], src, ACT.Square).then_inc(sq_ready, 1)

        def tp_copy(dst, n):
            act.wait_ge(tp_ready, n + 1)
            A(dst[:, 1:NCH, :], X[0][:, :].rearrange("p (c n) -> p c n", n=P), ACT.Copy)
            A(dst[:, 0, :], X[1][:, 0:P], ACT.Copy).then_inc(tp_out, 1)

        act.wait_ge(c_in, 16)
        A(sc[:, 0, :, :], c_sb[:, :, :], ACT.Tanh, scale=0.5).then_inc(ct_ready, 1)
        def row_copy(n):
            act.wait_ge(row_mm, n + 1)
            if n >= 2:
                act.wait_ge(ada_mm, n - 1)
            A(ada_row[:, n % 2, :], acc[n % 2][0:2, 0, :], ACT.Copy).then_inc(row_out, 1)

        row_copy(0)
        act.wait_ge(x_in, 16)
        for k in range(KC):
            square(0, k, xr[:, k, :])
        row_copy(1)
        root(0)
        row_copy(2)
        act.wait_ge(consts_in, 16 * 9)
        own.link(A(ea[:, :], ea[:, :], ACT.Exp))
        act.wait_ge(job_read, NF)

        for L in range(DEPTH):
            T0 = L * N_TILES

            if L > 0:
                root(2 * L)
            for k in range(KC):
                act.wait_ge(hpre_ready, 8 * L + k + 1)
                for v, cols in ((0, slice(0, CTX)), (1, slice(CTX, TOK))):
                    last = A(h_hi[:, k, cols], c_buf[k % 4][:, cols], ACT.Identity, bias=mods[:, 3 * L, v, k:k + 1])
                last.then_inc(hhi_ready, 1)

            act.wait_ge(tile_done, T0 + 1)
            for dst, src in pieces(acc_of(T0), c_buf[0][0:32, 0:CTX], c_buf[0][0:32, CTX:TOK], L, 32):
                last = A(dst, src, ACT.Identity, bias=dtb_sb[:, L:L + 1])
            free(T0, last)

            def a_copies(a):
                if a > 0:
                    c, g = A_UNITS[a - 1]
                    n = NU * L + a
                    act.wait_ge(s_mm, n)
                    cols = slice(g * GC, (g + 1) * GC)
                    if c == 0:
                        if g > 0 or L > 0:
                            act.wait_ge(st_stored, 32 * (NG * L + g))
                        A(ctx_st[:, :], X[3][:, :], ACT.Copy).then_inc(s_out, 1)
                        act.wait_ge(s_out, n)
                        for d in range(2):
                            act.dma_start(st_out[L, d, :, cols], ctx_st[:, d * GC:(d + 1) * GC])\
                                .then_inc(st_stored, 16)
                    else:
                        if c < NCH - 1:
                            last = A(states[2 * c][:, cols], X[3][:, 0:GC], ACT.Copy)
                        if c > 1:
                            last = A(states[2 * (c - 2) + 1][:, cols], X[3][:, GC:2 * GC], ACT.Copy)
                        last.then_inc(s_out, 1)
                if a < NU:
                    n = NU * L + a
                    act.wait_ge(bt_mm, n + 1)
                    if a >= 2:
                        act.wait_ge(s_mm, n - 1)
                    A(bt[:, a % 2, :], X[2][:, 0:P], ACT.Copy).then_inc(bt_ready, 1)

            def x_copy(j):
                tp_copy(x_tok[:, :, P * j:P * (j + 1)], 16 * L + j)

            def v_copy(j):
                tp_copy(v_tok[:, :, P * j:P * (j + 1)], 16 * L + 8 + j)

            for i in range(NCONV + 1):
                if 11 <= i < NCONV:
                    if L > 0 and i == 11:
                        act.wait_ge(x_stored, 16)
                    x_copy(i - 11)
                if i < NCONV:
                    t = T0 + T_CONV + i
                    act.wait_ge(tile_done, t + 1)
                    if i >= 2:
                        act.wait_ge(cv_ready, NCONV * L + i - 1)
                    else:
                        act.wait_ge(pads_ready, L + 1)
                    r = raw[:, i % 2, :]
                    for dst, src in pieces(acc_of(t), r[:, PAD:PAD + CTX], r[:, PAD + LAT0:PAD + LAT0 + LAT], L):
                        last = A(dst, src, ACT.Copy)
                    free(t, last)
                if i == 0:
                    act.wait_ge(dte_arg, L + 1)
                    A(c_buf[1][0:32, :], c_buf[1][0:32, :], ACT.Exp, scale=-1.0).then_inc(dte_ready, 1)
                    act.wait_ge(dtu_ready, L + 1)
                    A(c_buf[3][0:32, :], c_buf[2][0:32, :], ACT.Ln).then_inc(dtl_ready, 1)
                if i == 3:
                    act.wait_ge(tmT_ready, L + 1)
                    A(tm[:, :, :], X[2][:, 0:NCH * 64].rearrange("p (c r) -> p c r", r=64), ACT.Copy)\
                        .then_inc(tm_ready, 1)
                if i == 7:
                    act.wait_ge(cum_ready, L + 1)
                    for d in range(2):
                        act.dma_start(cum_dram[L, NH * d:NH * (d + 1), :], cum_t[32 * d:32 * d + NH, :])\
                            .then_inc(cum_stored, 16)
                    act.wait_ge(ex_arg, L + 1)
                    A(ex[:, :, :, :], ex[:, :, :, :], ACT.Exp).then_inc(ex_ready, 1)
                if i == NCONV:
                    x_copy(5)
                    a_copies(0)
                if i >= 1:
                    n = NCONV * L + i - 1
                    act.wait_ge(cv_ready, n + 1)
                    if n > 0:
                        act.wait_ge(conv_done, n)
                    A(cvt[:, 0:CW], cv[:, (i - 1) % 2, 0:CW], ACT.Tanh).then_inc(cvt_ready, 1)

            act.dma_start(states[0][:, :], h0[L, 0, :, :]).then_inc(st_in, 16)
            act.dma_start(states[2 * (NCH - 2) + 1][:, :], h0[L, 1, :, :]).then_inc(st_in, 16)
            for i in range(8):
                t = T0 + T_V + i
                if i == 1:
                    x_copy(7)
                for n in range(3):
                    if n == 2:
                        v_copy(i - 1) if i >= 1 else x_copy(6)
                    if 0 < 3 * i + n <= NU:
                        a_copies(3 * i + n)
                act.wait_ge(tile_done, t + 1)
                if i >= 2:
                    act.wait_ge(tp_ready, 16 * L + 8 + i - 1)
                free(t, A(halves(c_buf[i % 2]), acc_of(t)[:, :, 0:HALF], ACT.Gelu_apprx_tanh))

            def load_cum(b):
                c, g = B_UNITS[b]
                for d in range(2):
                    h = NH * d + HPG * g
                    act.dma_start(cum_bc[b % 2][:, d, :, :],
                                  cum_dram[L, h:h + HPG, P * c:P * (c + 1)].partition_broadcast(P))\
                        .then_inc(cum_in[b % 2], 16)

            v_copy(7)
            for what, n in order_uz():
                if what == "burst":
                    if 1 <= n <= NU:
                        act.wait_ge(d_ready, NU * L + n)
                        d = dmat[:, (n - 1) % 2, :, :]
                        A(d, d, ACT.Exp).then_inc(e_ready, 1)
                        if n + 1 < NU:
                            load_cum(n + 1)
                    if n < NU:
                        c, g = B_UNITS[n]
                        act.wait_ge(cum_in[n % 2], 32 * (NU // 2 * L + n // 2 + 1))
                        if n >= 2:
                            act.wait_ge(m_ready, NU * L + n - 1)
                        for h in range(HPG):
                            j = HPG * g + h
                            last = A(dmat[:, n % 2, h, :], cum_bc[n % 2][:, 0, h, :], ACT.Identity,
                                     bias=ncf[:, c, j:j + 1])
                        last.then_inc(t_ready, 1)
                        act.wait_ge(gm_ready, NU * L + n + 1)
                        for h in range(HPG):
                            j = NH + HPG * g + h
                            last = A(gdt[:, n % 2, h, :], gm[:, n % 2, 1, :], ACT.Copy, scale=tm[:, c, j:j + 1])
                        last.then_inc(gb_ready, 1)
                    if n == NCH + 2:
                        act.wait_ge(vvar, L + 1)
                        A(rv[:, :, :], mv[:, :, 1:2], ACT.Sqrt, bias=eps_sb[:, 0:1]).then_inc(vroot, 1)
                    continue
                t = T0 + T_UZ + n
                act.wait_ge(tile_done, t + 1)
                if n % 2 == 0:
                    free(t, A(halves(uz[:, n // 2, :]), acc_of(t)[:, :, 0:HALF], ACT.Gelu_apprx_tanh))
                    if n == 0:
                        act.wait_ge(cum_stored, 32 * (L + 1))
                        act.wait_ge(scan_done, L + 1)
                        load_cum(0)
                        load_cum(1)
                else:
                    if n > 1:
                        evacuated(act, t - 2)
                    A(halves(c_buf[0]), acc_of(t)[:, :, 0:HALF], ACT.Tanh, scale=0.5).then_inc(zt_ready, 1)

            act.wait_ge(y_ready, NU * (L + 1))
            act.dma_start(wsp_sb[:, :, :], wsp[L, :, :, :]).then_inc(wsp_in, 16)
            act.dma_start(lnb_sb[:, :], lnb[L:L + 1, :].partition_broadcast(P)).then_inc(wsp_in, 16)
            act.dma_start(bsp_row[:, :], bsp[L:L + 1, :]).then_inc(wsp_in, 16)
            for j in range(8):
                t = T0 + T_ZM + j
                if j == 0:
                    act.wait_ge(pbb_mm, L + 1)
                    for i in range(2):
                        A(pbb[:, 4 * i:4 * i + 4, :], X[2 + i][:, :].rearrange("p (g n) -> p g n", n=P), ACT.Copy)\
                            .then_inc(pbb_ready, 1)
                act.wait_ge(tile_done, t + 1)
                if j > 0:
                    evacuated(act, t - 1)
                else:
                    evacuated(act, T0 + T_UZ + 15)
                A(halves(c_buf[0]), acc_of(t)[:, :, 0:HALF], ACT.Tanh, scale=0.5).then_inc(zt_ready, 1)
                act.wait_ge(y2_ready, 8 * L + j + 1)
                square(2 * L + 1, j, c_buf[1][:, :])
                A(ym_hi[:, j, :], c_buf[1][:, :], ACT.Copy, scale=ssmw_sb[:, L, j:j + 1]).then_inc(ymhi_ready, 1)
                act.wait_ge(ya_ready, 8 * L + j + 1)
                A(yg_hi[:, j, :], c_buf[4][:, :], ACT.Copy).then_inc(yghi_ready, 1)

            act.dma_start(xr[:, :, :], xT if L == 0 else x_mid).then_inc(x_in, 16)
            for j in range(8):
                t = T0 + T_S5 + 4 * j
                for b, tt in ((0, t), (1, t + 2)):
                    act.wait_ge(tile_done, tt + 1)
                    if j > 0:
                        evacuated(act, t - 3 + 2 * b)
                    free(tt, A(halves(c_buf[b]), acc_of(tt)[:, :, 0:HALF], ACT.Tanh, scale=0.5))
                    if j == 0 and b == 0:
                        root(2 * L + 1)
                        act.wait_ge(rbc_ready, 2 * L + 2)
                        A(c_buf[2][:, CTX:TOK], X[0][:, :], ACT.Copy, scale=0.5)
                        A(c_buf[2][:, 0:CTX], X[1][:, 0:P], ACT.Copy, scale=0.5).then_inc(ry_ready, 1)
            for k in range(KC):
                act.wait_ge(mg_ready, 8 * L + k + 1)
                A(h_hi[:, k, :], mg[:, k, :], ACT.Copy).then_inc(mhi_ready, 1)
            warm_root()
            for j in range(8):
                evacuated(act, T0 + T_OUT + j)
                square(2 * L + 2, j, xr[:, j, :])
            if L < DEPTH - 1:
                act.dma_start(x_mid, xr[:, :, :]).then_inc(x_stored, 16)
        root(2 * DEPTH)

    @block.vector
    def _(dve):
        own = Chain(dve, s_dve)
        TT, STT, TS = nc.vector.tensor_tensor, nc.vector.scalar_tensor_tensor, nc.vector.tensor_scalar

        def free(t, ins):
            ins.then_inc(acc_free[t % 2], 1)

        def per_head(ap, w):
            return ap.unsqueeze(2).broadcast_to([P, ap.shape[1], w])

        def ada(n):
            job, part = n // 4, n % 4
            if job == 0:
                src = ada_first(4 * DVE_FIRST + n)
                dve.wait_ge(pre_in[(4 * DVE_FIRST + n) // 2], 32)
            else:
                src = ada_st[:, n % 2, :, :]
                dve.wait_ge(ada_in[n % 2], 16 * ((n - 4) // 2 + 1))
            if part == 0 and job >= 2:
                dve.wait_ge(ada_mm, DVE_FIRST + 1 if job == 2 else NF + job - 2)
            if part > 0:
                dve.wait_ge(ada_used, n)
            for kk in range(2):
                k = 2 * part + kk
                for v in range(2):
                    o, w, s = ada_acc[job % 2][:, v, :], src[:, kk, :], sc[:, 1, k, v:v + 1]
                    ins = TS(o, w, s, None, ALU.mult) if k == 0 else \
                        STT(out=o, in0=w, scalar=s, in1=o, op0=ALU.mult, op1=ALU.add)
                    if kk == 1 and v == 1:
                        ins.then_inc(ada_used, 1)
                    else:
                        own.mark(ins)
                if kk == 0:
                    own.wait()

        def job_out(n):
            L, q, hf = (JOBS_FIRST + JOBS_LATER)[n]
            dve.wait_ge(ada_mm, n + 1)
            cols = slice(4 * hf, 4 * hf + 4)
            total = X[2][:, 0:8].rearrange("p (v j) -> p v j", v=2)
            if n == DVE_FIRST or n >= NF:
                total = job_sum[:, :, :]
                for v in range(2):
                    last = nc.vector.tensor_reduce(total[:, v, :], X[2 + v][:, :].rearrange("p (j n) -> p j n", n=P),
                                                   AXX, ALU.add)
                own.link(last)
            TT(mods[:, 3 * L + q, :, cols], total,
               bada_sb[:, 3 * L + q, cols].unsqueeze(1).broadcast_to([P, 2, 4]), ALU.add).then_inc(job_read, 1)
            dve.wait_ge(job_read, n + 1)
            if q == 1 and hf == 1:
                own.link(STT(out=amul[:, L, :, :], in0=mods[:, 3 * L + 1, :, :], scalar=1.0,
                             in1=normw_sb[:, L, :].unsqueeze(1).broadcast_to([P, 2, KC]),
                             op0=ALU.add, op1=ALU.mult))

        def add_square(n, k):
            dve.wait_ge(sq_ready, 8 * n + k + 1)
            src = c_buf[2 + k % 2][:, :]
            ins = nc.vector.tensor_copy(ssq[:, :], src) if k == 0 else TT(ssq[:, :], ssq[:, :], src, ALU.add)
            if k < KC - 1:
                ins.then_inc(sq_used, 1)
                dve.wait_ge(sq_used, 7 * n + k + 1)
            else:
                ins.then_inc(ssq_ready, 1)

        def rstd(n):
            dve.wait_ge(root_ready, n + 1)
            nc.vector.reciprocal(rst[:, 1, :], rst[:, 0, :]).then_inc(rstd_ready, 1)

        dve.wait_ge(ct_ready, 1)
        own.link(STT(out=sc[:, 1, :, :], in0=sc[:, 0, :, :], scalar=1.0, in1=c_sb[:, :, :], op0=ALU.add, op1=ALU.mult))
        TS(sc[:, 1, :, :], sc[:, 1, :, :], 0.5, None, ALU.mult).then_inc(sc_ready, 1)
        dve.wait_ge(consts_in, 16 * 9)
        dve.wait_ge(consts_made, 1)
        job_out(0)
        for k in range(KC):
            add_square(0, k)
        own.link(TS(convw_sb[:, :, :, :], convw_sb[:, :, :, :], 0.5, None, ALU.mult))
        ada(0)
        rstd(0)
        ada(1)
        job_out(1)
        ada(2)
        ada(3)

        for L in range(DEPTH):
            T0 = L * N_TILES

            if L > 0:
                rstd(2 * L)
            lag = 1 if L > 0 else 3
            dve.wait_ge(rbc_ready, 2 * L + 1)
            SEG = ((0, slice(0, CTX), X[1][:, 0:CTX]), (1, slice(CTX, TOK), X[0][:, 0:LAT]))
            for k in range(KC + lag):
                if k < KC:
                    if k >= 4:
                        dve.wait_ge(h_ready, 8 * L + k - 3)
                    for v, cols, r in SEG:
                        last = STT(out=c_buf[k % 4][:, cols], in0=xr[:, k, cols], scalar=amul[:, L, v, k:k + 1],
                                   in1=r, op0=ALU.mult, op1=ALU.mult)
                    last.then_inc(hpre_ready, 1)
                if L == 0 and k == lag - 1:
                    job_out(2)
                    job_out(3)
                if k >= lag:
                    kk = k - lag
                    dve.wait_ge(hhi_ready, 8 * L + kk + 1)
                    for v, cols, r in SEG:
                        last = STT(out=h_lo[:, kk, cols], in0=c_buf[kk % 4][:, cols],
                                   scalar=mods[:, 3 * L, v, kk:kk + 1], in1=f(h_hi[:, kk, cols]),
                                   op0=ALU.add, op1=ALU.subtract)
                    last.then_inc(h_ready, 1)

            dve.wait_ge(h_ready, 8 * (L + 1))
            for at in (0, PAD + CTX, RAW - PAD):
                last = nc.vector.memset(raw[:, :, at:at + PAD], 0.0)
            last.then_inc(pads_ready, 1)

            def dt_abs():
                evacuated(dve, T0)
                x = c_buf[0][0:32, :]
                STT(out=c_buf[1][0:32, :], in0=x, scalar=-1.0, in1=x, op0=ALU.mult, op1=ALU.max).then_inc(dte_arg, 1)
                dve.wait_ge(dte_ready, L + 1)
                TS(c_buf[2][0:32, :], c_buf[1][0:32, :], 1.0, None, ALU.add).then_inc(dtu_ready, 1)

            def dt_finish():
                x, e, u, lu = (b[0:32, :] for b in c_buf[0:4])
                dve.wait_ge(dtu_ready, L + 1)
                STT(out=e, in0=u, scalar=1.0, in1=e, op0=ALU.subtract, op1=ALU.subtract)
                own.link(nc.vector.reciprocal(dta[0:32, :], u))
                own.link(TT(e, e, dta[0:32, :], ALU.mult))
                dve.wait_ge(dtl_ready, L + 1)
                own.link(TT(lu, lu, e, ALU.subtract))
                own.link(STT(out=dta[0:32, :], in0=x, scalar=0.0, in1=lu, op0=ALU.max, op1=ALU.add))
                TS(dta[32:64, :], dta[0:32, :], ea[:, L:L + 1], -1.0, ALU.mult, ALU.mult).then_inc(dta_ready, 1)

            def decay_args():
                dve.wait_ge(cum_mm, L + 1)
                cf = X[3][:, 0:80].rearrange("p (c h) -> p c h", h=NH)
                eb = X[3][:, 80:160].rearrange("p (c h) -> p c h", h=NH)
                tot = X[3][:, 160:320].rearrange("p (c d h) -> p d c h", d=2, h=NH)
                TS(ncf[:, :, :], cf, -1.0, None, ALU.mult)
                nc.vector.tensor_copy(ebs[:, :, :], eb)
                nc.vector.tensor_copy(ex[:, 1, :, :], eb)
                nc.vector.tensor_copy(ex[:, 2, :, :], cf)
                nc.vector.tensor_copy(ex[:, 4, :, :], tot[:, 0])
                own.link(nc.vector.tensor_copy(ex[:, 5, :, :], tot[:, 1]))
                TT(ex[:, 0, :, :], ex[:, 4, :, :], ncf[:, :, :], ALU.add)
                TT(ex[:, 3, :, :], ex[:, 5, :, :], ebs[:, :, :], ALU.subtract).then_inc(ex_arg, 1)

            def cum_rows():
                dve.wait_ge(cumT_mm, L + 1)
                for d, sign in ((0, 1.0), (1, -1.0)):
                    rows = slice(32 * d, 32 * d + NH)
                    TS(cum_t[rows, P:TOK], X[0][rows, :], sign, None, ALU.mult)
                    last = TS(cum_t[rows, 0:P], X[1][rows, 0:P], sign, None, ALU.mult)
                last.then_inc(cum_ready, 1)

            def state_weights():
                dve.wait_ge(ex_ready, L + 1)
                for d in range(2):
                    last = TT(ex[:, d, :, :], ex[:, d, :, :], tm[:, :, NH * d:NH * (d + 1)], ALU.mult)
                own.link(last)

            def a_unit(a):
                c, g = A_UNITS[a]
                n = NU * L + a
                dve.wait_ge(tp_out, 16 * L + 2 * (g + 1))
                if a >= 2:
                    dve.wait_ge(s_mm, n - 1)
                xg = x_tok[:, c, g * GC:(g + 1) * GC].rearrange("p (h w) -> p h w", w=HD)
                for d in range(2):
                    last = TT(xw[:, a % 2, d, :, :], xg, per_head(ex[:, d, c, HPG * g:HPG * (g + 1)], HD), ALU.mult)
                last.then_inc(xw_ready, 1)

            dt_abs()
            for i in range(NCONV + 1):
                if i == NCONV - 1:
                    a_unit(0)
                    a_unit(1)
                if i < NCONV:
                    evacuated(dve, T0 + T_CONV + i)
                    ch = (i + 8) % NCONV
                    w = convw_sb[:, L, ch, :]
                    r, o = raw[:, i % 2, :], cv[:, i % 2, 0:CW]
                    if NCONV * L + i > 1:
                        dve.wait_ge(conv_done, NCONV * L + i - 1)
                    own.link(TS(o, r[:, PAD:PAD + CW], w[:, PAD:PAD + 1], w[:, TAPS:TAPS + 1], ALU.mult, ALU.add))
                    for tap in (0, 1, 3, 4):
                        ins = STT(out=o, in0=r[:, tap:tap + CW], scalar=w[:, tap:tap + 1], in1=o,
                                  op0=ALU.mult, op1=ALU.add)
                        if tap < 4:
                            own.link(ins)
                        else:
                            ins.then_inc(cv_ready, 1)
                if i > 0:
                    n = i - 1
                    dve.wait_ge(cvt_ready, NCONV * L + i)
                    if n < 8:
                        dst = bc[:, n, :]
                    else:
                        dst = xo[:, n % 2, 0:CW]
                        if n >= 10:
                            dve.wait_ge(tp_ready, 16 * L + n - 9)
                    STT(out=dst, in0=cvt[:, 0:CW], scalar=1.0, in1=cv[:, n % 2, 0:CW],
                        op0=ALU.add, op1=ALU.mult).then_inc(conv_done, 1)
                if i == 0:
                    dt_finish()
                if i == 5:
                    decay_args()
                if i == 6:
                    cum_rows()
                if i == 8:
                    state_weights()

            for a in range(2, NU):
                a_unit(a)

            dve.wait_ge(st_in, 32 * (L + 1))
            dve.wait_ge(s_out, NU * (L + 1))
            for i in range(NCH - 2):
                for d in range(2):
                    c = 1 + i if d == 0 else NCH - 1 - i
                    frm = states[2 * (c - 1) + d]
                    to = states[2 * c] if d == 0 else states[2 * (c - 2) + 1]
                    own.link(TT(scan_tmp[:, :].rearrange("p (h w) -> p h w", w=HD),
                                frm[:, :].rearrange("p (h w) -> p h w", w=HD),
                                per_head(ex[:, 4 + d, c, :], HD), ALU.mult))
                    ins = TT(to[:, :], to[:, :], scan_tmp[:, :], ALU.add)
                    if i == NCH - 3 and d == 1:
                        ins.then_inc(scan_done, 1)
                    else:
                        own.link(ins)

            def layer_norm(b):
                if 1 <= b <= NCH:
                    c = b - 1
                    for hf in range(2):
                        ins = nc.vector.bn_stats(bst[:, c, 6 * hf:6 * hf + 6], v_tok[:, c, 512 * hf:512 * (hf + 1)])
                    own.mark(ins)
                if b == NCH + 1:
                    own.wait()
                    for c in range(NCH):
                        last = nc.vector.bn_aggr(mv[:, c, :], bst[:, c, :])
                    last.then_inc(vvar, 1)
                if b == NCH + 4:
                    dve.wait_ge(vroot, L + 1)
                    own.link(nc.vector.reciprocal(rv[:, :, :], rv[:, :, :]))
                if NCH + 5 <= b < 2 * NCH + 5:
                    c = b - NCH - 5
                    TS(v_tok[:, c, :], v_tok[:, c, :], mv[:, c, 0:1], rv[:, c, 0:1], ALU.subtract, ALU.mult)\
                        .then_inc(ln_ready, 1)

            def b_unit(b):
                if 1 <= b <= NU:
                    s = (b - 1) % 2
                    c, g = B_UNITS[b - 1]
                    dve.wait_ge(gb_ready, NU * L + b)
                    for h in range(HPG):
                        j = HPG * g + h
                        last = STT(out=gdt[:, s, h, :], in0=gm[:, s, 0, :], scalar=tm[:, c, j:j + 1],
                                   in1=gdt[:, s, h, :], op0=ALU.mult, op1=ALU.add)
                    own.link(last)
                    dve.wait_ge(e_ready, NU * L + b)
                    if b >= 3:
                        dve.wait_ge(fbg_ready, (NU + 2) * L + b)
                    TT(mmat[:, s, :, :], dmat[:, s, :, :], gdt[:, s, :, :], ALU.mult).then_inc(m_ready, 1)
                dve.wait_ge(fbg_ready, (NU + 2) * L + b + 1)
                if b < NU:
                    s = b % 2
                    if b >= 2:
                        dve.wait_ge(m_ready, NU * L + b - 1)
                    TT(gm[:, s, 0, :], X[2][:, 0:P], tri[:, 0, :], ALU.mult)
                    TT(gm[:, s, 1, :], X[2][:, 0:P], maskb[:, :], ALU.mult).then_inc(gm_ready, 1)
                if b >= 2:
                    c, g = B_UNITS[b - 2]
                    xf = x_tok[:, c, g * GC:(g + 1) * GC]
                    xg = xf.rearrange("p (h w) -> p h w", w=HD)
                    hs = slice(HPG * g, HPG * (g + 1))
                    yb = yab[:, 1, :, :]
                    flat = [yab[:, i, :, :].rearrange("p h w -> p (h w)") for i in range(2)]
                    if b > 2:
                        dve.wait_ge(y_ready, NU * L + b - 2)
                    if c > 0:
                        own.link(TT(yab[:, :, :, :], X[b % 2][:, :].rearrange("p (d h w) -> p d h w", d=2, w=HD),
                                    ex[:, 2:4, c, hs].unsqueeze(3).broadcast_to([P, 2, HPG, HD]), ALU.mult))
                        own.link(TT(flat[0], flat[0], flat[1], ALU.add))
                        own.mark(TT(yb, xg, per_head(dskip_sb[:, L, hs], HD), ALU.mult))
                        TT(flat[0], flat[0], X[3][:, 0:GC], ALU.add).then_inc(y_out, 1)
                    else:
                        own.link(nc.vector.tensor_copy(flat[0], X[3][:, 0:GC]))
                        TT(yb, xg, per_head(dskip_sb[:, L, hs], HD), ALU.mult).then_inc(y_out, 1)
                if b < NU:
                    c, g = B_UNITS[b]
                    s = b % 2
                    dve.wait_ge(t_ready, NU * L + b + 1)
                    for h in range(HPG):
                        j = HPG * g + h
                        last = STT(out=dmat[:, s, h, :], in0=cum_bc[s][:, 1, h, :], scalar=ebs[:, c, j:j + 1],
                                   in1=dmat[:, s, h, :], op0=ALU.add, op1=ALU.min)
                    last.then_inc(d_ready, 1)
                if b >= 2:
                    dve.wait_ge(y_out, NU * L + b - 1)
                    TT(xf, flat[0], flat[1], ALU.add).then_inc(y_ready, 1)

            for what, n in order_uz():
                if what == "burst":
                    if n == 0:
                        dve.wait_ge(tp_out, 16 * (L + 1))
                    b_unit(n)
                    layer_norm(n)
                    continue
                t, j = T0 + T_UZ + n, n // 2
                if n % 2 == 1:
                    dve.wait_ge(zt_ready, 16 * L + j + 1)
                    if n == 1:
                        dve.wait_ge(tp_ready, 16 * (L + 1))
                    free(t, STT(out=halves(c_buf[1]), in0=halves(c_buf[0]), scalar=1.0,
                                in1=acc_of(t)[:, :, 0:HALF], op0=ALU.add, op1=ALU.mult))
                    evacuated(dve, t)
                    evacuated(dve, t - 1)
                    own.mark(TT(uz[:, j, :], uz[:, j, :], c_buf[1][:, :], ALU.mult))

            own.wait()
            for j in range(8):
                t = T0 + T_ZM + j
                n = 8 * L + j
                dve.wait_ge(zt_ready, 16 * L + 8 + j + 1)
                if j > 0:
                    dve.wait_ge(ymhi_ready, n)
                    dve.wait_ge(ym_ready, n)
                free(t, STT(out=halves(c_buf[1]), in0=halves(c_buf[0]), scalar=1.0,
                            in1=acc_of(t)[:, :, 0:HALF], op0=ALU.add, op1=ALU.mult))
                evacuated(dve, t)
                dve.wait_ge(yT_mm, n + 1)
                cx = c_buf[1][:, 0:CTX]
                STT(out=cx, in0=X[1][:, 0:P], scalar=0.5, in1=cx, op0=ALU.mult, op1=ALU.mult)
                lat = c_buf[1][:, CTX:TOK].rearrange("p (r w) -> p r w", w=GW)
                src = X[0][:, :].rearrange("p (r w) -> p r w", w=GW) if L % 2 == 0 else \
                    X[0][:, :].rearrange("p (w r) -> p r w", r=GH)
                STT(out=lat, in0=src, scalar=0.5, in1=lat, op0=ALU.mult, op1=ALU.mult).then_inc(y2_ready, 1)
                dve.wait_ge(sp_mm, n + 1)
                if j > 0:
                    dve.wait_ge(yghi_ready, n)
                    dve.wait_ge(yg_ready, n)
                STT(out=c_buf[4][:, CTX:TOK].rearrange("p (c n) -> p c n", n=P),
                    in0=X[2][:, :].rearrange("p (c n) -> p c n", n=P), scalar=lnw_sb[:, L, j:j + 1],
                    in1=pbb[:, j, :].unsqueeze(1).broadcast_to([P, NCH - 1, P]), op0=ALU.mult, op1=ALU.add)
                STT(out=c_buf[4][:, 0:CTX], in0=X[3][:, 0:P], scalar=lnw_sb[:, L, j:j + 1], in1=pbb[:, j, :],
                    op0=ALU.mult, op1=ALU.add).then_inc(sp_used, 1)
                add_square(2 * L + 1, j)
                dve.wait_ge(sp_used, n + 1)
                STT(out=c_buf[4][:, :], in0=c_buf[4][:, :], scalar=0.5, in1=uz[:, j, :],
                    op0=ALU.mult, op1=ALU.mult).then_inc(ya_ready, 1)
                dve.wait_ge(ymhi_ready, n + 1)
                STT(out=ym_lo[:, j, :], in0=c_buf[1][:, :], scalar=ssmw_sb[:, L, j:j + 1], in1=f(ym_hi[:, j, :]),
                    op0=ALU.mult, op1=ALU.subtract).then_inc(ym_ready, 1)
                dve.wait_ge(yghi_ready, n + 1)
                TT(yg_lo[:, j, :], c_buf[4][:, :], f(yg_hi[:, j, :]), ALU.subtract).then_inc(yg_ready, 1)

            def merge_lo(k):
                dve.wait_ge(mhi_ready, 8 * L + k + 1)
                TT(h_lo[:, k, :], mg[:, k, :], f(h_hi[:, k, :]), ALU.subtract).then_inc(mh_ready, 1)

            for j in range(8):
                t = T0 + T_S5 + 4 * j
                if j == 0:
                    rstd(2 * L + 1)
                if L == 0:
                    ada(4 * j + 4)
                for b, tt in ((0, t + 1), (1, t + 3)):
                    if b == 1 and j == 7:
                        for k in range(KC - 1):
                            merge_lo(k)
                    evacuated(dve, tt - 1)
                    if b == 0:
                        dve.wait_ge(tile_done, tt + 1)
                        if j > 0:
                            dve.wait_ge(mg_ready, 8 * L + j)
                        free(tt, STT(out=halves(c_buf[4]), in0=halves(c_buf[0]), scalar=1.0,
                                     in1=acc_of(tt)[:, :, 0:HALF], op0=ALU.add, op1=ALU.mult))
                    else:
                        dve.wait_ge(ry_ready, L + 1)
                        own.link(STT(out=c_buf[1][:, :], in0=c_buf[1][:, :], scalar=1.0, in1=c_buf[2][:, :],
                                     op0=ALU.add, op1=ALU.mult))
                        dve.wait_ge(tile_done, tt + 1)
                        free(tt, TT(halves(mg[:, j, :]), halves(c_buf[1]), acc_of(tt)[:, :, 0:HALF], ALU.mult))
                    if L == 0 and b == 0:
                        ada(4 * j + 5)
                        ada(4 * j + 6)
                evacuated(dve, t + 3)
                STT(out=mg[:, j, :], in0=c_buf[4][:, :], scalar=0.5, in1=mg[:, j, :],
                    op0=ALU.mult, op1=ALU.add).then_inc(mg_ready, 1)
                if L == 0:
                    if j > 0:
                        job_out(3 + j)
                    ada(4 * j + 7)
            merge_lo(KC - 1)

            dve.wait_ge(x_in, 16 * (L + 2))
            for j in range(8):
                t = T0 + T_OUT + j
                dve.wait_ge(tile_done, t + 1)
                n0 = HALF
                for v, cols, src in ((0, slice(0, CTX), acc_of(t)[:, 0, 0:CTX]),
                                     (1, slice(CTX, n0), acc_of(t)[:, 0, CTX:HALF]),
                                     (1, slice(n0, TOK), acc_of(t)[:, 1, 0:HALF])):
                    last = STT(out=xr[:, j, cols], in0=src, scalar=mods[:, 3 * L + 2, v, j:j + 1],
                               in1=xr[:, j, cols], op0=ALU.mult, op1=ALU.add)
                free(t, last)
                if j > 0:
                    add_square(2 * L + 2, j - 1)
                if L == 0 and j == 1:
                    job_out(11)
            add_square(2 * L + 2, 7)

        rstd(2 * DEPTH)
        dve.wait_ge(rbc_ready, 2 * DEPTH + 1)
        for k in range(KC):
            for cols, r in ((slice(0, CTX), X[1][:, 0:CTX]), (slice(CTX, TOK), X[0][:, 0:LAT])):
                last = STT(out=xr[:, k, cols], in0=xr[:, k, cols], scalar=finalw_sb[:, k:k + 1], in1=r,
                           op0=ALU.mult, op1=ALU.mult)
            last.then_inc(fin_ready, 1)

    ctx.close()


def kernel(**inputs):
    import numpy as np
    import concourse.bacc as bacc
    from concourse.bass_utils import run_bass_kernel_spmd

    a = {k: np.asarray(v) for k, v in inputs.items()}
    f32 = np.float32

    def tiles(w):
        L, _, n = w.shape
        return w.reshape(L, KC, P, n // P, P).transpose(0, 3, 2, 1, 4).reshape(L, n // P, P, KC * P)

    def cols(v):
        v = v.reshape(v.shape[:-1] + (v.shape[-1] // P, P))
        return np.ascontiguousarray(np.moveaxis(v, -1, 0))

    w_in = a["w_in"]
    s = np.cumsum([0, NCONV * P, DM, 32, DM, DM, DM, DM, DM])
    part = [w_in[:, :, s[i]:s[i + 1]] for i in range(8)]
    xbc, zm, dt, u, v, zg, glm, glg = part
    dt = np.concatenate([dt, np.zeros((DEPTH, DM, P - 32), f32)], axis=2)
    xbc_t, zm_t, u_t, v_t, zg_t, glm_t, glg_t = (tiles(w) for w in (xbc, zm, u, v, zg, glm, glg))
    om_t, og_t, out_t = tiles(a["w_out_m"]), tiles(a["w_out_g"]), tiles(a["w_out"])
    uz = np.stack([u_t, zg_t], axis=2).reshape(DEPTH, 16, P, KC * P)
    s5 = np.stack([glg_t, og_t, glm_t, om_t], axis=2).reshape(DEPTH, 32, P, KC * P)
    wts = np.concatenate([tiles(dt), xbc_t[:, 8:], xbc_t[:, :8], v_t, uz, zm_t, s5, out_t], axis=1)
    wts = wts.reshape(DEPTH * N_TILES, P, KC * P)
    wada = a["w_ada"].reshape(DEPTH, 4, 2, P, 3, 2, 512).transpose(0, 4, 5, 1, 3, 2, 6)
    x = np.concatenate([a["x_prompt"][0], a["x_sample"][0]], axis=0)
    xT = x.T.reshape(KC, P, TOK).transpose(1, 0, 2)
    conv = np.concatenate([a["conv_w"], a["conv_b"][:, None, :]], axis=1)
    conv = conv.reshape(DEPTH, TAPS + 1, NCONV, P).transpose(3, 0, 2, 1)
    h0 = a["state_ssm"][0].reshape(DEPTH, 2, DM, P).transpose(0, 1, 3, 2)
    ins = {
        "xT": xT, "wts": wts, "wada": wada,
        "cT": cols(np.stack([a["c_ctx"], a["c"][0]])).transpose(0, 2, 1),
        "bada": cols(a["b_ada"].reshape(DEPTH * 3, DM)), "normw": cols(a["norm_w"]),
        "finalw": cols(a["final_norm_w"]), "ssmw": cols(a["ssm_norm_w"]), "convw": conv,
        "dtb": a["dt_bias"].reshape(DEPTH, 32).T, "alog": a["a_log"].reshape(DEPTH, 32).T,
        "dskip": np.broadcast_to(a["d_skip"][None], (P, DEPTH, NH)), "lnw": cols(a["sgu_ln_w"]),
        "lnb": a["sgu_ln_b"], "wsp": a["w_sp"].transpose(0, 3, 1, 2), "bsp": a["b_sp"].reshape(DEPTH, DM),
        "h0": h0,
    }
    ins = {k: np.ascontiguousarray(v) for k, v in ins.items()}
    nc = bacc.Bacc("TRN2", target_bir_lowering=False, num_devices=1, dynamic_dma_scratch_size=1024)
    aps = {k: nc.dram_tensor(f"in_{k}", v.shape, F32, kind="ExternalInput").ap() for k, v in ins.items()}
    yT = nc.dram_tensor("yT", (P, KC, TOK), F32, kind="ExternalOutput").ap()
    st = nc.dram_tensor("st", (DEPTH, 2, P, DM), F32, kind="ExternalOutput").ap()
    x_mid = nc.dram_tensor("x_mid", (P, KC, TOK), F32, kind="Internal").ap()
    cum_dram = nc.dram_tensor("cum_dram", (DEPTH, 2 * NH, TOK), F32, kind="Internal").ap()
    build(nc, **aps, yT=yT, st_out=st, x_mid=x_mid, cum_dram=cum_dram)
    r = run_bass_kernel_spmd(nc, [{f"in_{k}": v for k, v in ins.items()}], core_ids=[0])
    y = np.asarray(r.results[0]["yT"]).transpose(1, 0, 2).reshape(DM, TOK).T
    new = np.asarray(r.results[0]["st"]).transpose(0, 1, 3, 2).reshape(1, DEPTH, 2, NH, HD, P)
    return (np.ascontiguousarray(y[None, :CTX]), np.ascontiguousarray(y[None, CTX:]), np.ascontiguousarray(new))
```
